# Optimizing a Trainium2 kernel written in Bass

```python
import math
import jax, jax.numpy as jnp
from jax import lax
import numpy as np

D_MODEL = 1024
BATCH = 1
SEQ = 1024
DEPTH = 2
DEC_BATCH = 8
DEC_SEQ = 8
PAST_LEN = 1024
PAGE_SIZE = 128

HEAD_DIM = 64
NSA_HEADS = 8
NSA_KV_HEADS = 2
NSA_GROUP = NSA_HEADS // NSA_KV_HEADS
NSA_WIDTH = NSA_HEADS * HEAD_DIM
KV_WIDTH = NSA_KV_HEADS * HEAD_DIM
NSA_COLS = NSA_WIDTH + 6 * KV_WIDTH + 3 * NSA_HEADS
RWKV_HEADS = 8
RWKV_WIDTH = RWKV_HEADS * HEAD_DIM
MIX_WIDTH = NSA_WIDTH + RWKV_WIDTH
DECAY_LORA = 64
ICLR_LORA = 64
GATE_LORA = 128
RW_COLS = 3 * RWKV_WIDTH + DECAY_LORA + ICLR_LORA + GATE_LORA
RW_SPLITS = (RWKV_WIDTH, RWKV_WIDTH + DECAY_LORA, 2 * RWKV_WIDTH + DECAY_LORA,
             3 * RWKV_WIDTH + DECAY_LORA, 3 * RWKV_WIDTH + DECAY_LORA + ICLR_LORA)
IN_COLS = NSA_COLS + RW_COLS
CMP_BLOCK = 32
CMP_STRIDE = 16
CMP_HIDDEN = 256
SEL_BLOCK = 64
SEL_TOPK = 8
N_LOCAL_BLOCKS = 2
WINDOW = 256
QUERY_BLOCK = 128
D_FF = 2752
CONV_WIDTH = 3
ROPE_THETA = 10000.0
NORM_EPS = 1e-6
GN_EPS = 64e-5
NEG_BIG = -1e30

kernel_name = 'nsa_rwkv7_parallel_heads_convffn_step'

def rms_norm(x, g):
    xf = x.astype(jnp.float32)
    y = xf * lax.rsqrt(jnp.mean(xf * xf, axis=-1, keepdims=True) + NORM_EPS)
    return (y * g.astype(jnp.float32)).astype(x.dtype)

def rope(x, pos):
    half = HEAD_DIM // 2
    inv = ROPE_THETA ** (-jnp.arange(half, dtype=jnp.float32) / half)
    ang = pos.astype(jnp.float32)[:, None] * inv[None, :]
    cos = jnp.cos(ang)[None, :, None, :]
    sin = jnp.sin(ang)[None, :, None, :]
    xf = x.astype(jnp.float32)
    x1, x2 = xf[..., :half], xf[..., half:]
    return jnp.concatenate([x1 * cos - x2 * sin, x2 * cos + x1 * sin], axis=-1).astype(x.dtype)

def masked_softmax(s, mask):
    s = jnp.where(mask, s.astype(jnp.float32), NEG_BIG)
    m = jnp.max(s, axis=-1, keepdims=True)
    e = jnp.where(mask, jnp.exp(s - m), 0.0)
    return e / jnp.maximum(jnp.sum(e, axis=-1, keepdims=True), 1e-30)

def compress_blocks(rows, pe, w1, w2):
    b, length = rows.shape[:2]
    n_cmp = (length - CMP_BLOCK) // CMP_STRIDE + 1
    idx = jnp.arange(n_cmp)[:, None] * CMP_STRIDE + jnp.arange(CMP_BLOCK)[None, :]
    blocks = jnp.take(rows, idx, axis=1) + pe[:, None, :]
    flat = blocks.transpose(0, 1, 3, 2, 4).reshape(b, n_cmp, NSA_KV_HEADS, CMP_BLOCK * HEAD_DIM)
    return jax.nn.silu(flat @ w1) @ w2

def nsa_attention(q, gates, kv_all, win_ext, pe, w1, w2):
    b, t = q.shape[:2]
    dt = q.dtype
    length = kv_all.shape[1]
    past_len = length - t
    scale = HEAD_DIM ** -0.5
    k_cmp = compress_blocks(kv_all[:, :, 0], pe[0], w1[0], w2[0])
    v_cmp = compress_blocks(kv_all[:, :, 1], pe[1], w1[1], w2[1])
    n_cmp = k_cmp.shape[1]
    cmp_start = jnp.arange(n_cmp) * CMP_STRIDE
    cmp_end = cmp_start + CMP_BLOCK - 1
    n_sel = -(-length // SEL_BLOCK)
    sel_start = jnp.arange(n_sel) * SEL_BLOCK
    blk = jnp.arange(n_sel)
    overlap = ((cmp_start[:, None] < sel_start[None, :] + SEL_BLOCK)
               & (cmp_end[:, None] >= sel_start[None, :])).astype(jnp.float32)
    kv_sel = jnp.pad(kv_all[:, :, 2:4], ((0, 0), (0, n_sel * SEL_BLOCK - length), (0, 0), (0, 0), (0, 0)))
    sel_blocks = kv_sel.reshape(b, n_sel, SEL_BLOCK, 2, NSA_KV_HEADS, HEAD_DIM)
    sel_blocks = sel_blocks.transpose(0, 4, 1, 2, 3, 5).reshape(b, NSA_KV_HEADS, n_sel, SEL_BLOCK * 2 * HEAD_DIM)
    topk = min(SEL_TOPK, n_sel)
    qb = math.gcd(t, QUERY_BLOCK)
    nb = t // qb

    def block(args):
        q_blk, g_blk, bi = args
        s0 = bi * qb
        qpos = past_len + s0 + jnp.arange(qb)
        qg = q_blk.reshape(b, qb, NSA_KV_HEADS, NSA_GROUP, HEAD_DIM)
        s_c = jnp.einsum('bqgrd,bcgd->bqgrc', qg, k_cmp) * scale
        p_c = masked_softmax(s_c, (cmp_end[None, :] <= qpos[:, None])[None, :, None, None, :])
        o_c = jnp.einsum('bqgrc,bcgd->bqgrd', p_c.astype(dt), v_cmp)
        imp = jnp.einsum('bqgrc,cs->bqgs', p_c, overlap)
        cur = qpos // SEL_BLOCK
        forced = (blk[None, :] == 0) | ((blk[None, :] <= cur[:, None]) & (blk[None, :] > cur[:, None] - N_LOCAL_BLOCKS))
        future = sel_start[None, :] > qpos[:, None]
        score = jnp.where(forced[None, :, None, :], 1e9, jnp.where(future[None, :, None, :], -1e9, imp))
        _, idx = lax.top_k(score, topk)
        idx_t = idx.transpose(0, 2, 1, 3).reshape(b, NSA_KV_HEADS, qb * topk)
        gath = jnp.take_along_axis(sel_blocks, idx_t[..., None], axis=2)
        gath = gath.reshape(b, NSA_KV_HEADS, qb, topk * SEL_BLOCK, 2, HEAD_DIM)
        kpos = (idx[..., None] * SEL_BLOCK + jnp.arange(SEL_BLOCK)).reshape(b, qb, NSA_KV_HEADS, topk * SEL_BLOCK)
        s_s = jnp.einsum('bqgrd,bgqkd->bqgrk', qg, gath[..., 0, :]) * scale
        p_s = masked_softmax(s_s, (kpos <= qpos[None, :, None, None])[:, :, :, None, :])
        o_s = jnp.einsum('bqgrk,bgqkd->bqgrd', p_s.astype(dt), gath[..., 1, :])
        win = lax.dynamic_slice_in_dim(win_ext, s0, WINDOW + qb, axis=1)
        wpos = past_len - WINDOW + s0 + jnp.arange(WINDOW + qb)
        wmask = (wpos[None, :] >= 0) & (wpos[None, :] <= qpos[:, None]) & (wpos[None, :] > qpos[:, None] - WINDOW)
        s_w = jnp.einsum('bqgrd,bkgd->bqgrk', qg, win[:, :, 0]) * scale
        p_w = masked_softmax(s_w, wmask[None, :, None, None, :])
        o_w = jnp.einsum('bqgrk,bkgd->bqgrd', p_w.astype(dt), win[:, :, 1])
        g = jax.nn.sigmoid(g_blk.astype(jnp.float32)).reshape(b, qb, NSA_KV_HEADS, NSA_GROUP, 3)
        o = g[..., 0:1] * o_c + g[..., 1:2] * o_s + g[..., 2:3] * o_w
        return o.reshape(b, qb, NSA_WIDTH).astype(dt)

    q_blocks = q.reshape(b, nb, qb, NSA_HEADS, HEAD_DIM).swapaxes(0, 1)
    g_blocks = gates.reshape(b, nb, qb, NSA_HEADS, 3).swapaxes(0, 1)
    out = lax.map(block, (q_blocks, g_blocks, jnp.arange(nb)))
    return out.swapaxes(0, 1).reshape(b, t, NSA_WIDTH)

def rwkv_mixer(p_rw, shift_prev, wkv_prev, p):
    b, t = p_rw.shape[:2]
    f32 = jnp.float32
    dt = p_rw.dtype
    prev = jnp.concatenate([shift_prev[:, None].astype(dt), p_rw[:, :-1]], axis=1)
    xm = p_rw + (prev - p_rw) * p['rw_mu']
    r, wa, k, v, aa, ga = jnp.split(xm, list(RW_SPLITS), axis=-1)
    w = -jax.nn.softplus(-(p['rw_w0'] + jnp.tanh(wa) @ p['rw_w_b']).astype(f32)) - 0.5
    decay = jnp.exp(-jnp.exp(w))
    a = jax.nn.sigmoid((p['rw_a0'] + aa @ p['rw_a_b']).astype(f32))
    g = (jax.nn.sigmoid(ga) @ p['rw_g_b']).astype(f32)

    def heads(z):
        return z.astype(f32).reshape(b, t, RWKV_HEADS, HEAD_DIM)

    r_h, v_h, w_h, a_h = heads(r), heads(v), heads(decay), heads(a)
    kk = heads(k * p['rw_k_k'])
    kk = kk / jnp.maximum(jnp.sqrt(jnp.sum(kk * kk, axis=-1, keepdims=True)), 1e-12)
    k_a = p['rw_k_a'].astype(f32).reshape(RWKV_HEADS, HEAD_DIM)
    k_h = heads(k) * (1.0 + (a_h - 1.0) * k_a)

    def step(s, inp):
        rt, wt, kt, vt, at, bt = inp
        sa = jnp.einsum('bhij,bhj->bhi', s, at)
        s = s * wt[:, :, None, :] + sa[..., None] * bt[:, :, None, :] + vt[..., None] * kt[:, :, None, :]
        return s, jnp.einsum('bhij,bhj->bhi', s, rt)

    xs = tuple(z.swapaxes(0, 1) for z in (r_h, w_h, k_h, v_h, -kk, kk * a_h))
    s_fin, ys = lax.scan(step, wkv_prev.astype(f32), xs)
    y = ys.swapaxes(0, 1)
    mu = jnp.mean(y, axis=-1, keepdims=True)
    var = jnp.mean(jnp.square(y - mu), axis=-1, keepdims=True)
    yn = ((y - mu) * lax.rsqrt(var + GN_EPS)).reshape(b, t, RWKV_WIDTH)
    yn = yn * p['rw_gn_w'].astype(f32) + p['rw_gn_b'].astype(f32)
    bonus = jnp.sum(r_h * k_h * p['rw_r_k'].astype(f32), axis=-1, keepdims=True) * v_h
    out = (yn + bonus.reshape(b, t, RWKV_WIDTH)) * g
    return out.astype(dt), s_fin, p_rw[:, -1]

def conv_ffn(xn, conv_prev, p):
    t = xn.shape[1]
    gate = xn @ p['ffn_w_gate']
    up = xn @ p['ffn_w_up']
    ext = jnp.concatenate([conv_prev.astype(gate.dtype), gate], axis=1)
    cw = p['ffn_conv_w']
    c = p['ffn_conv_b'] + sum(cw[j] * ext[:, j:j + t] for j in range(CONV_WIDTH))
    h = jax.nn.silu(c) * up
    return h @ p['ffn_w_down'], ext[:, t:]

def layer(x, past_kv, win_prev, wkv_prev, shift_prev, conv_prev, p):
    b, t = x.shape[:2]
    past_len = past_kv.shape[1]
    pos = past_len + jnp.arange(t)
    xn = rms_norm(x, p['norm_mix'])
    proj = xn @ p['w_in']
    q = rope(proj[..., :NSA_WIDTH].reshape(b, t, NSA_HEADS, HEAD_DIM), pos)
    kv = proj[..., NSA_WIDTH:NSA_WIDTH + 6 * KV_WIDTH].reshape(b, t, 3, 2, NSA_KV_HEADS, HEAD_DIM)
    gates = proj[..., NSA_WIDTH + 6 * KV_WIDTH:NSA_COLS].reshape(b, t, NSA_HEADS, 3)
    p_rw = proj[..., NSA_COLS:]
    keys = rope(kv[:, :, :, 0].reshape(b, t, 3 * NSA_KV_HEADS, HEAD_DIM), pos).reshape(b, t, 3, NSA_KV_HEADS, HEAD_DIM)
    kv = jnp.stack([keys, kv[:, :, :, 1]], axis=3).reshape(b, t, 6, NSA_KV_HEADS, HEAD_DIM)
    rows = kv[:, :, :4]
    win_rows = kv[:, :, 4:]
    kv_all = jnp.concatenate([past_kv.astype(rows.dtype), rows], axis=1)
    win_valid = jnp.concatenate([win_prev.astype(rows.dtype), win_rows], axis=1)
    wb = win_prev.shape[1]
    win_ext = jnp.pad(win_valid, ((0, 0), (WINDOW - wb, 0), (0, 0), (0, 0), (0, 0)))
    n_keep = min(WINDOW, win_valid.shape[1])
    new_win = win_valid[:, win_valid.shape[1] - n_keep:]
    o_nsa = nsa_attention(q, gates, kv_all, win_ext, p['cmp_pe'], p['cmp_w1'], p['cmp_w2'])
    o_rw, wkv_new, shift_new = rwkv_mixer(p_rw, shift_prev, wkv_prev, p)
    x = x + jnp.concatenate([o_nsa, o_rw], axis=-1) @ p['w_out']
    f, conv_new = conv_ffn(rms_norm(x, p['norm_ffn']), conv_prev, p)
    x = x + f
    return x, rows, new_win, wkv_new, shift_new, conv_new

def setup_inputs(seed: int = 0) -> dict:
    key = jax.random.key(seed)
    keys = iter(jax.random.split(key, 40))
    f32 = jnp.float32

    def nrm(shape, scale):
        return jax.random.normal(next(keys), shape, f32) * scale

    n_pages = PAST_LEN // PAGE_SIZE
    in_use = DEC_BATCH * n_pages
    n_phys = in_use + max(1, in_use // 4)
    perm = jax.random.permutation(next(keys), n_phys)
    page_table = perm[:in_use].reshape(DEC_BATCH, n_pages).astype(jnp.int32)
    win_buf = min(WINDOW, PAST_LEN)
    return {
        'x_prompt': nrm((BATCH, SEQ, D_MODEL), 1.0),
        'x_sample': nrm((DEC_BATCH, DEC_SEQ, D_MODEL), 1.0),
        'cache_kv': nrm((DEPTH, n_phys, PAGE_SIZE, 4, NSA_KV_HEADS, HEAD_DIM), 1.0),
        'page_table': page_table,
        'state_win': nrm((DEPTH, DEC_BATCH, win_buf, 2, NSA_KV_HEADS, HEAD_DIM), 1.0),
        'state_wkv': nrm((DEPTH, DEC_BATCH, RWKV_HEADS, HEAD_DIM, HEAD_DIM), 0.3),
        'state_shift': nrm((DEPTH, DEC_BATCH, RW_COLS), 1.0),
        'state_conv': nrm((DEPTH, DEC_BATCH, CONV_WIDTH - 1, D_FF), 1.0),
        'norm_mix': 1.0 + nrm((DEPTH, D_MODEL), 0.02),
        'w_in': nrm((DEPTH, D_MODEL, IN_COLS), D_MODEL ** -0.5),
        'cmp_pe': nrm((DEPTH, 2, CMP_BLOCK, HEAD_DIM), 0.1),
        'cmp_w1': nrm((DEPTH, 2, CMP_BLOCK * HEAD_DIM, CMP_HIDDEN), (CMP_BLOCK * HEAD_DIM) ** -0.5),
        'cmp_w2': nrm((DEPTH, 2, CMP_HIDDEN, HEAD_DIM), 2.0 * CMP_HIDDEN ** -0.5),
        'rw_mu': jax.random.uniform(next(keys), (DEPTH, RW_COLS), f32),
        'rw_w0': nrm((DEPTH, RWKV_WIDTH), 0.5),
        'rw_w_b': nrm((DEPTH, DECAY_LORA, RWKV_WIDTH), 0.5 * DECAY_LORA ** -0.5),
        'rw_a0': nrm((DEPTH, RWKV_WIDTH), 0.3),
        'rw_a_b': nrm((DEPTH, ICLR_LORA, RWKV_WIDTH), 0.5 * ICLR_LORA ** -0.5),
        'rw_g_b': nrm((DEPTH, GATE_LORA, RWKV_WIDTH), GATE_LORA ** -0.5),
        'rw_k_k': 0.85 + nrm((DEPTH, RWKV_WIDTH), 0.05),
        'rw_k_a': 1.0 + nrm((DEPTH, RWKV_WIDTH), 0.05),
        'rw_r_k': nrm((DEPTH, RWKV_HEADS, HEAD_DIM), 0.3),
        'rw_gn_w': 1.0 + nrm((DEPTH, RWKV_WIDTH), 0.02),
        'rw_gn_b': nrm((DEPTH, RWKV_WIDTH), 0.02),
        'w_out': nrm((DEPTH, MIX_WIDTH, D_MODEL), MIX_WIDTH ** -0.5),
        'norm_ffn': 1.0 + nrm((DEPTH, D_MODEL), 0.02),
        'ffn_w_gate': nrm((DEPTH, D_MODEL, D_FF), D_MODEL ** -0.5),
        'ffn_w_up': nrm((DEPTH, D_MODEL, D_FF), D_MODEL ** -0.5),
        'ffn_conv_w': nrm((DEPTH, CONV_WIDTH, D_FF), 0.6),
        'ffn_conv_b': nrm((DEPTH, D_FF), 0.02),
        'ffn_w_down': nrm((DEPTH, D_FF, D_MODEL), D_FF ** -0.5),
        'norm_final': 1.0 + nrm((D_MODEL,), 0.02),
    }

def reference(x_prompt, x_sample, cache_kv, page_table, state_win, state_wkv, state_shift, state_conv,
              norm_mix, w_in, cmp_pe, cmp_w1, cmp_w2, rw_mu, rw_w0, rw_w_b, rw_a0, rw_a_b, rw_g_b,
              rw_k_k, rw_k_a, rw_r_k, rw_gn_w, rw_gn_b, w_out, norm_ffn, ffn_w_gate, ffn_w_up,
              ffn_conv_w, ffn_conv_b, ffn_w_down, norm_final):
    dt = x_prompt.dtype
    bp = x_prompt.shape[0]
    bd = x_sample.shape[0]
    past_rows = page_table.shape[1] * PAGE_SIZE
    x_p, x_s = x_prompt, x_sample
    rows_p, rows_s, win_p, win_s, wkv_p, wkv_s, sh_p, sh_s, cv_p, cv_s = ([] for _ in range(10))
    for l in range(DEPTH):
        p = {
            'norm_mix': norm_mix[l], 'w_in': w_in[l], 'cmp_pe': cmp_pe[l], 'cmp_w1': cmp_w1[l],
            'cmp_w2': cmp_w2[l], 'rw_mu': rw_mu[l], 'rw_w0': rw_w0[l], 'rw_w_b': rw_w_b[l],
            'rw_a0': rw_a0[l], 'rw_a_b': rw_a_b[l], 'rw_g_b': rw_g_b[l], 'rw_k_k': rw_k_k[l],
            'rw_k_a': rw_k_a[l], 'rw_r_k': rw_r_k[l], 'rw_gn_w': rw_gn_w[l], 'rw_gn_b': rw_gn_b[l],
            'w_out': w_out[l], 'norm_ffn': norm_ffn[l], 'ffn_w_gate': ffn_w_gate[l],
            'ffn_w_up': ffn_w_up[l], 'ffn_conv_w': ffn_conv_w[l], 'ffn_conv_b': ffn_conv_b[l],
            'ffn_w_down': ffn_w_down[l],
        }
        x_p, r_, w_, s_, h_, c_ = layer(
            x_p,
            jnp.zeros((bp, 0, 4, NSA_KV_HEADS, HEAD_DIM), dt),
            jnp.zeros((bp, 0, 2, NSA_KV_HEADS, HEAD_DIM), dt),
            jnp.zeros((bp, RWKV_HEADS, HEAD_DIM, HEAD_DIM), jnp.float32),
            jnp.zeros((bp, RW_COLS), dt),
            jnp.zeros((bp, CONV_WIDTH - 1, D_FF), dt),
            p)
        rows_p.append(r_); win_p.append(w_); wkv_p.append(s_); sh_p.append(h_); cv_p.append(c_)
        past_kv = cache_kv[l][page_table].reshape(bd, past_rows, 4, NSA_KV_HEADS, HEAD_DIM)
        x_s, r_, w_, s_, h_, c_ = layer(x_s, past_kv, state_win[l], state_wkv[l], state_shift[l], state_conv[l], p)
        rows_s.append(r_); win_s.append(w_); wkv_s.append(s_); sh_s.append(h_); cv_s.append(c_)
    y_prompt = rms_norm(x_p, norm_final)
    y_sample = rms_norm(x_s, norm_final)
    return (y_prompt, y_sample,
            jnp.stack(rows_p), jnp.stack(rows_s),
            jnp.stack(win_p), jnp.stack(win_s),
            jnp.stack(wkv_p), jnp.stack(wkv_s),
            jnp.stack(sh_p), jnp.stack(sh_s),
            jnp.stack(cv_p), jnp.stack(cv_s))


_drawn_inputs = setup_inputs


def setup_inputs(seed=0):
    import zlib

    import numpy as np

    out = dict(_drawn_inputs(seed))
    spreads = {}
    factors = {'rw_k_k': 4.346,
     'rw_gn_w': 5.182,
     'rw_gn_b': 4.833,
     'ffn_conv_b': 3.962,
     'norm_final': 2.902}
    for name, (base, spread) in spreads.items():
        noise = np.random.default_rng([zlib.crc32(name.encode()), seed]).standard_normal(out[name].shape)
        drawn = base * np.exp(spread * noise) if base else spread * noise
        out[name] = __import__('jax').numpy.asarray(drawn.astype(out[name].dtype))
    for name, factor in factors.items():
        out[name] = (out[name] * factor).astype(out[name].dtype)
    return out
```

```python
from contextlib import ExitStack, contextmanager
import itertools
import math

import numpy as np
import concourse.bass as bass
from concourse import mybir

F32 = mybir.dt.float32
I32 = mybir.dt.int32
ALU = mybir.AluOpType
ACT = mybir.ActivationFunctionType
AX = mybir.AxisListType

P = 128
D = 1024
KD = D // P
L = 2
L_RUN = L
SEQ = 1024
NB = 8
NQ = 8
NS = NB * NQ
NT = SEQ + NS
NTP = SEQ + P
TT = NTP // P
HD = 64
HH = 8
R4 = 4
WN = 1304
FR = 14
FF = 22
PAGES = 8
NPHYS = 80
CH = 64
NCH = SEQ // CH
SCALE = HD ** -0.5
NEG = -1e30
GROUPS = [(0, 384), (384, 384), (768, 320)]
BANK = 512
E05 = math.exp(-0.5)

_W = [("ident", P), ("ones", P), ("blk", P), ("gmask", P), ("gmask_s", P), ("lev", 6 * CH),
      ("restart", NT), ("cvalid", 8 * 64), ("cadd", 8 * 64), ("keep", 8 * 16), ("add", 8 * 16),
      ("causal", P), ("band", 384), ("low16", 256), ("low17", 289), ("swin", 264), ("snew", 8),
      ("skeep", 17), ("sadd", 17), ("hsel", 8), ("same", 64), ("seqt", NB * CH), ("seqp", NB)]
CO, _o = {}, 0
for _n, _w in _W:
    CO[_n] = (_o, _w)
    _o += _w
CW = _o


def constants():
    c = np.zeros((P, CW), np.float32)

    def put(name, a):
        o, w = CO[name]
        a = np.asarray(a, np.float32).reshape(a.shape[0], -1)
        c[:a.shape[0], o:o + w] = a

    p = np.arange(P)
    put("ident", np.eye(P))
    put("ones", np.ones((P, P)))
    put("blk", p[:, None] // 64 == p[None, :] // 64)
    s, t = p % 64, p % 64
    strict = np.concatenate([(s[:, None] < t[None, :64]), (s[:, None] <= t[None, :64])], 1)
    same = s[:, None] // NQ == (p % 64)[None, :] // NQ
    put("gmask", strict)
    put("gmask_s", strict & same)
    a = np.arange(CH)
    lev = []
    for n in range(6):
        w = 1 << n
        lev.append((a[None, :] // (2 * w) == a[:, None] // (2 * w)) & (a[None, :] // w % 2 == 1) & (a[:, None] // w % 2 == 0))
    put("lev", np.stack(lev, 1))
    r = np.ones(NT)
    r[0:SEQ:CH] = 0
    r[SEQ::NQ] = 0
    put("restart", np.tile(r, (P, 1)))
    q = np.arange(8)[None, :, None] * P + p[:, None, None]
    cc = np.arange(64)[None, None, :]
    valid = (cc < 63) & (16 * cc + 31 <= q)
    put("cvalid", valid)
    put("cadd", np.where(valid, 0, NEG))
    b = np.arange(16)[None, None, :]
    cur = q // 64
    forced = (b == 0) | ((b <= cur) & (b > cur - 2))
    future = b * 64 > q
    put("keep", ~(forced | future))
    put("add", np.where(forced, 1e9, np.where(future, -1e9, 0)))
    put("causal", np.where(p[None, :] > p[:, None], NEG, 0))
    k = np.arange(384)[None, :] - 256
    put("band", np.where((k <= p[:, None]) & (k > p[:, None] - 256), 0, NEG))
    for n in (16, 17):
        i = np.arange(n)
        put(f"low{n}", np.tile((i[None, None, :] < i[None, :, None]), (P, 1, 1)))
    q = (np.arange(64) % NQ)[:, None]
    k = np.arange(264)[None, :]
    put("swin", np.where((k > q) & (k <= 256 + q), 0, NEG))
    put("snew", np.where(np.arange(8)[None, :] <= q, 0, NEG))
    b = np.arange(17)[None, :] + 0 * q
    f = (b == 0) | (b >= 15)
    put("skeep", ~f)
    put("sadd", np.where(f, 1e9, 0))
    i = np.arange(64)
    put("hsel", (2 * (i // 8 % 4) + i // 32)[:, None] == np.arange(8)[None, :])
    put("same", (i[:, None] // 32 == i[None, :] // 32) & (i[:, None] % 8 == i[None, :] % 8))
    put("seqt", np.tile((a[None, None, :] // NQ == np.arange(NB)[None, :, None]), (P, 1, 1)))
    put("seqp", (p % 64)[:, None] // NQ == np.arange(NB)[None, :])
    return c


def rope_tables():
    pos = np.arange(NTP)
    pos[SEQ:] = SEQ + (pos[SEQ:] - SEQ) % NQ
    inv = (np.float32(10000.0) ** (-np.arange(32, dtype=np.float32) / 32)).astype(np.float32)
    ang = pos.astype(np.float32)[:, None] * inv[None, :]
    return np.concatenate([np.cos(ang), np.sin(ang)], 1).astype(np.float32).reshape(TT, P, 64)


class Chain:

    def __init__(self, eng, sem):
        self.eng, self.sem, self.n = eng, sem, 0

    def __call__(self, ins):
        ins.then_inc(self.sem, 1)
        self.n += 1
        self.eng.wait_ge(self.sem, self.n)


@contextmanager
def stage(nc, names):
    with ExitStack() as es:
        sems = [es.enter_context(nc.semaphore(n)) for n in names.split()]
        with nc.Block() as block:
            yield (block, *sems)
        for s in sems:
            nc.sync.sem_clear(s)
        nc.all_engine_barrier()


_NUMBER = itertools.count()


class Scope(ExitStack):

    def __init__(self, nc):
        super().__init__()
        self.nc = nc

    def sb(self, name, shape, dt=F32):
        return self.enter_context(self.nc.sbuf_tensor(f"{name}_{next(_NUMBER)}", shape, dt))


def ds(start, size):
    return bass.ds(start, size)


def bc(ap, n):
    return ap.unsqueeze(len(ap.shape)).to_broadcast([*ap.shape, n])


def mid(ap, n):
    return ap.unsqueeze(1).to_broadcast([ap.shape[0], n, ap.shape[1]])


def load_norm(nc, ps, cst, xres, gain, xn, store=None):
    with Scope(nc) as sc, stage(nc, "x_loaded squared summed rooted root_chain scaled normed stored") as (
            block, x_loaded, squared, summed, rooted, chain_sem, scaled, normed, stored):
        sq = sc.sb("n_sq", [P, 2, NT])
        rs = sc.sb("n_rs", [P, NT])
        g = sc.sb("n_g", [P, KD])

        @block.sync
        def _(sp):
            sp.dma_start(g[:, :], gain).then_inc(x_loaded, 16)
            for k in range(KD):
                sp.dma_start(xn[:, k, 0:NT], xres[k]).then_inc(x_loaded, 16)
            if store is not None:
                sp.wait_ge(normed, KD)
                for k in range(KD):
                    sp.dma_start(store[k], xn[:, k, 0:NT]).then_inc(stored, 16)
                sp.wait_ge(stored, 16 * KD)

        @block.scalar
        def _(act):
            act.wait_ge(x_loaded, 16 * (KD + 1))
            for k in range(KD):
                if k >= 2:
                    act.wait_ge(summed, k - 1)
                act.activation(sq[:, k % 2, :], xn[:, k, 0:NT], ACT.Square).then_inc(squared, 1)
            act.wait_ge(scaled, 1)
            act.activation(rs[:, :], rs[:, :], ACT.Sqrt).then_inc(rooted, 1)

        @block.tensor
        def _(pe):
            for k in range(KD):
                pe.wait_ge(squared, k + 1)
                for n, (o, w) in enumerate(GROUPS):
                    m = pe.matmul(ps[:, n * BANK:n * BANK + w], cst["ones"], sq[:, k % 2, o:o + w],
                                  start=(k == 0), stop=(k == KD - 1))
                m.then_inc(summed, 1)

        @block.vector
        def _(dve):
            dve.wait_ge(summed, KD)
            for n, (o, w) in enumerate(GROUPS):
                m = dve.tensor_scalar(rs[:, o:o + w], ps[:, n * BANK:n * BANK + w], 1.0 / D, 1e-6, ALU.mult, ALU.add)
            m.then_inc(scaled, 1)
            dve.wait_ge(rooted, 1)
            dve.reciprocal(rs[:, :], rs[:, :]).then_inc(chain_sem, 1)
            dve.wait_ge(chain_sem, 1)
            for k in range(KD):
                dve.scalar_tensor_tensor(out=xn[:, k, 0:NT], in0=xn[:, k, 0:NT], scalar=g[:, k:k + 1],
                                         in1=rs[:, :], op0=ALU.mult, op1=ALU.mult).then_inc(normed, 1)


def nsa_projection(nc, ps, cst, l, t, xn, w, K, qT, ksT, kwT, vs, vw, gate, kvrows, winr, rope_d, tmp):
    xt, kv, q, q2, tb, cs = tmp
    with stage(nc, "cs_loaded x_copied proj copied chain rotated turned kept stored") as (
            block, cs_loaded, x_copied, proj, copied, chain_sem, rotated, turned, kept, stored):

        @block.sync
        def _(sp):
            sp.dma_start(cs[:, :], rope_d[t]).then_inc(cs_loaded, 16)
            sp.wait_ge(rotated, 2)
            sp.dma_start(kvrows[l, ds(t * P, P), :], kv[:, 0:512]).then_inc(stored, 16)
            sp.dma_start(winr[ds(t * P, P), :], kv[:, 512:768]).then_inc(stored, 16)
            sp.wait_ge(stored, 32)

        @block.tensor
        def _(pe):
            pe.wait_ge(x_copied, 1)
            for n, (o, c) in enumerate([(512, 512), (1024, 280), (0, 512)]):
                for k in range(KD):
                    m = pe.matmul(ps[:, n * BANK:n * BANK + c], xt[:, k, :], w[:, k, o:o + c],
                                  start=(k == 0), stop=(k == KD - 1))
                m.then_inc(proj, 1)
            pe.wait_ge(rotated, 2)
            pe.transpose(ps[:, 4 * BANK:4 * BANK + P], kv[:, 256:384], cst["ident"])
            pe.transpose(ps[:, 4 * BANK + P:4 * BANK + 2 * P], kv[:, 512:640], cst["ident"]).then_inc(turned, 1)
            pe.wait_ge(rotated, 4)
            for r in range(R4):
                m = pe.transpose(ps[:, 3 * BANK + r * P:3 * BANK + (r + 1) * P], q2[:, r * P:(r + 1) * P], cst["ident"])
            m.then_inc(turned, 1)

        @block.scalar
        def _(act):
            act.wait_ge(proj, 1)
            act.copy(kv[:, 0:512], ps[:, 0:512]).then_inc(copied, 1)
            act.wait_ge(proj, 2)
            act.activation(gate[:, ds(t * 24, 24)], ps[:, BANK + 256:BANK + 280], ACT.Sigmoid)
            act.copy(kv[:, 512:768], ps[:, BANK:BANK + 256]).then_inc(copied, 1)
            act.wait_ge(proj, 3)
            act.copy(q[:, :], ps[:, 2 * BANK:3 * BANK]).then_inc(copied, 1)
            act.wait_ge(turned, 1)
            act.copy(ksT[:, ds(t * P, P)], ps[:, 4 * BANK:4 * BANK + P])
            act.copy(kwT[:, ds(t * P, P)], ps[:, 4 * BANK + P:4 * BANK + 2 * P])
            act.wait_ge(turned, 2)
            act.copy(qT[:, :, ds(t * P, P)], ps[:, 3 * BANK:4 * BANK].rearrange("p (r t) -> p r t", r=R4)).then_inc(kept, 1)

        @block.vector
        def _(dve):
            step = Chain(dve, chain_sem)
            dve.tensor_copy(xt[:, :, :], xn[:, :, ds(t * P, P)]).then_inc(x_copied, 1)
            dve.wait_ge(cs_loaded, 16)

            def rotate(x1, x2, o1, o2, shape, tmps):
                dims = list(shape)
                cos, sin = cs[:, 0:32], cs[:, 32:64]
                for d in dims[:-1]:
                    cos, sin = cos.unsqueeze(1), sin.unsqueeze(1)
                cos, sin = cos.to_broadcast([P, *dims]), sin.to_broadcast([P, *dims])
                ta, tc, td, te = tmps
                dve.tensor_tensor(ta, x1, cos, ALU.mult)
                dve.tensor_tensor(tc, x2, sin, ALU.mult)
                dve.tensor_tensor(td, x2, cos, ALU.mult)
                step(dve.tensor_tensor(te, x1, sin, ALU.mult))
                dve.tensor_tensor(o1, ta, tc, ALU.subtract).then_inc(rotated, 1)
                dve.tensor_tensor(o2, td, te, ALU.add).then_inc(rotated, 1)

            dve.wait_ge(copied, 2)
            kh = kv[:, :].rearrange("p (a k g e d) -> p a k g e d", a=3, k=2, g=2, e=2)[:, :, 0]
            tk = [tb[:, n, 0:192].rearrange("p (a g d) -> p a g d", a=3, g=2) for n in range(4)]
            rotate(kh[:, :, :, 0, :], kh[:, :, :, 1, :], kh[:, :, :, 0, :], kh[:, :, :, 1, :], (3, 2, 32), tk)
            dve.tensor_copy(vs[:, ds(t * P, P)], kv[:, 384:512])
            dve.tensor_copy(vw[:, ds(t * P, P)], kv[:, 640:768])
            dve.wait_ge(copied, 3)
            dve.wait_ge(rotated, 2)
            qh, q2h = (a[:, :].rearrange("p (h e d) -> p h e d", h=8, e=2) for a in (q, q2))
            tq = [tb[:, n, :].rearrange("p (h d) -> p h d", h=8) for n in range(4)]
            rotate(qh[:, :, 0, :], qh[:, :, 1, :], q2h[:, :, 0, :], q2h[:, :, 1, :], (8, 32), tq)


def rwkv_projection(nc, ps, cst, l, xn, w_rw, shift_in, mu_d, xmT, shift_out):
    with Scope(nc) as sc, stage(nc, "w_in0 w_in1 s_in0 s_in1 mu_in done raw mixed raw_read sent0 sent1 chain zeroed sp_hold") as (
            block, w0, w1, s0, s1, mu_in, products, raw_ready, mixed, raw_read, sent0, sent1, chain_sem, zeroed, sp_hold):
        w_in, s_in, sent = (w0, w1), (s0, s1), (sent0, sent1)
        wt = sc.sb("rp_w", [P, 2, KD, P])
        raw = sc.sb("rp_raw", [P, 2, SEQ + 1])
        rsm = sc.sb("rp_rsm", [P, 2, NB, NQ + 1])
        shi = sc.sb("rp_shi", [P, 2, NB])
        xm = sc.sb("rp_xm", [P, 2, NT])
        sho = sc.sb("rp_sho", [P, 2, NB + 1])
        mu = sc.sb("rp_mu", [P, FR])
        muc = sc.sb("rp_muc", [P, 2])

        @block.sync
        def _(sp):
            def load(f, u):
                sp.dma_start(wt[:, u], w_rw[l, f]).then_inc(w_in[u], 16)
                sp.dma_start(shi[:, u, :], shift_in[l, f]).then_inc(s_in[u], 16)

            def store(f, u):
                sp.dma_start(xmT[f], xm[:, u, :]).then_inc(sent[u], 16)
                sp.dma_start(shift_out[l, f], sho[:, u, :]).then_inc(sent[u], 16)

            sp.sem_inc(sent[0], 32)
            sp.sem_inc(sent[1], 32)
            load(0, 0)
            load(1, 1)
            sp.dma_start(mu[:, :], mu_d).then_inc(mu_in, 16)
            with sp.Fori(0, FR // 2 - 1) as i:
                for u in range(2):
                    sp.wait_ge(mixed, 2 * i + u + 1)
                    sp.sem_inc(sp_hold, 1)
                    store(2 * i + u, u)
                    load(2 * i + u + 2, u)
            for u in range(2):
                sp.wait_ge(mixed, FR - 1 + u)
                store(FR - 2 + u, u)
            for u in range(2):
                sp.wait_ge(sent[u], 32 * (FR // 2 + 1))

        @block.tensor
        def _(pe):
            with pe.Fori(0, FR // 2) as i:
                for u in range(2):
                    pe.wait_ge(w_in[u], 16 * i + 16)
                    pe.wait_ge(raw_ready, 2 * i + u + 1)
                    for k in range(KD):
                        for n, (o, w) in enumerate(GROUPS):
                            b = (3 * u + n) * BANK
                            m = pe.matmul(ps[:, b:b + w], wt[:, u, k, :], xn[:, k, o:o + w],
                                          start=(k == 0), stop=(k == KD - 1))
                    m.then_inc(products, 1)

        @block.scalar
        def _(act):
            act.sem_inc(raw_ready, 2)
            with act.Fori(0, FR // 2) as i:
                for u in range(2):
                    act.wait_ge(products, 2 * i + u + 1)
                    act.wait_ge(raw_read, 2 * i + u + 1)
                    b = 3 * u * BANK
                    act.copy(raw[:, u, 1:385], ps[:, b:b + 384])
                    act.copy(raw[:, u, 385:769], ps[:, b + BANK:b + BANK + 384])
                    act.copy(raw[:, u, 769:1025], ps[:, b + 2 * BANK:b + 2 * BANK + 256])
                    act.copy(rsm[:, u, :, 1:NQ + 1],
                             ps[:, b + 2 * BANK + 256:b + 2 * BANK + 320].rearrange("p (b q) -> p b q", b=NB)).then_inc(raw_ready, 1)

        @block.vector
        def _(dve):
            dve.memset(raw[:, :, 0:1], 0.0).then_inc(zeroed, 1)
            dve.wait_ge(zeroed, 1)
            dve.sem_inc(raw_read, 2)
            dve.wait_ge(mu_in, 16)
            with dve.Fori(0, FR // 2) as i:
                for u in range(2):
                    dve.wait_ge(raw_ready, 2 * i + u + 3)
                    dve.wait_ge(s_in[u], 16 * i + 16)
                    dve.wait_ge(sent[u], 32 * i + 32)
                    dve.tensor_copy(rsm[:, u, :, 0], shi[:, u, :])
                    dve.tensor_copy(muc[:, u:u + 1], mu[:, ds(2 * i + u, 1)]).then_inc(chain_sem, 1)
                    dve.wait_ge(chain_sem, 2 * (2 * i + u) + 1)
                    dve.tensor_copy(sho[:, u, 0:1], raw[:, u, SEQ:SEQ + 1])
                    dve.tensor_copy(sho[:, u, 1:NB + 1], rsm[:, u, :, NQ])
                    xs = xm[:, u, SEQ:NT].rearrange("p (b q) -> p b q", b=NB)
                    dve.tensor_tensor(xm[:, u, 0:SEQ], raw[:, u, 0:SEQ], raw[:, u, 1:SEQ + 1], ALU.subtract)
                    dve.tensor_tensor(xs, rsm[:, u, :, 0:NQ], rsm[:, u, :, 1:NQ + 1], ALU.subtract).then_inc(chain_sem, 1)
                    dve.wait_ge(chain_sem, 2 * (2 * i + u) + 2)
                    dve.scalar_tensor_tensor(out=xm[:, u, 0:SEQ], in0=xm[:, u, 0:SEQ], scalar=muc[:, u:u + 1],
                                             in1=raw[:, u, 1:SEQ + 1], op0=ALU.mult, op1=ALU.add)
                    dve.scalar_tensor_tensor(out=xs, in0=xs, scalar=muc[:, u:u + 1], in1=rsm[:, u, :, 1:NQ + 1],
                                             op0=ALU.mult, op1=ALU.add).then_inc(mixed, 1)
                    dve.wait_ge(mixed, 2 * i + u + 1)
                    dve.sem_inc(raw_read, 1)


def rwkv_features(nc, ps, cst, l, xmT, lora_d, vec_d, arbk_d, rk_d, wend, const_d):
    with Scope(nc) as sc:
        wa = sc.sb("rf_wa", [P, NT])
        restart = sc.sb("rf_restart", [P, NT])
        vec = sc.sb("rf_vec", [P, 4, 4])
        vc = sc.sb("rf_vc", [P, 4])
        lora = sc.sb("rf_lora", [P, P])
        r, k, sw, a, ld, w, wp, wi, kk, t1 = (sc.sb(f"rf_{n}", [P, NT]) for n in
                                              ("r", "k", "sw", "a", "ld", "w", "wp", "wi", "kk", "t1"))
        rk = sc.sb("rf_rk", [P, NT])
        out = sc.sb("rf_out", [P, NCH + 1, 4, CH])
        with stage(nc, "loaded tanned") as (block, loaded, tanned):
            @block.sync
            def _(sp):
                sp.dma_start(wa[:, :], xmT[12]).then_inc(loaded, 16)
                sp.dma_start(vec[:, :, :], vec_d).then_inc(loaded, 16)
                sp.dma_start(restart[:, :], const_d[:, CO["restart"][0]:CO["restart"][0] + NT]).then_inc(loaded, 16)
                sp.wait_ge(loaded, 48)

            @block.scalar
            def _(act):
                act.wait_ge(loaded, 48)
                act.activation(wa[0:64, :], wa[0:64, :], ACT.Tanh).then_inc(tanned, 1)

        with nc.Fori(0, 4) as hp, stage(nc, "r_in lora_in vec_ready z_done gates_ready chain cum_ready prev_ready decays sq_ready sq_done sum_ready rooted ready stored") as (
                block, r_in, lora_in, vec_ready, z_done, gates_ready, chain_sem, cum_ready, prev_ready, decays, sq_ready, sq_done, sum_ready, rooted, ready, stored):

            @block.sync
            def _(sp):
                sp.dma_start(lora[:, :], lora_d[:, ds(hp * P, P)]).then_inc(lora_in, 16)
                sp.dma_start(r[:, :], xmT[hp]).then_inc(r_in, 16)
                sp.dma_start(k[:, :], xmT[hp + 4]).then_inc(r_in, 16)
                sp.wait_ge(ready, 1)
                sp.dma_start(arbk_d[:, :, hp].rearrange("c p n -> p c n"), out[:, :, :, :].rearrange("p c a t -> p c (a t)")).then_inc(stored, 16)
                sp.dma_start(rk_d[hp], rk[:, :]).then_inc(stored, 16)
                sp.wait_ge(stored, 32)

            @block.tensor
            def _(pe):
                pe.wait_ge(lora_in, 16)
                for half in range(2):
                    for n, (o, c) in enumerate(GROUPS):
                        b = (3 * half + n) * BANK
                        m = pe.matmul(ps[:, b:b + c], lora[64 * half:64 * half + 64, :], wa[64 * half:64 * half + 64, o:o + c], start=True, stop=True)
                    m.then_inc(z_done, 1)
                pe.wait_ge(sq_ready, 1)
                pe.wait_ge(gates_ready, 1)
                for n, (o, c) in enumerate(GROUPS):
                    m = pe.matmul(ps[:, n * BANK:n * BANK + c], cst["blk"], t1[:, o:o + c], start=True, stop=True)
                m.then_inc(sq_done, 1)

            @block.scalar
            def _(act):
                act.wait_ge(vec_ready, 1)
                for half, dst in enumerate((sw, a)):
                    act.wait_ge(z_done, half + 1)
                    for n, (o, c) in enumerate(GROUPS):
                        b = (3 * half + n) * BANK
                        m = act.activation(dst[:, o:o + c], ps[:, b:b + c], ACT.Sigmoid, bias=vc[:, half:half + 1])
                    m.then_inc(gates_ready, 1)
                act.wait_ge(cum_ready, 1)
                act.activation(w[:, :], wp[:, :], ACT.Exp)
                act.activation(wi[:, :], wp[:, :], ACT.Exp, scale=-1.0).then_inc(decays, 1)
                act.wait_ge(prev_ready, 1)
                act.activation(ld[:, :], ld[:, :], ACT.Exp).then_inc(decays, 1)
                act.wait_ge(sum_ready, 1)
                act.activation(t1[:, :], t1[:, :], ACT.Sqrt).then_inc(rooted, 1)

            @block.vector
            def _(dve):
                step = Chain(dve, chain_sem)
                for n in range(4):
                    m = dve.tensor_copy(vc[:, n:n + 1], vec[:, n, ds(hp, 1)])
                m.then_inc(vec_ready, 1)
                dve.wait_ge(vec_ready, 1)
                dve.wait_ge(r_in, 32)
                step(dve.tensor_scalar(kk[:, :], k[:, :], vc[:, 2:3], None, ALU.mult))
                dve.tensor_tensor(t1[:, :], kk[:, :], kk[:, :], ALU.mult).then_inc(sq_ready, 1)
                dve.wait_ge(gates_ready, 1)
                step(dve.tensor_scalar(ld[:, :], sw[:, :], -E05, None, ALU.mult))
                step(dve.tensor_tensor_scan(wp[:, :], restart[:, :], ld[:, :], 0.0, ALU.mult, ALU.add))
                dve.tensor_tensor(ld[:, :], wp[:, :], ld[:, :], ALU.subtract).then_inc(prev_ready, 1)
                dve.sem_inc(cum_ready, 1)
                dve.wait_ge(gates_ready, 2)
                step(dve.tensor_scalar(sw[:, :], a[:, :], 1.0, vc[:, 3:4], ALU.subtract, ALU.mult))
                step(dve.scalar_tensor_tensor(out=sw[:, :], in0=sw[:, :], scalar=1.0, in1=k[:, :], op0=ALU.add, op1=ALU.mult))
                dve.tensor_tensor(rk[:, :], r[:, :], sw[:, :], ALU.mult)
                dve.wait_ge(sq_done, 1)
                for n, (o, c) in enumerate(GROUPS):
                    m = dve.tensor_scalar(t1[:, o:o + c], ps[:, n * BANK:n * BANK + c], 1e-24, None, ALU.max)
                m.then_inc(sum_ready, 1)
                dve.wait_ge(rooted, 1)
                step(dve.reciprocal(t1[:, :], t1[:, :]))
                step(dve.tensor_tensor(kk[:, :], kk[:, :], t1[:, :], ALU.mult))
                dve.wait_ge(decays, 2)

                def parts(x):
                    return x[:, :].rearrange("p (c t) -> p c t", t=CH)

                step(dve.tensor_tensor(out[:, :, 1, :], parts(r), parts(w), ALU.mult))
                dve.scalar_tensor_tensor(out=out[:, :, 0, :], in0=parts(kk), scalar=-1.0, in1=parts(ld), op0=ALU.mult, op1=ALU.mult)
                step(dve.tensor_tensor(out[:, :, 3, :], parts(sw), parts(wi), ALU.mult))
                step(dve.tensor_tensor(kk[:, :], kk[:, :], a[:, :], ALU.mult))
                dve.tensor_tensor(out[:, :, 2, :], parts(kk), parts(wi), ALU.mult)
                dve.tensor_copy(wend[:, ds(hp, 1), 0:NCH], w[:, CH - 1:SEQ:CH].unsqueeze(1))
                dve.tensor_copy(wend[:, ds(hp, 1), NCH:NCH + NB], w[:, SEQ + NQ - 1:NT:NQ].unsqueeze(1)).then_inc(ready, 1)


def rwkv_chunk(nc, ps, cst, c, sample, bufs, S, wend, arbk_d, xmT, yr_d, vr_d):
    arbk, vT, G, CT, X, XT, ys, p1, bkr, UV, yo, masks, AM, RM, S8, UVm = bufs
    levels = 3 if sample else 6
    gm = masks[:, 0:P]
    with stage(nc, "in_ gram gram_masked rows rows_copied ct_ready y_done y_copied z_done x_done am_ready p1_done p1_copied u_done u_copied out_done out_copied uvm_ready st_done chain ident_ready stored") as (
            block, in_, gram, gram_masked, rows, rows_copied, ct_ready, y_done, y_copied, z_done, x_done, am_ready,
            p1_done, p1_copied, u_done, u_copied, out_done, out_copied, uvm_ready, st_done, chain_sem, ident_ready, stored):

        def at(h):
            return h % 4, 64 * (h // 4)

        @block.sync
        def _(sp):
            sp.dma_start(arbk[:, :, :, :], arbk_d[c].rearrange("p h (a t) -> p h a t", a=4)).then_inc(in_, 16)
            sp.dma_start(vT[:, :, :], xmT[8:12, :, ds(c * CH, CH)].rearrange("h p t -> p h t")).then_inc(in_, 16)
            sp.wait_ge(out_copied, 1)
            sp.dma_start(yr_d[ds(c * CH, CH), :], yo[:, :]).then_inc(stored, 16)
            sp.dma_start(vr_d[ds(c * CH, CH), :], UV[64:128, :]).then_inc(stored, 16)
            sp.wait_ge(stored, 32)

        @block.tensor
        def _(pe):
            pe.wait_ge(in_, 32)
            for h in range(HH):
                hp, b = at(h)
                m = pe.matmul(ps[:, h * P:(h + 1) * P], arbk[b:b + 64, hp, 2:4, :].rearrange("p a t -> p (a t)"),
                              arbk[b:b + 64, hp, 0:2, :].rearrange("p a t -> p (a t)"), start=True, stop=True)
            m.then_inc(gram, 1)
            for hp in range(4):
                pe.transpose(ps[:, 2 * BANK + hp * P:2 * BANK + (hp + 1) * P], arbk[:, hp, 2:4, :].rearrange("p a t -> p (a t)"), cst["ident"])
                m = pe.matmul(ps[64:128, 3 * BANK + hp * P:3 * BANK + (hp + 1) * P], vT[:, hp, :], cst["ident"], start=True, stop=True)
            m.then_inc(rows, 1)

            def with_state(banks, which, masked):
                for h in range(HH):
                    hp, b = at(h)
                    o = ps[0:64, banks[h // 4] * BANK + hp * 64:banks[h // 4] * BANK + (hp + 1) * 64]
                    if sample:
                        for n in range(NB):
                            pe.matmul(o, masked[b:b + 64, hp, n, :], S8[b:b + 64, hp, n, :], start=(n == 0), stop=False)
                    else:
                        pe.matmul(o, arbk[b:b + 64, hp, which, :], S[b:b + 64, hp, :], start=True, stop=False)
                    m = pe.matmul(o, G[:, h, 64 * which:64 * which + 64], UV[:, h * 64:(h + 1) * 64], start=False, stop=True)
                return m

            pe.wait_ge(gram_masked, 2)
            pe.wait_ge(rows_copied, 1)
            if sample:
                pe.wait_ge(am_ready, 1)
            pe.wait_ge(ident_ready, 1)
            with_state((7, 3), 0, AM).then_inc(p1_done, 1)
            for n in range(levels):
                pe.wait_ge(ct_ready, n + 1)
                if n:
                    pe.wait_ge(x_done, n)
                for h in range(HH):
                    m = pe.matmul(ps[0:64, 4 * BANK + h * 64:4 * BANK + (h + 1) * 64], CT[:, n % 2, h, :], X[:, h, :], start=True, stop=True)
                m.then_inc(y_done, 1)
                pe.wait_ge(y_copied, n + 1)
                for h in range(HH):
                    pe.matmul(ps[0:64, 5 * BANK + h * 64:5 * BANK + (h + 1) * 64], XT[:, h, :], ys[:, h, :], start=True, stop=True)
                    m = pe.matmul(ps[0:64, 6 * BANK + h * 64:6 * BANK + (h + 1) * 64], ys[:, h, :], XT[:, h, :], start=True, stop=True)
                m.then_inc(z_done, 1)
            pe.wait_ge(x_done, levels)
            pe.wait_ge(p1_copied, 1)
            for h in range(HH):
                m = pe.matmul(ps[0:64, h * 64:(h + 1) * 64], XT[:, h, :], p1[:, h * 64:(h + 1) * 64], start=True, stop=True)
            m.then_inc(u_done, 1)
            pe.wait_ge(u_copied, 1)
            with_state((0, 1), 1, RM).then_inc(out_done, 1)
            if sample:
                pe.wait_ge(uvm_ready, 1)
                for h in range(HH):
                    hp, b = at(h)
                    m = pe.matmul(ps[b:b + 64, (4 + hp) * BANK:(5 + hp) * BANK], bkr[:, hp * P + b:hp * P + b + 64],
                                  UVm[:, :, h * 64:(h + 1) * 64], start=True, stop=True)
            else:
                for h in range(HH):
                    hp, b = at(h)
                    m = pe.matmul(ps[b:b + 64, 2 * BANK + hp * 64:2 * BANK + (hp + 1) * 64], bkr[:, hp * P + b:hp * P + b + 64],
                                  UV[:, h * 64:(h + 1) * 64], start=True, stop=True)
            m.then_inc(st_done, 1)

        @block.scalar
        def _(act):
            act.wait_ge(rows, 1)
            act.copy(bkr[:, :], ps[:, 2 * BANK:3 * BANK])
            act.copy(UV[64:128, :].rearrange("p (e h d) -> p e h d", e=2, h=4),
                     ps[64:128, 3 * BANK:4 * BANK].rearrange("p (h e d) -> p e h d", h=4, e=2)).then_inc(rows_copied, 1)
            act.wait_ge(p1_done, 1)
            act.copy(p1[:, 0:256], ps[0:64, 7 * BANK:7 * BANK + 256])
            act.copy(p1[:, 256:512], ps[0:64, 3 * BANK:3 * BANK + 256]).then_inc(p1_copied, 1)
            for n in range(levels):
                act.wait_ge(y_done, n + 1)
                if n:
                    act.wait_ge(z_done, n)
                act.copy(ys[:, :, :], ps[0:64, 4 * BANK:5 * BANK].rearrange("p (h t) -> p h t", h=HH)).then_inc(y_copied, 1)
            act.wait_ge(u_done, 1)
            act.copy(UV[0:64, :], ps[0:64, 0:BANK]).then_inc(u_copied, 1)
            act.wait_ge(out_done, 1)
            act.copy(yo[:, 0:256], ps[0:64, 0:256])
            act.copy(yo[:, 256:512], ps[0:64, BANK:BANK + 256]).then_inc(out_copied, 1)

        @block.vector
        def _(dve):
            step = Chain(dve, chain_sem)
            dve.memset(UV[0:64, :], 0.0)
            dve.tensor_copy(X[:, :, :], mid(cst["ident"][0:64, 0:64], HH))
            dve.tensor_copy(XT[:, :, :], mid(cst["ident"][0:64, 0:64], HH)).then_inc(ident_ready, 1)
            dve.wait_ge(gram, 1)
            for n in range(2):
                dve.tensor_tensor(G[:, 4 * n:4 * n + 4, :], ps[:, n * BANK:(n + 1) * BANK].rearrange("p (h t) -> p h t", h=4),
                                  mid(gm, 4), ALU.mult).then_inc(gram_masked, 1)
            dve.wait_ge(gram_masked, 2)
            if sample:
                dve.wait_ge(in_, 32)
                for which, dst in ((0, AM), (1, RM)):
                    for hp in range(4):
                        m = dve.tensor_tensor(dst[:, hp], mid(arbk[:, hp, which, :], NB), masks[:, P + 384:P + 384 + 512].rearrange("p (b t) -> p b t", b=NB), ALU.mult)
                m.then_inc(am_ready, 1)
            for n in range(levels):
                if n >= 2:
                    dve.wait_ge(y_done, n - 1)
                dve.tensor_tensor(CT[:, n % 2], G[0:64, :, 0:64], mid(masks[0:64, P + n * 64:P + (n + 1) * 64], HH), ALU.mult).then_inc(ct_ready, 1)
                dve.wait_ge(z_done, n + 1)
                dve.tensor_tensor(X[:, :, :], X[:, :, :], ps[0:64, 5 * BANK:6 * BANK].rearrange("p (h t) -> p h t", h=HH), ALU.add)
                dve.tensor_tensor(XT[:, :, :], XT[:, :, :], ps[0:64, 6 * BANK:7 * BANK].rearrange("p (h t) -> p h t", h=HH), ALU.add).then_inc(x_done, 1)
                dve.wait_ge(x_done, n + 1)
            if sample:
                dve.wait_ge(u_copied, 1)
                for n in range(NB):
                    m = dve.tensor_scalar(UVm[:, n, :], UV[:, :], masks[:, P + 384 + 512 + n:P + 384 + 512 + n + 1], None, ALU.mult)
                m.then_inc(uvm_ready, 1)
                dve.wait_ge(st_done, 1)
                for hp in range(4):
                    dve.tensor_tensor(S8[:, hp], S8[:, hp], ps[:, (4 + hp) * BANK:(5 + hp) * BANK].rearrange("p (b t) -> p b t", b=NB), ALU.add).then_inc(chain_sem, 1)
                dve.wait_ge(chain_sem, 4)
                for hp in range(4):
                    dve.tensor_tensor(S8[:, hp], S8[:, hp], bc(wend[:, hp, NCH:NCH + NB], 64), ALU.mult)
            else:
                dve.wait_ge(st_done, 1)
                step(dve.tensor_tensor(S[:, :, :], S[:, :, :], ps[:, 2 * BANK:2 * BANK + 256].rearrange("p (h t) -> p h t", h=4), ALU.add))
                dve.tensor_tensor(S[:, :, :], S[:, :, :], wend[:, :, ds(c, 1)].to_broadcast([P, 4, 64]), ALU.mult)


def rwkv_scan(nc, ps, cst, l, wend, const_d, arbk_d, xmT, yr_d, vr_d, s_in, s_out):
    with Scope(nc) as sc:
        arbk = sc.sb("rc_arbk", [P, 4, 4, CH])
        vT = sc.sb("rc_vT", [P, 4, CH])
        G = sc.sb("rc_G", [P, HH, P])
        CT = sc.sb("rc_CT", [64, 2, HH, CH])
        X = sc.sb("rc_X", [64, HH, CH])
        XT = sc.sb("rc_XT", [64, HH, CH])
        ys = sc.sb("rc_ys", [64, HH, CH])
        p1 = sc.sb("rc_p1", [64, 512])
        bkr = sc.sb("rc_bkr", [P, 512])
        UV = sc.sb("rc_UV", [P, 512])
        yo = sc.sb("rc_yo", [64, 512])
        masks = sc.sb("rc_masks", [P, P + 384 + 512 + NB])
        S = sc.sb("rc_S", [P, 4, 64])
        AM = sc.sb("rc_AM", [P, 4, NB, CH])
        RM = sc.sb("rc_RM", [P, 4, NB, CH])
        S8 = sc.sb("rc_S8", [P, 4, NB, 64])
        UVm = sc.sb("rc_UVm", [P, NB, 512])
        bufs = (arbk, vT, G, CT, X, XT, ys, p1, bkr, UV, yo, masks, AM, RM, S8, UVm)
        with stage(nc, "loaded zeroed") as (block, loaded, zeroed):
            @block.sync
            def _(sp):
                o = 0
                for name in ("gmask", "lev", "seqt", "seqp"):
                    a, w = CO[name]
                    sp.dma_start(masks[:, o:o + w], const_d[:, a:a + w]).then_inc(loaded, 16)
                    o += w
                sp.dma_start(S8[:, :, :, :], s_in[l]).then_inc(loaded, 16)
                sp.wait_ge(loaded, 80)

            @block.vector
            def _(dve):
                dve.memset(S[:, :, :], 0.0).then_inc(zeroed, 1)

        with nc.Fori(0, NCH) as c:
            rwkv_chunk(nc, ps, cst, c, False, bufs, S, wend, arbk_d, xmT, yr_d, vr_d)
        with stage(nc, "loaded") as (block, loaded):
            @block.sync
            def _(sp):
                a, w = CO["gmask_s"]
                sp.dma_start(masks[:, 0:P], const_d[:, a:a + w]).then_inc(loaded, 16)
                sp.wait_ge(loaded, 16)
        rwkv_chunk(nc, ps, cst, NCH, True, bufs, S, wend, arbk_d, xmT, yr_d, vr_d)
        with stage(nc, "stored") as (block, stored):
            @block.sync
            def _(sp):
                sp.dma_start(s_out[l, :, :, 0], S[:, :, :]).then_inc(stored, 16)
                sp.dma_start(s_out[l, :, :, 1:NB + 1], S8[:, :, :, :]).then_inc(stored, 16)
                sp.wait_ge(stored, 32)


def rwkv_output(nc, ps, cst, l, mixT, xmT, rk_d, yr_d, vr_d, gb_d, gn_d, rk8_d):
    with Scope(nc) as sc:
        y, v, o, t1 = (sc.sb(f"ro_{n}", [P, 512]) for n in ("y", "v", "o", "t1"))
        rk = sc.sb("ro_rk", [P, 4, P])
        ga = sc.sb("ro_ga", [P, P])
        gb = sc.sb("ro_gb", [P, 512])
        gn = sc.sb("ro_gn", [P, 2, 512])
        rk8 = sc.sb("ro_rk8", [P, 4, 8])
        mean, var, bonus = (sc.sb(f"ro_{n}", [P, 8]) for n in ("mean", "var", "bonus"))
        with stage(nc, "loaded") as (block, loaded):
            @block.sync
            def _(sp):
                sp.dma_start(gb[:, :], gb_d[l]).then_inc(loaded, 16)
                for n in range(2):
                    sp.dma_start(gn[:, n], gn_d[l, n].partition_broadcast(P)).then_inc(loaded, 16)
                sp.dma_start(rk8[:, :, :], rk8_d[l]).then_inc(loaded, 16)
                sp.wait_ge(loaded, 64)

        def tile(t, m):
            with stage(nc, "y_in g_in sig g_done b_done chain centred var_ready rooted ready turned kept") as (
                    block, y_in, g_in, sig, g_done, b_done, chain_sem, centred, var_ready, rooted, ready, turned, kept):
                @block.sync
                def _(sp):
                    sp.dma_start(y[0:m, :], yr_d[ds(t * P, m), :]).then_inc(y_in, 16)
                    sp.dma_start(v[0:m, :], vr_d[ds(t * P, m), :]).then_inc(y_in, 16)
                    sp.dma_start(ga[:, 0:m], xmT[13, :, ds(t * P, m)]).then_inc(g_in, 16)
                    sp.dma_start(rk[:, :, 0:m], rk_d[:, :, ds(t * P, m)].rearrange("h p t -> p h t")).then_inc(g_in, 16)

                @block.scalar
                def _(act):
                    act.wait_ge(g_in, 32)
                    act.activation(ga[:, 0:m], ga[:, 0:m], ACT.Sigmoid).then_inc(sig, 1)
                    act.wait_ge(centred, 1)
                    act.activation(t1[0:m, :], y[0:m, :], ACT.Square).then_inc(sig, 1)
                    act.wait_ge(var_ready, 1)
                    act.activation(var[0:m, :], var[0:m, :], ACT.Sqrt).then_inc(rooted, 1)
                    act.wait_ge(turned, 1)
                    act.copy(mixT[:, 4:8, ds(t * P, m)], ps[:, 2 * BANK:3 * BANK].rearrange("p (h t) -> p h t", h=4)[:, :, 0:m]).then_inc(kept, 1)

                @block.tensor
                def _(pe):
                    pe.wait_ge(g_in, 32)
                    for hp in range(4):
                        mm = pe.matmul(ps[0:m, BANK:BANK + 8], rk[:, hp, 0:m], rk8[:, hp, :], start=(hp == 0), stop=(hp == 3))
                    mm.then_inc(b_done, 1)
                    pe.wait_ge(sig, 1)
                    pe.matmul(ps[0:m, 0:BANK], ga[:, 0:m], gb[:, :], start=True, stop=True).then_inc(g_done, 1)
                    pe.wait_ge(ready, 1)
                    for hp in range(4):
                        mm = pe.transpose(ps[:, 2 * BANK + hp * P:2 * BANK + hp * P + m], o[0:m, hp * P:(hp + 1) * P], cst["ident"][0:m, 0:m])
                    mm.then_inc(turned, 1)

                @block.vector
                def _(dve):
                    step = Chain(dve, chain_sem)

                    def hv(x):
                        return x[0:m, :].rearrange("p (h d) -> p h d", h=HH)

                    dve.wait_ge(y_in, 32)
                    step(dve.tensor_reduce(mean[0:m, :], hv(y), AX.X, ALU.add))
                    step(dve.tensor_scalar(mean[0:m, :], mean[0:m, :], 1.0 / HD, None, ALU.mult))
                    dve.tensor_tensor(hv(y), hv(y), bc(mean[0:m, :], HD), ALU.subtract).then_inc(centred, 1)
                    dve.wait_ge(b_done, 1)
                    step(dve.tensor_copy(bonus[0:m, :], ps[0:m, BANK:BANK + 8]))
                    dve.tensor_tensor(hv(v), hv(v), bc(bonus[0:m, :], HD), ALU.mult)
                    dve.wait_ge(sig, 2)
                    step(dve.tensor_reduce(var[0:m, :], hv(t1), AX.X, ALU.add))
                    dve.tensor_scalar(var[0:m, :], var[0:m, :], 1.0 / HD, 64e-5, ALU.mult, ALU.add).then_inc(var_ready, 1)
                    dve.wait_ge(rooted, 1)
                    step(dve.reciprocal(var[0:m, :], var[0:m, :]))
                    step(dve.tensor_tensor(hv(y), hv(y), bc(var[0:m, :], HD), ALU.mult))
                    step(dve.tensor_tensor(y[0:m, :], y[0:m, :], gn[0:m, 0, :], ALU.mult))
                    step(dve.tensor_tensor(y[0:m, :], y[0:m, :], gn[0:m, 1, :], ALU.add))
                    step(dve.tensor_tensor(y[0:m, :], y[0:m, :], v[0:m, :], ALU.add))
                    dve.wait_ge(g_done, 1)
                    dve.tensor_tensor(o[0:m, :], y[0:m, :], ps[0:m, 0:BANK], ALU.mult).then_inc(ready, 1)

        with nc.Fori(0, SEQ // P) as t:
            tile(t, P)
        tile(SEQ // P, NS)


def block_ranks(dve, step, sel, score, rows, g, nb, low, gt, eq, rank):
    a = score[0:rows].unsqueeze(2).to_broadcast([rows, g, nb, nb])
    b = bc(score[0:rows], nb)
    lo = low[0:rows].rearrange("p (s t) -> p s t", s=nb).unsqueeze(1).to_broadcast([rows, g, nb, nb])
    for n in range(g):
        dve.tensor_tensor(gt[0:rows, n], a[:, n], b[:, n], ALU.is_gt)
        m = dve.tensor_tensor(eq[0:rows, n], a[:, n], b[:, n], ALU.is_equal)
    step(m)
    for n in range(g):
        m = dve.tensor_tensor(eq[0:rows, n], eq[0:rows, n], lo[:, n], ALU.mult)
    step(m)
    step(dve.tensor_tensor(gt[0:rows], gt[0:rows], eq[0:rows], ALU.add))
    step(dve.tensor_reduce(rank[0:rows], gt[0:rows], AX.X, ALU.add))
    return dve.tensor_scalar(sel, rank[0:rows], 7.5, NEG, ALU.is_ge, ALU.mult)


class Compressor:

    def __init__(self, nc, sc):
        self.kvp = sc.sb("cp_kvp", [P, 4, 1024])
        self.kvc = sc.sb("cp_kvc", [P, 4, 4, P])
        self.kt = sc.sb("cp_kt", [P, 4, 512])
        self.w1 = sc.sb("cp_w1", [P, 2, 16, 256])
        self.w2 = sc.sb("cp_w2", [P, 2, 2, HD])
        self.pe_ = sc.sb("cp_pe", [P, 2, 16])
        self.bias = sc.sb("cp_bias", [P, 4])
        self.hid = sc.sb("cp_hid", [P, 2, 2, 2, 64])
        self.kc = sc.sb("cp_kc", [P, 64])
        self.vc = sc.sb("cp_vc", [64, 2, HD])

    def weights(self, nc, ps, l, w1_d, w2_d, pe_d):
        with stage(nc, "loaded bias_done zeroed") as (block, loaded, bias_done, zeroed):
            @block.sync
            def _(sp):
                for n in range(2):
                    sp.dma_start(self.w1[:, n], w1_d[l, n]).then_inc(loaded, 16)
                    sp.dma_start(self.w2[:, n], w2_d[l, n]).then_inc(loaded, 16)
                    sp.dma_start(self.pe_[:, n], pe_d[l, n]).then_inc(loaded, 16)

            @block.tensor
            def _(pe):
                pe.wait_ge(loaded, 96)
                for n in range(4):
                    for q in range(16):
                        m = pe.matmul(ps[:, n:n + 1], self.w1[:, n // 2, q, (n % 2) * P:(n % 2 + 1) * P],
                                      self.pe_[:, n // 2, q:q + 1], start=(q == 0), stop=(q == 15))
                m.then_inc(bias_done, 1)

            @block.vector
            def _(dve):
                dve.memset(self.hid[:, :, :, :, :], 0.0).then_inc(zeroed, 1)
                dve.wait_ge(bias_done, 1)
                dve.tensor_copy(self.bias[:, :], ps[:, 0:4])
                dve.wait_ge(zeroed, 1)

    def run(self, nc, ps, cst, loads, extra=None):
        with stage(nc, "loaded sorted_ turned odd_copied even_copied hidden hid_ready c_done") as (
                block, loaded, sorted_, turned, odd_copied, even_copied, hidden, hid_ready, c_done):
            count = []

            @block.sync
            def _(sp):
                count.append(loads(sp, loaded))
                sp.wait_ge(loaded, count[0])

            @block.tensor
            def _(pe):
                for kg in range(4):
                    pe.wait_ge(sorted_, 4)
                    for n in range(4):
                        m = pe.transpose(ps[:, kg * BANK + n * P:kg * BANK + (n + 1) * P], self.kvc[:, n, kg, :], cst["ident"])
                    m.then_inc(turned, 1)
                for kv in range(2):
                    pe.wait_ge(even_copied, kv + 1)
                    pe.wait_ge(odd_copied, kv + 1)
                    for half in range(2):
                        b = (4 + 2 * kv + half) * BANK
                        for q in range(16):
                            m = pe.matmul(ps[:, b:b + 126], self.w1[:, kv, q, half * P:(half + 1) * P],
                                          self.kt[:, 2 * kv:2 * kv + 2, q:q + 8 * 62 + 1:8], start=(q == 0), stop=(q == 15))
                        m.then_inc(hidden, 1)
                pe.wait_ge(hid_ready, 4)
                for g in range(2):
                    for half in range(2):
                        pe.matmul(ps[64 * g:64 * g + 64, 0:64], self.w2[:, 0, half, :], self.hid[:, 0, half, g, :], start=(half == 0), stop=(half == 1))
                for g in range(2):
                    for half in range(2):
                        m = pe.matmul(ps[0:64, BANK + g * 64:BANK + g * 64 + 64], self.hid[:, 1, half, g, :], self.w2[:, 1, half, :], start=(half == 0), stop=(half == 1))
                m.then_inc(c_done, 1)

            @block.vector
            def _(dve):
                dve.wait_ge(loaded, count[0])
                for n in range(4):
                    dve.tensor_copy(self.kvc[:, n].rearrange("p kg (e d) -> p e kg d", e=2),
                                    self.kvp[:, n].rearrange("p (e a kg d) -> p e a kg d", e=2, a=2, kg=4)[:, :, 0]).then_inc(sorted_, 1)
                for kg in range(1, 4, 2):
                    dve.wait_ge(turned, kg + 1)
                    dve.tensor_copy(self.kt[:, kg, :], ps[:, kg * BANK:(kg + 1) * BANK]).then_inc(odd_copied, 1)
                dve.wait_ge(c_done, 1)
                dve.tensor_copy(self.kc[:, :], ps[:, 0:64])
                dve.tensor_copy(self.vc[:, :, :], ps[0:64, BANK:BANK + P].rearrange("p (g d) -> p g d", g=2))

            @block.scalar
            def _(act):
                for kg in range(0, 4, 2):
                    act.wait_ge(turned, kg + 1)
                    act.copy(self.kt[:, kg, :], ps[:, kg * BANK:(kg + 1) * BANK]).then_inc(even_copied, 1)
                for n in range(4):
                    act.wait_ge(hidden, n + 1)
                    b = (4 + n) * BANK
                    act.activation(self.hid[:, n // 2, n % 2, :, 0:63], ps[:, b:b + 126].rearrange("p (g c) -> p g c", g=2),
                                   ACT.Silu, bias=self.bias[:, n:n + 1]).then_inc(hid_ready, 1)


def sample_attention(nc, ps, cst, l, cp, qT, cache, ptab, kvrows, winr, gs_d, os_d, state_win, const_d):
    with Scope(nc) as sc:
        q = sc.sb("sa_q", [P, R4, NQ])
        wk = sc.sb("sa_wk", [P, 2, 256])
        kn = sc.sb("sa_kn", [NQ, 512])
        wn = sc.sb("sa_wn", [NQ, 256])
        g3 = sc.sb("sa_g3", [64, 3, 8])
        ksT = sc.sb("sa_ksT", [P, 2, 512])
        wT = sc.sb("sa_wT", [P, 272])
        s = sc.sb("sa_s", [64, 1032])
        sw = sc.sb("sa_sw", [64, 264])
        pT = sc.sb("sa_pT", [P, 9, 64])
        pwT = sc.sb("sa_pwT", [P, 3, 64])
        pc = sc.sb("sa_pc", [64, 64])
        pcT = sc.sb("sa_pcT", [64, 64])
        pg = sc.sb("sa_pg", [64, 72])
        im = sc.sb("sa_im", [64, 17])
        im2 = sc.sb("sa_im2", [64, 1, 17])
        sel = sc.sb("sa_sel", [64, 1, 17])
        gt = sc.sb("sa_gt", [64, 1, 17, 17])
        eq = sc.sb("sa_eq", [64, 1, 17, 17])
        rank = sc.sb("sa_rank", [64, 1, 17])
        st = sc.sb("sa_st", [64, 16])
        o = sc.sb("sa_o", [64, HD])
        names = ("low17", "swin", "snew", "skeep", "sadd", "hsel", "same")
        off, w = {}, 0
        for n in names:
            off[n] = w
            w += CO[n][1]
        cm = sc.sb("sa_cm", [64, w])
        K = {n: cm[:, off[n]:off[n] + CO[n][1]] for n in names}
        with stage(nc, "loaded zeroed") as (block, loaded, zeroed):
            @block.sync
            def _(sp):
                for n in names:
                    a, ww = CO[n]
                    sp.dma_start(cm[:, off[n]:off[n] + ww], const_d[0:64, a:a + ww]).then_inc(loaded, 16)
                sp.wait_ge(loaded, 16 * len(names))

            @block.vector
            def _(dve):
                dve.memset(pg[:, :], 0.0).then_inc(zeroed, 1)

        with nc.Fori(0, NB) as b:
            def loads(sp, sem):
                for p in range(PAGES):
                    page = sp.value_load(ptab[0:1, ds(b * PAGES + p, 1)], min_val=0, max_val=NPHYS - 1)
                    sp.dma_start(cp.kvp[64 * (p % 2):64 * (p % 2) + 64, p // 2, :], cache[l, page]).then_inc(sem, 16)
                sp.dma_start(wk[:, :, :], state_win[l, b].rearrange("(h p) n -> p h n", p=P)).then_inc(sem, 16)
                sp.dma_start(kn[:, :], kvrows[l, ds(SEQ + b * NQ, NQ), :]).then_inc(sem, 16)
                sp.dma_start(wn[:, :], winr[ds(SEQ + b * NQ, NQ), :]).then_inc(sem, 16)
                for gr in range(8):
                    src = gs_d[ds(b * NQ, NQ), :].rearrange("q (c h) -> q c h", c=3)
                    sp.dma_start(g3[gr * 8:gr * 8 + 8, :, :], src).then_inc(sem, 16)
                return 16 * (PAGES + 11)

            cp.run(nc, ps, cst, loads)
            with stage(nc, "q_ready turned k_copied c_scored s_scored w_scored c_masked c_exp c_ready c_turned c_copied c_out imp_ready imp_done s_masked s_exp s_turned s_copied s_out w_masked w_exp w_turned w_copied w_out chain out_ready stored") as (
                    block, q_ready, turned, k_copied, c_scored, s_scored, w_scored, c_masked, c_exp, c_ready, c_turned, c_copied, c_out, imp_ready, imp_done,
                    s_masked, s_exp, s_turned, s_copied, s_out, w_masked, w_exp, w_turned, w_copied, w_out, chain_sem, out_ready, stored):
                @block.sync
                def _(sp):
                    sp.wait_ge(out_ready, 1)
                    for g in range(2):
                        for r in range(R4):
                            row = g * 32 + r * 8
                            sp.dma_start(os_d[ds(b * NQ, NQ), r * P + g * HD:r * P + (g + 1) * HD], o[row:row + 8, :]).then_inc(stored, 16)
                    sp.wait_ge(stored, 128)

                @block.tensor
                def _(pe):
                    for e in range(2):
                        for n in range(4):
                            m = pe.transpose(ps[:, e * BANK + n * P:e * BANK + (n + 1) * P], cp.kvp[:, n, e * 512 + 256:e * 512 + 384], cst["ident"])
                    m.then_inc(turned, 1)
                    for n in range(2):
                        pe.transpose(ps[:, 2 * BANK + n * P:2 * BANK + (n + 1) * P], wk[:, n, 0:P], cst["ident"])
                    pe.transpose(ps[:, 2 * BANK + 256:2 * BANK + 264], wn[:, 0:P], cst["ident"][0:8, 0:8])
                    pe.transpose(ps[:, 2 * BANK + 264:2 * BANK + 272], kn[:, 256:384], cst["ident"][0:8, 0:8]).then_inc(turned, 1)
                    pe.wait_ge(q_ready, 1)
                    for g in range(2):
                        ql = q[64 * g:64 * g + 64, :, :].rearrange("p r t -> p (r t)")
                        m = pe.matmul(ps[32 * g:32 * g + 32, 3 * BANK:3 * BANK + 64], ql, cp.kc[64 * g:64 * g + 64, :], start=True, stop=True)
                    m.then_inc(c_scored, 1)
                    pe.wait_ge(k_copied, 2)
                    for g in range(2):
                        ql = q[64 * g:64 * g + 64, :, :].rearrange("p r t -> p (r t)")
                        rows = slice(32 * g, 32 * g + 32)
                        for e in range(2):
                            pe.matmul(ps[rows, (4 + e) * BANK:(5 + e) * BANK], ql, ksT[64 * g:64 * g + 64, e, :], start=True, stop=True)
                        pe.matmul(ps[rows, 6 * BANK:6 * BANK + 8], ql, wT[64 * g:64 * g + 64, 264:272], start=True, stop=True)
                        m = pe.matmul(ps[rows, 7 * BANK:7 * BANK + 264], ql, wT[64 * g:64 * g + 64, 0:264], start=True, stop=True)
                    m.then_inc(s_scored, 1)
                    pe.wait_ge(c_ready, 1)
                    pe.transpose(ps[0:64, 2 * BANK:2 * BANK + 64], pc[:, :], cst["ident"][0:64, 0:64]).then_inc(c_turned, 1)
                    pe.wait_ge(imp_ready, 1)
                    pe.matmul(ps[0:64, 0:17], K["same"], im[:, :], start=True, stop=True).then_inc(imp_done, 1)
                    pe.wait_ge(c_copied, 1)
                    for g in range(2):
                        m = pe.matmul(ps[32 * g:32 * g + 32, 3 * BANK + 64:3 * BANK + 128], pcT[0:63, 32 * g:32 * g + 32], cp.vc[0:63, g, :], start=True, stop=True)
                    m.then_inc(c_out, 1)
                    pe.wait_ge(w_exp, 1)
                    for n in range(2):
                        pe.transpose(ps[:, BANK + n * 64:BANK + n * 64 + 64], sw[:, n * P:(n + 1) * P], cst["ident"][0:64, 0:64])
                    pe.transpose(ps[0:8, BANK + 128:BANK + 192], sw[:, 256:264], cst["ident"][0:64, 0:64]).then_inc(w_turned, 1)
                    pe.wait_ge(w_copied, 1)
                    for g in range(2):
                        oo = ps[32 * g:32 * g + 32, 7 * BANK:7 * BANK + 64]
                        for n in range(2):
                            pe.matmul(oo, pwT[:, n, 32 * g:32 * g + 32], wk[:, n, P + g * HD:P + (g + 1) * HD], start=(n == 0), stop=False)
                        m = pe.matmul(oo, pwT[0:8, 2, 32 * g:32 * g + 32], wn[:, P + g * HD:P + (g + 1) * HD], start=False, stop=True)
                    m.then_inc(w_out, 1)
                    pe.wait_ge(s_exp, 1)
                    for n in range(8):
                        pe.transpose(ps[:, n * 64:n * 64 + 64], s[:, n * P:(n + 1) * P], cst["ident"][0:64, 0:64])
                    pe.transpose(ps[0:8, BANK + 192:BANK + 256], s[:, 1024:1032], cst["ident"][0:64, 0:64]).then_inc(s_turned, 1)
                    pe.wait_ge(s_copied, 1)
                    for g in range(2):
                        oo = ps[32 * g:32 * g + 32, 4 * BANK:4 * BANK + 64]
                        for n in range(8):
                            e, pp = n // 4, n % 4
                            v = cp.kvp[:, pp, e * 512 + 384 + g * HD:e * 512 + 384 + (g + 1) * HD]
                            pe.matmul(oo, pT[:, n, 32 * g:32 * g + 32], v, start=(n == 0), stop=False)
                        m = pe.matmul(oo, pT[0:8, 8, 32 * g:32 * g + 32], kn[:, 384 + g * HD:384 + (g + 1) * HD], start=False, stop=True)
                    m.then_inc(s_out, 1)

                @block.scalar
                def _(act):
                    act.wait_ge(turned, 1)
                    act.copy(ksT[:, :, :], ps[:, 0:1024].rearrange("p (e n) -> p e n", e=2)).then_inc(k_copied, 1)
                    act.wait_ge(turned, 2)
                    act.copy(wT[:, :], ps[:, 2 * BANK:2 * BANK + 272]).then_inc(k_copied, 1)
                    act.wait_ge(c_masked, 1)
                    act.activation(pc[:, :], pc[:, :], ACT.Exp, bias=st[:, 1:2], scale=SCALE).then_inc(c_exp, 1)
                    act.wait_ge(c_turned, 1)
                    act.copy(pcT[:, :], ps[0:64, 2 * BANK:2 * BANK + 64]).then_inc(c_copied, 1)
                    act.wait_ge(w_masked, 1)
                    act.activation(sw[:, :], sw[:, :], ACT.Exp, bias=st[:, 5:6], scale=SCALE, accum_out=st[:, 6:7]).then_inc(w_exp, 1)
                    act.wait_ge(w_turned, 1)
                    act.copy(pwT[:, 0:2, :], ps[:, BANK:BANK + 128].rearrange("p (n t) -> p n t", n=2))
                    act.copy(pwT[0:8, 2, :], ps[0:8, BANK + 128:BANK + 192]).then_inc(w_copied, 1)
                    act.wait_ge(s_masked, 1)
                    act.activation(s[:, :], s[:, :], ACT.Exp, bias=st[:, 9:10], scale=SCALE, accum_out=st[:, 10:11]).then_inc(s_exp, 1)
                    act.wait_ge(s_turned, 1)
                    act.copy(pT[:, 0:8, :], ps[:, 0:512].rearrange("p (n t) -> p n t", n=8))
                    act.copy(pT[0:8, 8, :], ps[0:8, BANK + 192:BANK + 256]).then_inc(s_copied, 1)

                @block.vector
                def _(dve):
                    step = Chain(dve, chain_sem)
                    dve.tensor_copy(q[:, :, :], qT[:, :, ds(SEQ + b * NQ, NQ)]).then_inc(q_ready, 1)
                    dve.wait_ge(c_scored, 1)
                    step(dve.tensor_copy(pc[:, 0:63], ps[0:64, 3 * BANK:3 * BANK + 63]))
                    dve.memset(pc[:, 63:64], NEG)
                    step(dve.tensor_reduce(st[:, 0:1], pc[:, 0:63], AX.X, ALU.max))
                    step(dve.tensor_scalar(st[:, 1:2], st[:, 0:1], -SCALE, None, ALU.mult))
                    dve.sem_inc(c_masked, 1)
                    dve.wait_ge(c_exp, 1)
                    step(dve.tensor_reduce(st[:, 2:3], pc[:, 0:63], AX.X, ALU.add))
                    step(dve.reciprocal(st[:, 3:4], st[:, 2:3]))
                    step(dve.tensor_scalar(pc[:, :], pc[:, :], st[:, 3:4], None, ALU.mult))
                    dve.sem_inc(c_ready, 1)
                    step(dve.tensor_copy(pg[:, 1:65], pc[:, :]))
                    step(dve.tensor_reduce(im[:, :], pg[:, 1:69].rearrange("p (s c) -> p s c", c=4), AX.X, ALU.add))
                    step(dve.tensor_tensor(im[:, :], im[:, :], pg[:, 0:65:4], ALU.add))
                    dve.sem_inc(imp_ready, 1)
                    dve.wait_ge(s_scored, 1)
                    step(dve.tensor_tensor(sw[:, :], ps[0:64, 7 * BANK:7 * BANK + 264], K["swin"], ALU.add))
                    step(dve.tensor_reduce(st[:, 4:5], sw[:, :], AX.X, ALU.max))
                    step(dve.tensor_scalar(st[:, 5:6], st[:, 4:5], -SCALE, None, ALU.mult))
                    dve.sem_inc(w_masked, 1)
                    dve.wait_ge(imp_done, 1)
                    step(dve.tensor_tensor(im2[:, 0, :], ps[0:64, 0:17], K["skeep"], ALU.mult))
                    step(dve.tensor_tensor(im2[:, 0, :], im2[:, 0, :], K["sadd"], ALU.add))
                    step(block_ranks(dve, step, sel[:, :, :], im2, 64, 1, 17, K["low17"], gt, eq, rank))
                    for e in range(2):
                        dve.tensor_tensor(s[:, e * 512:(e + 1) * 512].rearrange("p (s t) -> p s t", s=16),
                                          ps[0:64, (4 + e) * BANK:(5 + e) * BANK].rearrange("p (s t) -> p s t", s=16),
                                          bc(sel[:, 0, 0:16], 32), ALU.add)
                    step(dve.scalar_tensor_tensor(out=s[:, 1024:1032], in0=ps[0:64, 6 * BANK:6 * BANK + 8], scalar=sel[:, 0, 16:17], in1=K["snew"], op0=ALU.add, op1=ALU.add))
                    step(dve.tensor_reduce(st[:, 8:9], s[:, :], AX.X, ALU.max))
                    step(dve.tensor_scalar(st[:, 9:10], st[:, 8:9], -SCALE, None, ALU.mult))
                    dve.sem_inc(s_masked, 1)
                    dve.wait_ge(w_exp, 1)
                    dve.reciprocal(st[:, 7:8], st[:, 6:7])
                    dve.wait_ge(s_exp, 1)
                    step(dve.reciprocal(st[:, 11:12], st[:, 10:11]))
                    step(dve.tensor_tensor(g3[:, :, :], g3[:, :, :], K["hsel"].rearrange("p (a b) -> p a b", a=1).to_broadcast([64, 3, 8]), ALU.mult))
                    step(dve.tensor_reduce(st[:, 12:15], g3[:, :, :], AX.X, ALU.add))
                    dve.tensor_tensor(st[:, 13:14], st[:, 13:14], st[:, 11:12], ALU.mult)
                    step(dve.tensor_tensor(st[:, 14:15], st[:, 14:15], st[:, 7:8], ALU.mult))
                    dve.wait_ge(c_out, 1)
                    step(dve.tensor_scalar(o[:, :], ps[0:64, 3 * BANK + 64:3 * BANK + 128], st[:, 12:13], None, ALU.mult))
                    dve.wait_ge(s_out, 1)
                    dve.wait_ge(w_out, 1)
                    step(dve.scalar_tensor_tensor(out=o[:, :], in0=ps[0:64, 4 * BANK:4 * BANK + 64], scalar=st[:, 13:14], in1=o[:, :], op0=ALU.mult, op1=ALU.add))
                    dve.scalar_tensor_tensor(out=o[:, :], in0=ps[0:64, 7 * BANK:7 * BANK + 64], scalar=st[:, 14:15], in1=o[:, :], op0=ALU.mult, op1=ALU.add).then_inc(out_ready, 1)


def prompt_compressed(nc, ps, cst, t, cp, qT, gate, oacc, selm, bufs, K):
    qt, s, pT, m8, pgm, pgb, im, gt, eq, rank, m8b = bufs
    with stage(nc, "q_ready scored masked exped chain p_ready turned copied out_done") as (
            block, q_ready, scored, masked, exped, chain_sem, p_ready, turned, copied, out_done):
        sv = s[:, :].rearrange("p (h c) -> p h c", h=HH)

        @block.tensor
        def _(pe):
            pe.wait_ge(q_ready, 1)
            for h in range(HH):
                r, g = h // 2, h % 2
                b = 4 * g * BANK + r * 64
                m = pe.matmul(ps[:, b:b + 64], qt[64 * g:64 * g + 64, r, :], cp.kc[64 * g:64 * g + 64, :], start=True, stop=True)
            m.then_inc(scored, 1)
            pe.wait_ge(p_ready, 1)
            for h in range(HH):
                m = pe.transpose(ps[0:64, BANK + h * P:BANK + (h + 1) * P], s[:, h * 64:(h + 1) * 64], cst["ident"])
            m.then_inc(turned, 1)
            pe.wait_ge(copied, 1)
            for h in range(HH):
                m = pe.matmul(ps[:, 3 * BANK + h * 64:3 * BANK + (h + 1) * 64], pT[0:63, h, :], cp.vc[0:63, h % 2, :], start=True, stop=True)
            m.then_inc(out_done, 1)

        @block.scalar
        def _(act):
            act.wait_ge(masked, 1)
            act.activation(s[:, :], s[:, :], ACT.Exp, scale=SCALE).then_inc(exped, 1)
            act.wait_ge(turned, 1)
            act.copy(pT[:, :, :], ps[0:64, BANK:3 * BANK].rearrange("p (h t) -> p h t", h=HH)).then_inc(copied, 1)

        @block.vector
        def _(dve):
            step = Chain(dve, chain_sem)
            dve.tensor_copy(qt[:, :, :], qT[:, :, ds(t * P, P)]).then_inc(q_ready, 1)
            dve.wait_ge(scored, 1)
            for g in range(2):
                m = dve.tensor_tensor(sv[:, g:HH:2], ps[:, 4 * g * BANK:4 * g * BANK + 256].rearrange("p (r c) -> p r c", r=R4),
                                      K["cadd"][:, ds(t * 64, 64)].unsqueeze(1).to_broadcast([P, R4, 64]), ALU.add)
            step(m)
            step(dve.tensor_reduce(m8[:, :], sv, AX.X, ALU.max))
            dve.tensor_tensor(sv, sv, bc(m8[:, :], 64), ALU.subtract).then_inc(masked, 1)
            dve.wait_ge(exped, 1)
            step(dve.tensor_tensor(sv, sv, K["cvalid"][:, ds(t * 64, 64)].unsqueeze(1).to_broadcast([P, HH, 64]), ALU.mult))
            step(dve.tensor_reduce(m8[:, :], sv, AX.X, ALU.add))
            step(dve.tensor_scalar(m8[:, :], m8[:, :], 1e-30, None, ALU.max))
            step(dve.reciprocal(m8[:, :], m8[:, :]))
            dve.tensor_tensor(sv, sv, bc(m8[:, :], 64), ALU.mult).then_inc(p_ready, 1)
            dve.wait_ge(p_ready, 1)
            for g in range(2):
                m = dve.tensor_reduce(pgb[:, g, 1:65], s[:, :].rearrange("p (r g c) -> p g c r", r=R4, g=2)[:, g], AX.X, ALU.add)
            step(m)
            step(dve.tensor_reduce(im[:, :, :], pgb[:, :, 1:65].rearrange("p g (s c) -> p g s c", c=4), AX.X, ALU.add))
            step(dve.tensor_tensor(im[:, :, :], im[:, :, :], pgb[:, :, 0:61:4], ALU.add))
            step(dve.tensor_tensor(im[:, :, :], im[:, :, :], K["keep"][:, ds(t * 16, 16)].unsqueeze(1).to_broadcast([P, 2, 16]), ALU.mult))
            step(dve.tensor_tensor(im[:, :, :], im[:, :, :], K["add"][:, ds(t * 16, 16)].unsqueeze(1).to_broadcast([P, 2, 16]), ALU.add))
            step(block_ranks(dve, step, selm[:, ds(t, 1)].rearrange("p a g s -> p (a g) s"), im, P, 2, 16, K["low16"], gt, eq, rank))
            dve.wait_ge(out_done, 1)
            dve.tensor_tensor(oacc[:, ds(t, 1), :].rearrange("p a (h d) -> p (a h) d", h=HH),
                              ps[:, 3 * BANK:4 * BANK].rearrange("p (h d) -> p h d", h=HH),
                              bc(gate[:, ds(t * 24, 8)], HD), ALU.mult)


def prompt_attention(nc, ps, cst, r, qT, ksT, kwT, vs, vw, gate, oacc, selm, bufs, K):
    qr, s, pT, st, gr = bufs
    jobs = [(t, g, br) for t in range(SEQ // P) for g in range(2) for br in range(2)]

    def keys(job):
        t, g, br = job
        first = max(0, t - 2) if br else 0
        return first, t + 1 - first

    with stage(nc, "q_ready scored added maxed exped turned copied out_done summed gates_in chain") as (
            block, q_ready, scored, added, maxed, exped, turned, copied, out_done, summed, gates_in, chain_sem):
        @block.tensor
        def _(pe):
            pe.wait_ge(q_ready, 1)

            def scores(j):
                t, g, br = jobs[j]
                first, n = keys(jobs[j])
                if j >= 2:
                    pe.wait_ge(added, j - 1)
                kT = kwT if br else ksT
                for a in range(0, n * P, BANK):
                    w = min(BANK, n * P - a)
                    o = (j % 2) * 2 * BANK + a
                    m = pe.matmul(ps[:, o:o + w], qr[64 * g:64 * g + 64, t * P:(t + 1) * P],
                                  kT[64 * g:64 * g + 64, first * P + a:first * P + a + w], start=True, stop=True)
                m.then_inc(scored, 1)

            scores(0)
            for j, job in enumerate(jobs):
                t, g, br = job
                first, n = keys(job)
                if j + 1 < len(jobs):
                    scores(j + 1)
                pe.wait_ge(exped, j + 1)
                if j:
                    pe.wait_ge(copied, j)
                for a in range(n):
                    m = pe.transpose(ps[:, 4 * BANK + a * P:4 * BANK + (a + 1) * P], s[:, j % 2, a * P:(a + 1) * P], cst["ident"])
                m.then_inc(turned, 1)
                pe.wait_ge(copied, j + 1)
                if j >= 2:
                    pe.wait_ge(summed, j - 1)
                v = vw if br else vs
                for a in range(n):
                    c = (first + a) * P + g * HD
                    m = pe.matmul(ps[:, (6 + j % 2) * BANK:(6 + j % 2) * BANK + HD], pT[:, a, :], v[:, c:c + HD], start=(a == 0), stop=(a == n - 1))
                m.then_inc(out_done, 1)

        @block.scalar
        def _(act):
            for j, job in enumerate(jobs):
                w = keys(job)[1] * P
                act.wait_ge(maxed, j + 1)
                act.activation(s[:, j % 2, 0:w], s[:, j % 2, 0:w], ACT.Exp, bias=st[:, j % 2, 1:2], scale=SCALE,
                               accum_out=st[:, j % 2, 2:3]).then_inc(exped, 1)
                act.wait_ge(turned, j + 1)
                if j:
                    act.wait_ge(out_done, j)
                act.copy(pT[:, :, :].rearrange("p a t -> p (a t)")[:, 0:w], ps[:, 4 * BANK:4 * BANK + w]).then_inc(copied, 1)

        @block.vector
        def _(dve):
            step = Chain(dve, chain_sem)
            dve.tensor_copy(gr[:, :, :, :], gate[:, 0:24 * 8].rearrange("p (t c r g) -> p t c r g", t=8, c=3, r=R4)[:, :, :, ds(r, 1), :].rearrange("p t c a g -> p t c (a g)")).then_inc(gates_in, 1)
            dve.tensor_copy(qr[:, :], qT[:, ds(r, 1), 0:SEQ].rearrange("p a t -> p (a t)")).then_inc(q_ready, 1)
            dve.wait_ge(gates_in, 1)

            def finish(j):
                t, g, br = jobs[j]
                dve.wait_ge(exped, j + 1)
                step(dve.reciprocal(st[:, j % 2, 3:4], st[:, j % 2, 2:3]))
                step(dve.tensor_tensor(st[:, j % 2, 3:4], st[:, j % 2, 3:4], gr[:, t, 1 + br, g:g + 1], ALU.mult))
                dve.wait_ge(out_done, j + 1)
                o = oacc[:, t, ds(r * P + g * HD, HD)]
                dve.scalar_tensor_tensor(out=o, in0=ps[:, (6 + j % 2) * BANK:(6 + j % 2) * BANK + HD], scalar=st[:, j % 2, 3:4],
                                         in1=o, op0=ALU.mult, op1=ALU.add).then_inc(summed, 1)
                dve.wait_ge(summed, j + 1)

            for j, job in enumerate(jobs):
                t, g, br = job
                first, n = keys(job)
                dve.wait_ge(scored, j + 1)
                if j >= 2:
                    dve.wait_ge(turned, j - 1)
                a = (j % 2) * 2 * BANK
                w = n * P
                sj = s[:, j % 2, :]
                if br:
                    dve.tensor_tensor(sj[:, 0:w], ps[:, a:a + w], K["band"][:, 384 - w:384], ALU.add).then_inc(added, 1)
                else:
                    if n > 1:
                        dve.tensor_tensor(sj[:, 0:w - P].rearrange("p (s d) -> p s d", d=64), ps[:, a:a + w - P].rearrange("p (s d) -> p s d", d=64),
                                          bc(selm[:, t, g, 0:2 * t], 64), ALU.add)
                    step(dve.tensor_tensor(sj[:, w - P:w], ps[:, a + w - P:a + w], K["causal"], ALU.add))
                    dve.tensor_tensor(sj[:, w - P:w].rearrange("p (s d) -> p s d", d=64), sj[:, w - P:w].rearrange("p (s d) -> p s d", d=64),
                                      bc(selm[:, t, g, 2 * t:2 * t + 2], 64), ALU.add).then_inc(added, 1)
                dve.wait_ge(added, j + 1)
                step(dve.tensor_reduce(st[:, j % 2, 0:1], sj[:, 0:w], AX.X, ALU.max))
                dve.tensor_scalar(st[:, j % 2, 1:2], st[:, j % 2, 0:1], -SCALE, None, ALU.mult).then_inc(maxed, 1)
                if j:
                    finish(j - 1)
            finish(len(jobs) - 1)


def nsa_out(nc, ps, cst, oacc, os_d, mixT):
    with Scope(nc) as sc, stage(nc, "loaded turned kept") as (block, loaded, turned, kept):
        os_ = sc.sb("no_os", [NS, 512])

        @block.sync
        def _(sp):
            sp.dma_start(os_[:, :], os_d).then_inc(loaded, 16)

        @block.tensor
        def _(pe):
            pe.wait_ge(loaded, 16)
            for t in range(9):
                m = P if t < 8 else NS
                if t >= 4:
                    pe.wait_ge(kept, t - 3)
                for r in range(R4):
                    src = oacc[:, t, r * P:(r + 1) * P] if t < 8 else os_[:, r * P:(r + 1) * P]
                    mm = pe.transpose(ps[:, (t % 4) * BANK + r * P:(t % 4) * BANK + r * P + m], src, cst["ident"][0:m, 0:m])
                mm.then_inc(turned, 1)

        @block.scalar
        def _(act):
            for t in range(9):
                m = P if t < 8 else NS
                act.wait_ge(turned, t + 1)
                act.copy(mixT[:, 0:4, t * P:t * P + m],
                         ps[:, (t % 4) * BANK:(t % 4 + 1) * BANK].rearrange("p (r t) -> p r t", r=R4)[:, :, 0:m]).then_inc(kept, 1)


def residual_product(nc, ps, l, kt, rhs, w_d, xres):
    with Scope(nc) as sc, stage(nc, "w_in0 w_in1 x_in0 x_in1 products added banks_read stored0 stored1 sp_hold") as (
            block, w0, w1, x0, x1, products, added, banks_read, st0, st1, sp_hold):
        w_in, x_in, stored = (w0, w1), (x0, x1), (st0, st1)
        wt = sc.sb("rs_w", [P, 2, kt, P])
        xr = sc.sb("rs_x", [P, 2, NT])

        @block.sync
        def _(sp):
            def load_w(n, u):
                sp.dma_start(wt[:, u], w_d[l, n]).then_inc(w_in[u], 16)

            def load_x(n, u):
                sp.dma_start(xr[:, u, :], xres[n]).then_inc(x_in[u], 16)

            for u in range(2):
                load_w(u, u)
            for u in range(2):
                load_x(u, u)
            with sp.Fori(0, KD // 2 - 1) as i:
                for u in range(2):
                    sp.wait_ge(added, 2 * i + u + 1)
                    sp.sem_inc(sp_hold, 1)
                    sp.dma_start(xres[2 * i + u], xr[:, u, :]).then_inc(stored[u], 16)
                    load_w(2 * i + u + 2, u)
                    sp.wait_ge(stored[u], 16 * i + 16)
                    sp.sem_inc(sp_hold, 1)
                    load_x(2 * i + u + 2, u)
            for u in range(2):
                sp.wait_ge(added, KD - 1 + u)
                sp.dma_start(xres[KD - 2 + u], xr[:, u, :]).then_inc(stored[u], 16)
            for u in range(2):
                sp.wait_ge(stored[u], 16 * (KD // 2))

        @block.tensor
        def _(pe):
            with pe.Fori(0, KD // 2) as i:
                for u in range(2):
                    pe.wait_ge(w_in[u], 16 * i + 16)
                    pe.wait_ge(banks_read, 2 * i + u + 1)
                    for k in range(kt):
                        for n, (o, w) in enumerate(GROUPS):
                            b = (3 * u + n) * BANK
                            m = pe.matmul(ps[:, b:b + w], wt[:, u, k, :], rhs[:, k, o:o + w], start=(k == 0), stop=(k == kt - 1))
                    m.then_inc(products, 1)

        @block.vector
        def _(dve):
            dve.sem_inc(banks_read, 2)
            with dve.Fori(0, KD // 2) as i:
                for u in range(2):
                    dve.wait_ge(x_in[u], 16 * i + 16)
                    dve.wait_ge(products, 2 * i + u + 1)
                    for n, (o, w) in enumerate(GROUPS):
                        b = (3 * u + n) * BANK
                        m = dve.tensor_tensor(xr[:, u, o:o + w], xr[:, u, o:o + w], ps[:, b:b + w], ALU.add)
                    m.then_inc(added, 1)
                    dve.wait_ge(added, 2 * i + u + 1)
                    dve.sem_inc(banks_read, 1)


def ffn_up(nc, ps, l, xn, hT, wg_d, wu_d, conv_d, cstate_d, conv_out):
    with Scope(nc) as sc, stage(nc, "w_in0 w_in1 gate_done up_done gate_copied conv_done silu_done h_done ext_free gate_free h_free sent0 sent1 chain zeroed sp_hold") as (
            block, w0, w1, gate_done, up_done, gate_copied, conv_done, silu_done, h_done, ext_free, gate_free, h_free, sent0, sent1, chain_sem, zeroed, sp_hold):
        w_in, sent = (w0, w1), (sent0, sent1)
        wt = sc.sb("fu_w", [P, 2, 2, KD, P])
        cw = sc.sb("fu_cw", [P, 2, 4])
        cst_ = sc.sb("fu_cst", [P, 2, NB, 2])
        ge = sc.sb("fu_ge", [P, SEQ + 2])
        gs = sc.sb("fu_gs", [P, NB, NQ + 2])
        c = sc.sb("fu_c", [P, NT])
        co = sc.sb("fu_co", [P, 2, NB + 1, 2])

        @block.sync
        def _(sp):
            def load(f, u):
                sp.dma_start(wt[:, u, 0], wg_d[l, f]).then_inc(w_in[u], 16)
                sp.dma_start(wt[:, u, 1], wu_d[l, f]).then_inc(w_in[u], 16)
                sp.dma_start(cw[:, u, :], conv_d[l, f]).then_inc(w_in[u], 16)
                sp.dma_start(cst_[:, u], cstate_d[l, f]).then_inc(w_in[u], 16)

            def store(f, u):
                sp.dma_start(conv_out[l, f], co[:, u].rearrange("p b e -> p (b e)")).then_inc(sent[u], 16)

            sp.sem_inc(sent[0], 16)
            sp.sem_inc(sent[1], 16)
            load(0, 0)
            load(1, 1)
            with sp.Fori(0, FF // 2 - 1) as i:
                for u in range(2):
                    sp.wait_ge(conv_done, 2 * i + u + 1)
                    sp.sem_inc(sp_hold, 1)
                    store(2 * i + u, u)
                    sp.wait_ge(up_done, 2 * i + u + 1)
                    sp.sem_inc(sp_hold, 1)
                    load(2 * i + u + 2, u)
            for u in range(2):
                sp.wait_ge(conv_done, FF - 1 + u)
                store(FF - 2 + u, u)
            for u in range(2):
                sp.wait_ge(sent[u], 16 * (FF // 2 + 1))

        @block.tensor
        def _(pe):
            with pe.Fori(0, FF // 2) as i:
                for u in range(2):
                    pe.wait_ge(w_in[u], 64 * i + 64)
                    for half, (free, done) in enumerate(((gate_free, gate_done), (h_free, up_done))):
                        pe.wait_ge(free, 2 * i + u + 1)
                        for k in range(KD):
                            for n, (o, w) in enumerate(GROUPS):
                                b = (3 * half + n) * BANK
                                m = pe.matmul(ps[:, b:b + w], wt[:, u, half, k, :], xn[:, k, o:o + w], start=(k == 0), stop=(k == KD - 1))
                        m.then_inc(done, 1)

        @block.scalar
        def _(act):
            act.sem_inc(gate_free, 1)
            with act.Fori(0, FF // 2) as i:
                for u in range(2):
                    act.wait_ge(gate_done, 2 * i + u + 1)
                    act.wait_ge(ext_free, 2 * i + u + 1)
                    act.copy(ge[:, 2:386], ps[:, 0:384])
                    act.copy(ge[:, 386:770], ps[:, BANK:BANK + 384])
                    act.copy(ge[:, 770:1026], ps[:, 2 * BANK:2 * BANK + 256])
                    act.copy(gs[:, :, 2:NQ + 2], ps[:, 2 * BANK + 256:2 * BANK + 320].rearrange("p (b q) -> p b q", b=NB)).then_inc(gate_copied, 1)
                    act.wait_ge(gate_copied, 2 * i + u + 1)
                    act.sem_inc(gate_free, 1)
                    act.wait_ge(conv_done, 2 * i + u + 1)
                    act.activation(c[:, :], c[:, :], ACT.Silu).then_inc(silu_done, 1)

        @block.vector
        def _(dve):
            dve.memset(ge[:, 0:2], 0.0).then_inc(zeroed, 1)
            dve.wait_ge(zeroed, 1)
            dve.sem_inc(ext_free, 1)
            dve.sem_inc(h_free, 1)
            csam = c[:, SEQ:NT].rearrange("p (b q) -> p b q", b=NB)
            with dve.Fori(0, FF // 2) as i:
                for u in range(2):
                    dve.wait_ge(w_in[u], 64 * i + 64)
                    dve.wait_ge(gate_copied, 2 * i + u + 1)
                    dve.wait_ge(sent[u], 16 * i + 16)
                    dve.tensor_copy(co[:, u, 0, :], ge[:, SEQ:SEQ + 2])
                    dve.tensor_copy(co[:, u, 1:NB + 1, :], gs[:, :, NQ:NQ + 2])
                    dve.tensor_copy(gs[:, :, 0:2], cst_[:, u]).then_inc(chain_sem, 1)
                    dve.wait_ge(chain_sem, 3 * (2 * i + u) + 1)
                    dve.tensor_scalar(c[:, 0:SEQ], ge[:, 0:SEQ], cw[:, u, 0:1], cw[:, u, 3:4], ALU.mult, ALU.add)
                    dve.tensor_scalar(csam, gs[:, :, 0:NQ], cw[:, u, 0:1], cw[:, u, 3:4], ALU.mult, ALU.add).then_inc(chain_sem, 1)
                    dve.wait_ge(chain_sem, 3 * (2 * i + u) + 2)
                    dve.scalar_tensor_tensor(out=c[:, 0:SEQ], in0=ge[:, 1:SEQ + 1], scalar=cw[:, u, 1:2], in1=c[:, 0:SEQ], op0=ALU.mult, op1=ALU.add)
                    dve.scalar_tensor_tensor(out=csam, in0=gs[:, :, 1:NQ + 1], scalar=cw[:, u, 1:2], in1=csam, op0=ALU.mult, op1=ALU.add).then_inc(chain_sem, 1)
                    dve.wait_ge(chain_sem, 3 * (2 * i + u) + 3)
                    dve.scalar_tensor_tensor(out=c[:, 0:SEQ], in0=ge[:, 2:SEQ + 2], scalar=cw[:, u, 2:3], in1=c[:, 0:SEQ], op0=ALU.mult, op1=ALU.add)
                    dve.scalar_tensor_tensor(out=csam, in0=gs[:, :, 2:NQ + 2], scalar=cw[:, u, 2:3], in1=csam, op0=ALU.mult, op1=ALU.add).then_inc(conv_done, 1)
                    dve.wait_ge(conv_done, 2 * i + u + 1)
                    dve.sem_inc(ext_free, 1)
                    dve.wait_ge(silu_done, 2 * i + u + 1)
                    dve.wait_ge(up_done, 2 * i + u + 1)
                    for n, (o, w) in enumerate(GROUPS):
                        m = dve.tensor_tensor(hT[:, ds(2 * i + u, 1), o:o + w].rearrange("p a t -> p (a t)"), c[:, o:o + w], ps[:, (3 + n) * BANK:(3 + n) * BANK + w], ALU.mult)
                    m.then_inc(h_done, 1)
                    dve.wait_ge(h_done, 2 * i + u + 1)
                    dve.sem_inc(h_free, 1)


def trunk(nc, A, O, X, upto=99):
    with ExitStack() as top:
        pst = top.enter_context(nc.psum_tensor("ps", [P, 8 * BANK], F32))
        ps = pst[:, :]
        cbuf = top.enter_context(nc.sbuf_tensor("cbuf", [P, 3 * P], F32))
        ptab = top.enter_context(nc.sbuf_tensor("ptab", [1, NB * PAGES], I32))
        cst = {n: cbuf[:, i * P:(i + 1) * P] for i, n in enumerate(("ident", "ones", "blk"))}
        xres = X["xres"]
        with stage(nc, "loaded") as (block, loaded):
            @block.sync
            def _(sp):
                sp.dma_start(cbuf[:, :], A["const"][:, 0:3 * P]).then_inc(loaded, 16)
                sp.dma_start(ptab[:, :], A["page_table"]).then_inc(loaded, 16)
                for k in range(KD):
                    sp.dma_start(xres[k], A["xT"][k]).then_inc(loaded, 16)
                sp.wait_ge(loaded, 16 * (KD + 2))

        with nc.Fori(0, L_RUN) as l:
            with Scope(nc) as mixed:
                qT = mixed.sb("qT", [P, R4, NTP])
                ksT, kwT, vs, vw = (mixed.sb(n, [P, NTP]) for n in ("ksT", "kwT", "vs", "vw"))
                gate = mixed.sb("gate", [P, TT * 24])
                mixT = mixed.sb("mixT", [P, KD, NT])
                with Scope(nc) as sc:
                    xn = sc.sb("xn", [P, KD, NTP])
                    with stage(nc, "zeroed") as (block, zeroed):
                        @block.vector
                        def _(dve):
                            dve.memset(xn[:, :, NT:NTP], 0.0).then_inc(zeroed, 1)
                    load_norm(nc, ps, cst, xres, A["norm_mix"][l], xn)
                    if upto < 2:
                        return
                    with Scope(nc) as sn:
                        w = sn.sb("wn", [P, KD, WN])
                        tmp = (sn.sb("np_xt", [P, KD, P]), sn.sb("np_kv", [P, 768]), sn.sb("np_q", [P, 512]), sn.sb("np_q2", [P, 512]),
                               sn.sb("np_tb", [P, 4, 256]), sn.sb("np_cs", [P, 64]))
                        with stage(nc, "loaded") as (block, loaded):
                            @block.sync
                            def _(sp):
                                for k in range(KD):
                                    sp.dma_start(w[:, k, :], A["w_nsa"][l, k]).then_inc(loaded, 16)
                                sp.wait_ge(loaded, 16 * KD)
                        with nc.Fori(0, TT) as t:
                            nsa_projection(nc, ps, cst, l, t, xn, w, None, qT, ksT, kwT, vs, vw, gate, O["kvrows"], X["winr"], A["rope"], tmp)
                    if upto < 3:
                        return
                    rwkv_projection(nc, ps, cst, l, xn, A["w_rw"], A["shift_in"], A["mu"][l], X["xmT"], O["shift"])
                if upto < 4:
                    return
                with Scope(nc) as sc:
                    wend = sc.sb("wend", [P, 4, NCH + NB])
                    rwkv_features(nc, ps, cst, l, X["xmT"], A["lora"][l], A["rvec"][l], X["arbk"], X["rk"], wend, A["const"])
                    if upto < 5:
                        return
                    rwkv_scan(nc, ps, cst, l, wend, A["const"], X["arbk"], X["xmT"], X["yr"], X["vr"], A["wkv_in"], O["wkv"])
                    if upto < 6:
                        return
                    rwkv_output(nc, ps, cst, l, mixT, X["xmT"], X["rk"], X["yr"], X["vr"], A["g_b"], A["gn"], A["rk8"])
                if upto < 7:
                    return
                with Scope(nc) as sc:
                    cp = Compressor(nc, sc)
                    with stage(nc, "stored") as (block, stored):
                        @block.sync
                        def _(sp):
                            sp.dma_start(O["win_p"][l], X["winr"][SEQ - 256:SEQ, :]).then_inc(stored, 16)
                            sp.dma_start(O["win_s"][l, :, 0:256 - NQ, :], A["state_win"][l, :, NQ:256, :]).then_inc(stored, 16)
                            sp.dma_start(O["win_s"][l, :, 256 - NQ:256, :], X["winr"][SEQ:NT, :].rearrange("(b q) n -> b q n", b=NB)).then_inc(stored, 16)
                            sp.dma_start(X["gs"], gate[0:NS, 24 * (TT - 1):24 * TT]).then_inc(stored, 16)
                            sp.wait_ge(stored, 64)
                    cp.weights(nc, ps, l, A["w1"], A["w2"], A["pe"])
                    sample_attention(nc, ps, cst, l, cp, qT, A["cache"], ptab, O["kvrows"], X["winr"], X["gs"], X["os"], A["state_win"], A["const"])
                    if upto < 8:
                        return

                    def prompt_rows(sp, sem):
                        for n in range(4):
                            sp.dma_start(cp.kvp[:, n, :], O["kvrows"][l, n * 256:(n + 1) * 256, :].rearrange("(p e) n -> p (e n)", e=2)).then_inc(sem, 16)
                        return 64

                    cp.run(nc, ps, cst, prompt_rows)
                    oacc = sc.sb("oacc", [P, 8, 512])
                    selm = sc.sb("selm", [P, 8, 2, 16])
                    names = ("cvalid", "cadd", "keep", "add", "causal", "band", "low16")
                    off, w = {}, 0
                    for n in names:
                        off[n] = w
                        w += CO[n][1]
                    km = sc.sb("km", [P, w])
                    K = {n: km[:, off[n]:off[n] + CO[n][1]] for n in names}
                    pgb = sc.sb("pc_pgb", [P, 2, 66])
                    with stage(nc, "loaded zeroed") as (block, loaded, zeroed):
                        @block.sync
                        def _(sp):
                            for n in names:
                                a, ww = CO[n]
                                sp.dma_start(km[:, off[n]:off[n] + ww], A["const"][:, a:a + ww]).then_inc(loaded, 16)
                            sp.wait_ge(loaded, 16 * len(names))

                        @block.vector
                        def _(dve):
                            dve.memset(pgb[:, :, :], 0.0).then_inc(zeroed, 1)
                    with Scope(nc) as s2:
                        bufs = (s2.sb("pc_qt", [P, R4, P]), s2.sb("pc_s", [P, 512]), s2.sb("pc_pT", [64, HH, P]), s2.sb("pc_m8", [P, 8]), None, pgb,
                                s2.sb("pc_im", [P, 2, 16]), s2.sb("pc_gt", [P, 2, 16, 16]), s2.sb("pc_eq", [P, 2, 16, 16]), s2.sb("pc_rank", [P, 2, 16]), None)
                        with nc.Fori(0, SEQ // P) as t:
                            prompt_compressed(nc, ps, cst, t, cp, qT, gate, oacc, selm, bufs, K)
                    if upto < 9:
                        return
                    with Scope(nc) as s2:
                        bufs = (s2.sb("pa_qr", [P, SEQ]), s2.sb("pa_s", [P, 2, SEQ]), s2.sb("pa_pT", [P, 8, P]), s2.sb("pa_st", [P, 2, 4]), s2.sb("pa_gr", [P, 8, 3, 2]))
                        with nc.Fori(0, R4) as r:
                            prompt_attention(nc, ps, cst, r, qT, ksT, kwT, vs, vw, gate, oacc, selm, bufs, K)
                    nsa_out(nc, ps, cst, oacc, X["os"], mixT)
                if upto < 10:
                    return
                residual_product(nc, ps, l, KD, mixT, A["w_out"], xres)
            if upto < 11:
                return
            with Scope(nc) as sc:
                hT = sc.sb("hT", [P, FF, NT])
                with Scope(nc) as s2:
                    xn2 = s2.sb("xn2", [P, KD, NT])
                    load_norm(nc, ps, cst, xres, A["norm_ffn"][l], xn2)
                    ffn_up(nc, ps, l, xn2, hT, A["w_gate"], A["w_up"], A["conv_w"], A["conv_in"], O["conv"])
                if upto < 12:
                    return
                residual_product(nc, ps, l, FF, hT, A["w_down"], xres)
        with Scope(nc) as sc:
            xf = sc.sb("xf", [P, KD, NT])
            load_norm(nc, ps, cst, xres, A["norm_final"], xf, store=O["yT"])


QPERM = np.arange(512).reshape(2, 4, 64).transpose(1, 0, 2).reshape(-1)
GPERM = np.arange(24).reshape(2, 4, 3).transpose(2, 1, 0).reshape(-1)
RPERM = np.concatenate([np.arange(0, 512), np.arange(576, 1088), np.arange(1088, 1600),
                        np.arange(512, 576), np.arange(1600, 1664), np.arange(1664, 1792)])

SPERM = np.arange(512).reshape(4, 2, 64).transpose(1, 0, 2).reshape(-1)


def tiles(v, n):
    return np.ascontiguousarray(v.reshape(v.shape[0], n, P).transpose(0, 2, 1))


def layout(i):
    c = np.ascontiguousarray
    a = {"const": constants(), "rope": rope_tables()}
    x = np.concatenate([i["x_prompt"].reshape(SEQ, D), i["x_sample"].reshape(NS, D)])
    a["xT"] = c(x.T.reshape(KD, P, NT))
    a["page_table"] = c(i["page_table"].reshape(1, NB * PAGES))
    a["cache"] = c(i["cache_kv"].reshape(L, NPHYS, 64, 1024))
    a["state_win"] = c(i["state_win"].reshape(L, NB, 256, 256))
    w = i["w_in"]
    nsa = np.concatenate([QPERM, np.arange(512, 1280), 1280 + GPERM])
    a["w_nsa"] = c(w[:, :, nsa].reshape(L, KD, P, WN))
    a["w_rw"] = c(w[:, :, 1304 + RPERM].reshape(L, KD, P, FR, P).transpose(0, 3, 2, 1, 4))
    a["mu"] = tiles(i["rw_mu"][:, RPERM], FR)
    a["shift_in"] = c(i["state_shift"][:, :, RPERM].reshape(L, NB, FR, P).transpose(0, 2, 3, 1))
    a["lora"] = c(np.concatenate([i["rw_w_b"], i["rw_a_b"]], 1))
    a["rvec"] = c(np.stack([tiles(i[n], 4) for n in ("rw_w0", "rw_a0", "rw_k_k", "rw_k_a")], 2))
    a["g_b"] = c(i["rw_g_b"][:, :, SPERM])
    a["gn"] = c(np.stack([i["rw_gn_w"], i["rw_gn_b"]], 1)[:, :, SPERM])
    rk8 = np.zeros((L, P, 4, 8), np.float32)
    for h in range(HH):
        rk8[:, 64 * (h % 2):64 * (h % 2) + 64, h // 2, h % 2 * 4 + h // 2] = i["rw_r_k"][:, h]
    a["rk8"] = rk8
    a["wkv_in"] = c(i["state_wkv"].reshape(L, NB, 4, 2, HD, HD).transpose(0, 3, 5, 2, 1, 4).reshape(L, P, 4, NB, HD))
    a["w1"] = c(i["cmp_w1"].reshape(L, 2, 16, P, 256).transpose(0, 1, 3, 2, 4))
    a["w2"] = c(i["cmp_w2"].reshape(L, 2, 2, P, HD).transpose(0, 1, 3, 2, 4))
    a["pe"] = c(i["cmp_pe"].reshape(L, 2, 16, P).transpose(0, 1, 3, 2))
    wo = i["w_out"][:, np.concatenate([QPERM, 512 + SPERM]), :]
    a["w_out"] = c(wo.reshape(L, KD, P, KD, P).transpose(0, 3, 2, 1, 4))
    for n, k in (("w_gate", "ffn_w_gate"), ("w_up", "ffn_w_up")):
        z = np.zeros((L, D, FF * P), np.float32)
        z[:, :, :2752] = i[k]
        a[n] = c(z.reshape(L, KD, P, FF, P).transpose(0, 3, 2, 1, 4))
    z = np.zeros((L, FF * P, D), np.float32)
    z[:, :2752] = i["ffn_w_down"]
    a["w_down"] = c(z.reshape(L, FF, P, KD, P).transpose(0, 3, 2, 1, 4))
    z = np.zeros((L, FF * P, 4), np.float32)
    z[:, :2752, 0:3] = i["ffn_conv_w"].transpose(0, 2, 1)
    z[:, :2752, 3] = i["ffn_conv_b"]
    a["conv_w"] = z.reshape(L, FF, P, 4)
    z = np.zeros((L, FF * P, NB, 2), np.float32)
    z[:, :2752] = i["state_conv"].transpose(0, 3, 1, 2)
    a["conv_in"] = z.reshape(L, FF, P, NB, 2)
    a["norm_mix"] = tiles(i["norm_mix"], KD)
    a["norm_ffn"] = tiles(i["norm_ffn"], KD)
    a["norm_final"] = tiles(i["norm_final"][None], KD)[0]
    return a


OUTS = {"yT": (KD, P, NT), "kvrows": (L, NTP, 512), "win_p": (L, 256, 256), "win_s": (L, NB, 256, 256),
        "wkv": (L, P, 4, NB + 1, HD), "shift": (L, FR, P, NB + 1), "conv": (L, FF, P, 2 * (NB + 1))}
SCRATCH = {"xres": (KD, P, NT), "winr": (NTP, 256), "xmT": (FR, P, NT), "arbk": (NCH + 1, P, 4, 4 * CH),
           "rk": (4, P, NT), "yr": (NT, 512), "vr": (NT, 512), "gs": (NS, 24), "os": (NS, 512)}


def build(nc, arrays, upto=99):
    A = {n: nc.dram_tensor(f"in_{n}", a.shape, mybir.dt.from_np(a.dtype), kind="ExternalInput").ap() for n, a in arrays.items()}
    O = {n: nc.dram_tensor(f"out_{n}", s, F32, kind="ExternalOutput").ap() for n, s in OUTS.items()}
    X = {n: nc.dram_tensor(f"scr_{n}", s, F32, kind="Internal").ap() for n, s in SCRATCH.items()}
    trunk(nc, A, O, X, upto)


def unlay(o):
    y = o["yT"].reshape(D, NT).T
    kv = o["kvrows"]
    rp = np.argsort(RPERM)
    wkv = o["wkv"].reshape(L, 2, HD, 4, NB + 1, HD).transpose(0, 4, 3, 1, 5, 2).reshape(L, NB + 1, HH, HD, HD)
    sh = o["shift"].reshape(L, FR * P, NB + 1)[:, rp].transpose(0, 2, 1)
    cv = o["conv"].reshape(L, FF * P, NB + 1, 2)[:, :2752].transpose(0, 2, 3, 1)
    c = np.ascontiguousarray
    return (c(y[:SEQ].reshape(1, SEQ, D)), c(y[SEQ:].reshape(NB, NQ, D)),
            c(kv[:, :SEQ].reshape(L, 1, SEQ, 4, 2, HD)), c(kv[:, SEQ:NT].reshape(L, NB, NQ, 4, 2, HD)),
            o["win_p"].reshape(L, 1, 256, 2, 2, HD), o["win_s"].reshape(L, NB, 256, 2, 2, HD),
            c(wkv[:, 0:1]), c(wkv[:, 1:]), c(sh[:, 0:1]), c(sh[:, 1:]), c(cv[:, 0:1]), c(cv[:, 1:]))


def kernel(**inputs):
    import concourse.bacc as bacc
    from concourse.bass_utils import run_bass_kernel_spmd as run

    arrays = layout({k: np.asarray(v) for k, v in inputs.items()})
    nc = bacc.Bacc("TRN2", target_bir_lowering=False, num_devices=1)
    build(nc, arrays)
    r = run(nc, [{f"in_{n}": a for n, a in arrays.items()}], core_ids=[0])
    return unlay({n: r.results[0][f"out_{n}"] for n in OUTS})
```

```python
from contextlib import ExitStack, contextmanager
import itertools
import math

import numpy as np
import concourse.bass as bass
from concourse import mybir

F32 = mybir.dt.float32
F32R = mybir.dt.float32r
I32 = mybir.dt.int32
ALU = mybir.AluOpType
ACT = mybir.ActivationFunctionType
AX = mybir.AxisListType

P = 128
D = 1024
KD = D // P
L = 2
L_RUN = L
SEQ = 1024
NB = 8
NQ = 8
NS = NB * NQ
NT = SEQ + NS
NTP = SEQ + P
TT = NTP // P
HD = 64
HH = 8
R4 = 4
WN = 1304
FR = 14
FF = 22
PAGES = 8
NPHYS = 80
CH = 64
NCH = SEQ // CH
SCALE = HD ** -0.5
NEG = -1e30
GROUPS = [(0, 384), (384, 384), (768, 320)]
BANK = 512
E05 = math.exp(-0.5)

_W = [("ident", P), ("ones", P), ("blk", P), ("gmask", P), ("gmask_s", P), ("lev", 6 * CH),
      ("restart", NT), ("cvalid", 8 * 64), ("cadd", 8 * 64), ("keep", 8 * 16), ("add", 8 * 16),
      ("causal", P), ("band", 384), ("low16", 256), ("low17", 289), ("swin", 264), ("snew", 8),
      ("skeep", 17), ("sadd", 17), ("hsel", 8), ("same", 64), ("seqt", NB * CH), ("seqp", NB)]
CO, _o = {}, 0
for _n, _w in _W:
    CO[_n] = (_o, _w)
    _o += _w
CW = _o


def constants():
    c = np.zeros((P, CW), np.float32)

    def put(name, a):
        o, w = CO[name]
        a = np.asarray(a, np.float32).reshape(a.shape[0], -1)
        c[:a.shape[0], o:o + w] = a

    p = np.arange(P)
    put("ident", np.eye(P))
    put("ones", np.ones((P, P)))
    put("blk", p[:, None] // 64 == p[None, :] // 64)
    s, t = p % 64, p % 64
    strict = np.concatenate([(s[:, None] < t[None, :64]), (s[:, None] <= t[None, :64])], 1)
    same = s[:, None] // NQ == (p % 64)[None, :] // NQ
    put("gmask", strict)
    put("gmask_s", strict & same)
    a = np.arange(CH)
    lev = []
    for n in range(6):
        w = 1 << n
        lev.append((a[None, :] // (2 * w) == a[:, None] // (2 * w)) & (a[None, :] // w % 2 == 1) & (a[:, None] // w % 2 == 0))
    put("lev", np.tile(np.stack(lev, 1), (2, 1, 1)))
    r = np.ones(NT)
    r[0:SEQ:CH] = 0
    r[SEQ::NQ] = 0
    put("restart", np.tile(r, (P, 1)))
    q = np.arange(8)[None, :, None] * P + p[:, None, None]
    cc = np.arange(64)[None, None, :]
    valid = (cc < 63) & (16 * cc + 31 <= q)
    put("cvalid", valid)
    put("cadd", np.where(valid, 0, NEG))
    b = np.arange(16)[None, None, :]
    cur = q // 64
    forced = (b == 0) | ((b <= cur) & (b > cur - 2))
    future = b * 64 > q
    put("keep", ~(forced | future))
    put("add", np.where(forced, 1e9, np.where(future, -1e9, 0)))
    put("causal", np.where(p[None, :] > p[:, None], NEG, 0))
    k = np.arange(384)[None, :] - 256
    put("band", np.where((k <= p[:, None]) & (k > p[:, None] - 256), 0, NEG))
    for n in (16, 17):
        i = np.arange(n)
        put(f"low{n}", np.tile((i[None, None, :] < i[None, :, None]), (P, 1, 1)))
    q = (np.arange(64) % NQ)[:, None]
    k = np.arange(264)[None, :]
    put("swin", np.where((k > q) & (k <= 256 + q), 0, NEG))
    put("snew", np.where(np.arange(8)[None, :] <= q, 0, NEG))
    b = np.arange(17)[None, :] + 0 * q
    f = (b == 0) | (b >= 15)
    put("skeep", ~f)
    put("sadd", np.where(f, 1e9, 0))
    i = np.arange(64)
    put("hsel", (2 * (i // 8 % 4) + i // 32)[:, None] == np.arange(8)[None, :])
    put("same", (i[:, None] // 32 == i[None, :] // 32) & (i[:, None] % 8 == i[None, :] % 8))
    put("seqt", np.tile((a[None, None, :] // NQ == np.arange(NB)[None, :, None]), (P, 1, 1)))
    put("seqp", (p % 64)[:, None] // NQ == np.arange(NB)[None, :])
    return c


def rope_tables():
    pos = np.arange(NTP)
    pos[SEQ:] = SEQ + (pos[SEQ:] - SEQ) % NQ
    inv = (np.float32(10000.0) ** (-np.arange(32, dtype=np.float32) / 32)).astype(np.float32)
    ang = pos.astype(np.float32)[:, None] * inv[None, :]
    return np.concatenate([np.cos(ang), np.sin(ang)], 1).astype(np.float32).reshape(TT, P, 64)


class Chain:

    def __init__(self, eng, sem):
        self.eng, self.sem, self.n = eng, sem, 0

    def __call__(self, ins):
        ins.then_inc(self.sem, 1)
        self.n += 1
        self.eng.wait_ge(self.sem, self.n)


def clear(sp, sems):
    nums = sorted(s.num for s in sems)
    first = nums[0]
    for n, after in zip(nums, nums[1:] + [None]):
        if after != n + 1:
            sp.sem_clear(range(first, n + 1))
            first = after


@contextmanager
def stage(nc, names):
    with ExitStack() as es:
        sems = [es.enter_context(nc.semaphore(n)) for n in names.split()]
        with nc.Block() as block:
            yield (block, *sems)
        clear(nc.sync, sems)
        nc.all_engine_barrier()


_NUMBER = itertools.count()


class Scope(ExitStack):

    def __init__(self, nc):
        super().__init__()
        self.nc = nc

    def sb(self, name, shape, dt=F32):
        return self.enter_context(self.nc.sbuf_tensor(f"{name}_{next(_NUMBER)}", shape, dt))


def ds(start, size):
    return bass.ds(start, size)


def bc(ap, n):
    return ap.unsqueeze(len(ap.shape)).to_broadcast([*ap.shape, n])


def mid(ap, n):
    return ap.unsqueeze(1).to_broadcast([ap.shape[0], n, ap.shape[1]])


def f32(ap):
    return ap.bitcast(F32)



CHUNK = 2


def split_weights(pool, w, hi, lo, kt, hi_ready, ready, count):
    for c in range(kt // CHUNK):
        k = slice(c * CHUNK, (c + 1) * CHUNK)
        pool.tensor_copy(hi[:, k, :], w[:, k, :]).then_inc(hi_ready, 1)
        pool.wait_ge(hi_ready, count(c) + 1)
        pool.tensor_tensor(lo[:, k, :], w[:, k, :], f32(hi[:, k, :]), ALU.subtract).then_inc(ready, 1)


def product3(pe, ps, bank, wh, wl, xh, xl, kt, ready, count):
    for k in range(kt):
        if k % CHUNK == 0:
            pe.wait_ge(ready, count(k // CHUNK) + 1)
        for j, (w, x) in enumerate(((wh, xh), (wh, xl), (wl, xh))):
            for n, (o, c) in enumerate(GROUPS):
                b = (bank + n) * BANK
                m = pe.matmul(ps[:, b:b + c], w[:, k, :], x[:, k, o:o + c], start=(k == 0 and j == 0), stop=(k == kt - 1 and j == 2))
    return m


def load_norm(nc, ps, cst, xres, gain, xn, store=None, hi=None, lo=None):
    with Scope(nc) as sc, stage(nc, "x_loaded squared summed rooted root_chain scaled normed stored hi_ready split") as (
            block, x_loaded, squared, summed, rooted, chain_sem, scaled, normed, stored, hi_ready, split):
        sq = sc.sb("n_sq", [P, 2, NT])
        rs = sc.sb("n_rs", [P, NT])
        g = sc.sb("n_g", [P, KD])

        @block.sync
        def _(sp):
            sp.dma_start(g[:, :], gain).then_inc(x_loaded, 16)
            for k in range(KD):
                sp.dma_start(xn[:, k, 0:NT], xres[k]).then_inc(x_loaded, 16)
            if store is not None:
                sp.wait_ge(normed, KD)
                for k in range(KD):
                    sp.dma_start(store[k], xn[:, k, 0:NT]).then_inc(stored, 16)
                sp.wait_ge(stored, 16 * KD)

        @block.scalar
        def _(act):
            act.wait_ge(x_loaded, 16 * (KD + 1))
            for k in range(KD):
                if k >= 2:
                    act.wait_ge(summed, k - 1)
                act.activation(sq[:, k % 2, :], xn[:, k, 0:NT], ACT.Square).then_inc(squared, 1)
            act.wait_ge(scaled, 1)
            act.activation(rs[:, :], rs[:, :], ACT.Sqrt).then_inc(rooted, 1)
            if hi is not None:
                for k in range(KD):
                    act.wait_ge(normed, k + 1)
                    act.copy(hi[:, k, 0:NT], xn[:, k, 0:NT]).then_inc(hi_ready, 1)

        @block.tensor
        def _(pe):
            for k in range(KD):
                pe.wait_ge(squared, k + 1)
                for n, (o, w) in enumerate(GROUPS):
                    m = pe.matmul(ps[:, n * BANK:n * BANK + w], cst["ones"], sq[:, k % 2, o:o + w],
                                  start=(k == 0), stop=(k == KD - 1))
                m.then_inc(summed, 1)

        @block.vector
        def _(dve):
            dve.wait_ge(summed, KD)
            for n, (o, w) in enumerate(GROUPS):
                m = dve.tensor_scalar(rs[:, o:o + w], ps[:, n * BANK:n * BANK + w], 1.0 / D, 1e-6, ALU.mult, ALU.add)
            m.then_inc(scaled, 1)
            dve.wait_ge(rooted, 1)
            dve.reciprocal(rs[:, :], rs[:, :]).then_inc(chain_sem, 1)
            dve.wait_ge(chain_sem, 1)
            for k in range(KD + 1):
                if k < KD:
                    dve.scalar_tensor_tensor(out=xn[:, k, 0:NT], in0=xn[:, k, 0:NT], scalar=g[:, k:k + 1],
                                             in1=rs[:, :], op0=ALU.mult, op1=ALU.mult).then_inc(normed, 1)
                if hi is not None and k > 0:
                    dve.wait_ge(hi_ready, k)
                    dve.tensor_tensor(lo[:, k - 1, 0:NT], xn[:, k - 1, 0:NT], f32(hi[:, k - 1, 0:NT]), ALU.subtract).then_inc(split, 1)


def nsa_projection(nc, ps, cst, l, t, xh, xl, w, K, qT, ksT, kwT, vs, vw, gate, kvrows, winr, rope_d, tmp):
    xt, kv, q, q2, tb, cs = tmp
    with stage(nc, "cs_loaded x_copied proj copied chain rotated turned kept stored") as (
            block, cs_loaded, x_copied, proj, copied, chain_sem, rotated, turned, kept, stored):

        @block.sync
        def _(sp):
            sp.dma_start(cs[:, :], rope_d[t]).then_inc(cs_loaded, 16)
            sp.wait_ge(rotated, 2)
            sp.dma_start(kvrows[l, ds(t * P, P), :], kv[:, 0:512]).then_inc(stored, 16)
            sp.dma_start(winr[ds(t * P, P), :], kv[:, 512:768]).then_inc(stored, 16)
            sp.wait_ge(stored, 32)

        @block.tensor
        def _(pe):
            pe.wait_ge(x_copied, 1)
            for n, (o, c) in enumerate([(512, 512), (1024, 280), (0, 512)]):
                for k in range(KD):
                    m = pe.matmul(ps[:, n * BANK:n * BANK + c], xt[:, k, :], w[:, k, o:o + c],
                                  start=(k == 0), stop=(k == KD - 1))
                m.then_inc(proj, 1)
            pe.wait_ge(rotated, 2)
            pe.transpose(ps[:, 4 * BANK:4 * BANK + P], kv[:, 256:384], cst["ident"])
            pe.transpose(ps[:, 4 * BANK + P:4 * BANK + 2 * P], kv[:, 512:640], cst["ident"]).then_inc(turned, 1)
            pe.wait_ge(rotated, 4)
            for r in range(R4):
                m = pe.transpose(ps[:, 3 * BANK + r * P:3 * BANK + (r + 1) * P], q2[:, r * P:(r + 1) * P], cst["ident"])
            m.then_inc(turned, 1)

        @block.scalar
        def _(act):
            act.wait_ge(proj, 1)
            act.copy(kv[:, 0:512], ps[:, 0:512]).then_inc(copied, 1)
            act.wait_ge(proj, 2)
            act.activation(gate[:, ds(t * 24, 24)], ps[:, BANK + 256:BANK + 280], ACT.Sigmoid)
            act.copy(kv[:, 512:768], ps[:, BANK:BANK + 256]).then_inc(copied, 1)
            act.wait_ge(proj, 3)
            act.copy(q[:, :], ps[:, 2 * BANK:3 * BANK]).then_inc(copied, 1)
            act.wait_ge(turned, 1)
            act.copy(ksT[:, ds(t * P, P)], ps[:, 4 * BANK:4 * BANK + P])
            act.copy(kwT[:, ds(t * P, P)], ps[:, 4 * BANK + P:4 * BANK + 2 * P])
            act.wait_ge(turned, 2)
            act.copy(qT[:, :, ds(t * P, P)], ps[:, 3 * BANK:4 * BANK].rearrange("p (r t) -> p r t", r=R4)).then_inc(kept, 1)

        @block.vector
        def _(dve):
            step = Chain(dve, chain_sem)
            dve.tensor_tensor(xt[:, :, :], f32(xh[:, :, ds(t * P, P)]), f32(xl[:, :, ds(t * P, P)]), ALU.add).then_inc(x_copied, 1)
            dve.wait_ge(cs_loaded, 16)

            def rotate(x1, x2, o1, o2, shape, tmps):
                dims = list(shape)
                cos, sin = cs[:, 0:32], cs[:, 32:64]
                for d in dims[:-1]:
                    cos, sin = cos.unsqueeze(1), sin.unsqueeze(1)
                cos, sin = cos.to_broadcast([P, *dims]), sin.to_broadcast([P, *dims])
                ta, tc, td, te = tmps
                dve.tensor_tensor(ta, x1, cos, ALU.mult)
                dve.tensor_tensor(tc, x2, sin, ALU.mult)
                dve.tensor_tensor(td, x2, cos, ALU.mult)
                step(dve.tensor_tensor(te, x1, sin, ALU.mult))
                dve.tensor_tensor(o1, ta, tc, ALU.subtract).then_inc(rotated, 1)
                dve.tensor_tensor(o2, td, te, ALU.add).then_inc(rotated, 1)

            dve.wait_ge(copied, 2)
            kh = kv[:, :].rearrange("p (a k g e d) -> p a k g e d", a=3, k=2, g=2, e=2)[:, :, 0]
            tk = [tb[:, n, 0:192].rearrange("p (a g d) -> p a g d", a=3, g=2) for n in range(4)]
            rotate(kh[:, :, :, 0, :], kh[:, :, :, 1, :], kh[:, :, :, 0, :], kh[:, :, :, 1, :], (3, 2, 32), tk)
            dve.tensor_copy(vs[:, ds(t * P, P)], kv[:, 384:512])
            dve.tensor_copy(vw[:, ds(t * P, P)], kv[:, 640:768])
            dve.wait_ge(copied, 3)
            dve.wait_ge(rotated, 2)
            qh, q2h = (a[:, :].rearrange("p (h e d) -> p h e d", h=8, e=2) for a in (q, q2))
            tq = [tb[:, n, :].rearrange("p (h d) -> p h d", h=8) for n in range(4)]
            rotate(qh[:, :, 0, :], qh[:, :, 1, :], q2h[:, :, 0, :], q2h[:, :, 1, :], (8, 32), tq)


def rwkv_projection(nc, ps, cst, l, xh, xl, w_rw, shift_in, mu_d, xmT, shift_out):
    with Scope(nc) as sc, stage(nc, "w_in0 w_in1 w_hi w_ready pool_hold s_in0 s_in1 mu_in done raw mixed raw_read sent0 sent1 chain zeroed sp_hold") as (
            block, w0, w1, w_hi, w_ready, pool_hold, s0, s1, mu_in, products, raw_ready, mixed, raw_read, sent0, sent1, chain_sem, zeroed, sp_hold):
        w_in, s_in, sent = (w0, w1), (s0, s1), (sent0, sent1)
        wt = sc.sb("rp_w", [P, 2, KD, P])
        wh = sc.sb("rp_wh", [P, 2, KD, P], F32R)
        wl = sc.sb("rp_wl", [P, 2, KD, P], F32R)
        raw = sc.sb("rp_raw", [P, 2, SEQ + 1])
        rsm = sc.sb("rp_rsm", [P, 2, NB, NQ + 1])
        shi = sc.sb("rp_shi", [P, 2, NB])
        xm = sc.sb("rp_xm", [P, 2, NT])
        sho = sc.sb("rp_sho", [P, 2, NB + 1])
        mu = sc.sb("rp_mu", [P, FR])
        muc = sc.sb("rp_muc", [P, 2])

        @block.sync
        def _(sp):
            def load(f, u):
                sp.dma_start(wt[:, u], w_rw[l, f]).then_inc(w_in[u], 16)
                sp.dma_start(shi[:, u, :], shift_in[l, f]).then_inc(s_in[u], 16)

            def store(f, u):
                sp.dma_start(xmT[f], xm[:, u, :]).then_inc(sent[u], 16)
                sp.dma_start(shift_out[l, f], sho[:, u, :]).then_inc(sent[u], 16)

            sp.sem_inc(sent[0], 32)
            sp.sem_inc(sent[1], 32)
            load(0, 0)
            load(1, 1)
            sp.dma_start(mu[:, :], mu_d).then_inc(mu_in, 16)
            with sp.Fori(0, FR // 2 - 1) as i:
                for u in range(2):
                    sp.wait_ge(mixed, 2 * i + u + 1)
                    sp.sem_inc(sp_hold, 1)
                    store(2 * i + u, u)
                    load(2 * i + u + 2, u)
            for u in range(2):
                sp.wait_ge(mixed, FR - 1 + u)
                store(FR - 2 + u, u)
            for u in range(2):
                sp.wait_ge(sent[u], 32 * (FR // 2 + 1))

        @block.gpsimd
        def _(pool):
            with pool.Fori(0, FR // 2) as i:
                for u in range(2):
                    pool.wait_ge(w_in[u], 16 * i + 16)
                    pool.sem_inc(pool_hold, 1)
                    split_weights(pool, wt[:, u], wh[:, u], wl[:, u], KD, w_hi, w_ready, lambda c: KD // CHUNK * (2 * i + u) + c)

        @block.tensor
        def _(pe):
            with pe.Fori(0, FR // 2) as i:
                for u in range(2):
                    pe.wait_ge(raw_ready, 2 * i + u + 1)
                    product3(pe, ps, 3 * u, wh[:, u], wl[:, u], xh, xl, KD, w_ready,
                             lambda c: KD // CHUNK * (2 * i + u) + c).then_inc(products, 1)

        @block.scalar
        def _(act):
            act.sem_inc(raw_ready, 2)
            with act.Fori(0, FR // 2) as i:
                for u in range(2):
                    act.wait_ge(products, 2 * i + u + 1)
                    act.wait_ge(raw_read, 2 * i + u + 1)
                    b = 3 * u * BANK
                    act.copy(raw[:, u, 1:385], ps[:, b:b + 384])
                    act.copy(raw[:, u, 385:769], ps[:, b + BANK:b + BANK + 384])
                    act.copy(raw[:, u, 769:1025], ps[:, b + 2 * BANK:b + 2 * BANK + 256])
                    act.copy(rsm[:, u, :, 1:NQ + 1],
                             ps[:, b + 2 * BANK + 256:b + 2 * BANK + 320].rearrange("p (b q) -> p b q", b=NB)).then_inc(raw_ready, 1)

        @block.vector
        def _(dve):
            dve.memset(raw[:, :, 0:1], 0.0).then_inc(zeroed, 1)
            dve.wait_ge(zeroed, 1)
            dve.sem_inc(raw_read, 2)
            dve.wait_ge(mu_in, 16)
            with dve.Fori(0, FR // 2) as i:
                for u in range(2):
                    dve.wait_ge(raw_ready, 2 * i + u + 3)
                    dve.wait_ge(s_in[u], 16 * i + 16)
                    dve.wait_ge(sent[u], 32 * i + 32)
                    dve.tensor_copy(rsm[:, u, :, 0], shi[:, u, :])
                    dve.tensor_copy(muc[:, u:u + 1], mu[:, ds(2 * i + u, 1)]).then_inc(chain_sem, 1)
                    dve.wait_ge(chain_sem, 2 * (2 * i + u) + 1)
                    dve.tensor_copy(sho[:, u, 0:1], raw[:, u, SEQ:SEQ + 1])
                    dve.tensor_copy(sho[:, u, 1:NB + 1], rsm[:, u, :, NQ])
                    xs = xm[:, u, SEQ:NT].rearrange("p (b q) -> p b q", b=NB)
                    dve.tensor_tensor(xm[:, u, 0:SEQ], raw[:, u, 0:SEQ], raw[:, u, 1:SEQ + 1], ALU.subtract)
                    dve.tensor_tensor(xs, rsm[:, u, :, 0:NQ], rsm[:, u, :, 1:NQ + 1], ALU.subtract).then_inc(chain_sem, 1)
                    dve.wait_ge(chain_sem, 2 * (2 * i + u) + 2)
                    dve.scalar_tensor_tensor(out=xm[:, u, 0:SEQ], in0=xm[:, u, 0:SEQ], scalar=muc[:, u:u + 1],
                                             in1=raw[:, u, 1:SEQ + 1], op0=ALU.mult, op1=ALU.add)
                    dve.scalar_tensor_tensor(out=xs, in0=xs, scalar=muc[:, u:u + 1], in1=rsm[:, u, :, 1:NQ + 1],
                                             op0=ALU.mult, op1=ALU.add).then_inc(mixed, 1)
                    dve.wait_ge(mixed, 2 * i + u + 1)
                    dve.sem_inc(raw_read, 1)


def rwkv_features(nc, ps, cst, l, xmT, lora_d, vec_d, arbk_d, rk_d, wend, const_d):
    with Scope(nc) as sc:
        wa = sc.sb("rf_wa", [P, NT])
        restart = sc.sb("rf_restart", [P, NT])
        vec = sc.sb("rf_vec", [P, 4, 4])
        vc = sc.sb("rf_vc", [P, 4])
        lora = sc.sb("rf_lora", [P, P])
        r, k, sw, a, ld, w, wp, wi, kk, t1 = (sc.sb(f"rf_{n}", [P, NT]) for n in
                                              ("r", "k", "sw", "a", "ld", "w", "wp", "wi", "kk", "t1"))
        rk = sc.sb("rf_rk", [P, NT])
        out = sc.sb("rf_out", [P, NCH + 1, 4, CH])
        with stage(nc, "loaded tanned") as (block, loaded, tanned):
            @block.sync
            def _(sp):
                sp.dma_start(wa[:, :], xmT[12]).then_inc(loaded, 16)
                sp.dma_start(vec[:, :, :], vec_d).then_inc(loaded, 16)
                sp.dma_start(restart[:, :], const_d[:, CO["restart"][0]:CO["restart"][0] + NT]).then_inc(loaded, 16)
                sp.wait_ge(loaded, 48)

            @block.scalar
            def _(act):
                act.wait_ge(loaded, 48)
                act.activation(wa[0:64, :], wa[0:64, :], ACT.Tanh).then_inc(tanned, 1)

        with nc.Fori(0, 4) as hp, stage(nc, "r_in lora_in vec_ready z_done gates_ready chain cum_ready prev_ready decays sq_ready sq_done sum_ready rooted ready stored") as (
                block, r_in, lora_in, vec_ready, z_done, gates_ready, chain_sem, cum_ready, prev_ready, decays, sq_ready, sq_done, sum_ready, rooted, ready, stored):

            @block.sync
            def _(sp):
                sp.dma_start(lora[:, :], lora_d[:, ds(hp * P, P)]).then_inc(lora_in, 16)
                sp.dma_start(r[:, :], xmT[hp]).then_inc(r_in, 16)
                sp.dma_start(k[:, :], xmT[hp + 4]).then_inc(r_in, 16)
                sp.wait_ge(ready, 1)
                sp.dma_start(arbk_d[:, :, hp].rearrange("c p n -> p c n"), out[:, :, :, :].rearrange("p c a t -> p c (a t)")).then_inc(stored, 16)
                sp.dma_start(rk_d[hp], rk[:, :]).then_inc(stored, 16)
                sp.wait_ge(stored, 32)

            @block.tensor
            def _(pe):
                pe.wait_ge(lora_in, 16)
                for half in range(2):
                    for n, (o, c) in enumerate(GROUPS):
                        b = (3 * half + n) * BANK
                        m = pe.matmul(ps[:, b:b + c], lora[64 * half:64 * half + 64, :], wa[64 * half:64 * half + 64, o:o + c], start=True, stop=True)
                    m.then_inc(z_done, 1)
                pe.wait_ge(sq_ready, 1)
                pe.wait_ge(gates_ready, 1)
                for n, (o, c) in enumerate(GROUPS):
                    m = pe.matmul(ps[:, n * BANK:n * BANK + c], cst["blk"], t1[:, o:o + c], start=True, stop=True)
                m.then_inc(sq_done, 1)

            @block.scalar
            def _(act):
                act.wait_ge(vec_ready, 1)
                for half, dst in enumerate((sw, a)):
                    act.wait_ge(z_done, half + 1)
                    for n, (o, c) in enumerate(GROUPS):
                        b = (3 * half + n) * BANK
                        m = act.activation(dst[:, o:o + c], ps[:, b:b + c], ACT.Sigmoid, bias=vc[:, half:half + 1])
                    m.then_inc(gates_ready, 1)
                act.wait_ge(cum_ready, 1)
                act.activation(w[:, :], wp[:, :], ACT.Exp)
                act.activation(wi[:, :], wp[:, :], ACT.Exp, scale=-1.0).then_inc(decays, 1)
                act.wait_ge(prev_ready, 1)
                act.activation(ld[:, :], ld[:, :], ACT.Exp).then_inc(decays, 1)
                act.wait_ge(sum_ready, 1)
                act.activation(t1[:, :], t1[:, :], ACT.Sqrt).then_inc(rooted, 1)

            @block.vector
            def _(dve):
                step = Chain(dve, chain_sem)
                for n in range(4):
                    m = dve.tensor_copy(vc[:, n:n + 1], vec[:, n, ds(hp, 1)])
                m.then_inc(vec_ready, 1)
                dve.wait_ge(vec_ready, 1)
                dve.wait_ge(r_in, 32)
                step(dve.tensor_scalar(kk[:, :], k[:, :], vc[:, 2:3], None, ALU.mult))
                dve.tensor_tensor(t1[:, :], kk[:, :], kk[:, :], ALU.mult).then_inc(sq_ready, 1)
                dve.wait_ge(gates_ready, 1)
                step(dve.tensor_scalar(ld[:, :], sw[:, :], -E05, None, ALU.mult))
                step(dve.tensor_tensor_scan(wp[:, :], restart[:, :], ld[:, :], 0.0, ALU.mult, ALU.add))
                dve.tensor_tensor(ld[:, :], wp[:, :], ld[:, :], ALU.subtract).then_inc(prev_ready, 1)
                dve.sem_inc(cum_ready, 1)
                dve.wait_ge(gates_ready, 2)
                step(dve.tensor_scalar(sw[:, :], a[:, :], 1.0, vc[:, 3:4], ALU.subtract, ALU.mult))
                step(dve.scalar_tensor_tensor(out=sw[:, :], in0=sw[:, :], scalar=1.0, in1=k[:, :], op0=ALU.add, op1=ALU.mult))
                dve.tensor_tensor(rk[:, :], r[:, :], sw[:, :], ALU.mult)
                dve.wait_ge(sq_done, 1)
                for n, (o, c) in enumerate(GROUPS):
                    m = dve.tensor_scalar(t1[:, o:o + c], ps[:, n * BANK:n * BANK + c], 1e-24, None, ALU.max)
                m.then_inc(sum_ready, 1)
                dve.wait_ge(rooted, 1)
                step(dve.reciprocal(t1[:, :], t1[:, :]))
                step(dve.tensor_tensor(kk[:, :], kk[:, :], t1[:, :], ALU.mult))
                dve.wait_ge(decays, 2)

                def parts(x):
                    return x[:, :].rearrange("p (c t) -> p c t", t=CH)

                step(dve.tensor_tensor(out[:, :, 1, :], parts(r), parts(w), ALU.mult))
                dve.scalar_tensor_tensor(out=out[:, :, 0, :], in0=parts(kk), scalar=-1.0, in1=parts(ld), op0=ALU.mult, op1=ALU.mult)
                for e in range(2):
                    hf = slice(64 * e, 64 * e + 64)
                    m = dve.tensor_tensor(out[hf, :, 3 - e, :], parts(sw)[hf], parts(wi)[hf], ALU.mult)
                step(m)
                step(dve.tensor_tensor(kk[:, :], kk[:, :], a[:, :], ALU.mult))
                for e in range(2):
                    hf = slice(64 * e, 64 * e + 64)
                    dve.tensor_tensor(out[hf, :, 2 + e, :], parts(kk)[hf], parts(wi)[hf], ALU.mult)
                dve.tensor_copy(wend[:, ds(hp, 1), 0:NCH], w[:, CH - 1:SEQ:CH].unsqueeze(1))
                dve.tensor_copy(wend[:, ds(hp, 1), NCH:NCH + NB], w[:, SEQ + NQ - 1:NT:NQ].unsqueeze(1)).then_inc(ready, 1)


def rwkv_chunks(nc, ps, cst, cs, sample, B, wend, arbk_d, xmT, yr_d, vr_d):
    levels = 3 if sample else 6
    streams = range(len(cs))
    arbk, vT, G, AT, CT, XX, ys, p1, bkr, UV, yo, masks, S, AM, RM, S8, UVm = (B[n] for n in (
        "arbk", "vT", "G", "AT", "CT", "XX", "ys", "p1", "bkr", "UV", "yo", "masks", "S", "AM", "RM", "S8", "UVm"))
    HALF = (slice(0, 64), slice(64, 128))
    OTHER = (slice(64, 128), slice(0, 64))
    with stage(nc, "in0 in1 gram0 gram1 masked rows0 rows1 rows_copied started x_ready0 x_ready1 ct_ready0 ct_ready1 y_done0 y_done1 "
                   "y_copied0 y_copied1 z_done0 z_done1 x_done0 x_done1 am_ready p1_done p1_copied u_done u_copied st_done s_ready "
                   "out_done out_copied uvm_ready chain stored") as (
            block, in0, in1, gram0, gram1, masked, rows0, rows1, rows_copied, started, xr0, xr1, ct0, ct1, yd0, yd1, yc0, yc1, zd0, zd1,
            xd0, xd1, am_ready, p1_done, p1_copied, u_done, u_copied, st_done, s_ready, out_done, out_copied, uvm_ready, chain_sem, stored):
        in_, gram, rows, x_ready, ct_ready = (in0, in1), (gram0, gram1), (rows0, rows1), (xr0, xr1), (ct0, ct1)
        y_done, y_copied, z_done, x_done = (yd0, yd1), (yc0, yc1), (zd0, zd1), (xd0, xd1)

        @block.sync
        def _(sp):
            for s in streams:
                sp.dma_start(arbk[:, s], arbk_d[cs[s]].rearrange("p h (a t) -> p h a t", a=4)).then_inc(in_[s], 16)
                sp.dma_start(vT[:, s], xmT[8:12, :, ds(cs[s] * CH, CH)].rearrange("h p t -> p h t")).then_inc(in_[s], 16)
            for s in streams:
                sp.wait_ge(out_copied, s + 1)
                for e in range(2):
                    tokens, cols = ds(cs[s] * CH, CH), slice(256 * e, 256 * e + 256)
                    sp.dma_start(yr_d[tokens, cols], yo[HALF[e], s].rearrange("p h d -> p (h d)")).then_inc(stored, 16)
                    sp.dma_start(vr_d[tokens, cols], UV[OTHER[e], s, e].rearrange("p h d -> p (h d)")).then_inc(stored, 16)
            sp.wait_ge(stored, 64 * len(cs))

        @block.tensor
        def _(pe):
            for s in streams:
                pe.wait_ge(in_[s], 32)
                for e in range(2):
                    for h in range(4):
                        bk = arbk[HALF[e], s, h, 2:4, :].rearrange("p a t -> p (a t)")
                        ar = arbk[HALF[e], s, h, 0:2, :].rearrange("p a t -> p (a t)")
                        o = (4 + 2 * s + e) * BANK + h * P
                        m = pe.matmul(ps[:, o:o + P], bk, ar, start=True, stop=True)
                m.then_inc(gram[s], 1)
                for h in range(4):
                    o = 2 * s * BANK + h * P
                    pe.transpose(ps[:, o:o + P], arbk[:, s, h, 2:4, :].rearrange("p a t -> p (a t)"), cst["ident"])
                for h in range(4):
                    for e in range(2):
                        o = (2 * s + 1) * BANK + e * 256 + h * 64
                        m = pe.matmul(ps[OTHER[e], o:o + 64], vT[:, s, h, :], cst["ident"][:, 64 * e:64 * e + 64], start=True, stop=True)
                m.then_inc(rows[s], 1)
            for n in range(levels):
                for s in streams:
                    pe.wait_ge(ct_ready[s], n + 1)
                    if n:
                        pe.wait_ge(x_done[s], n)
                    else:
                        pe.wait_ge(x_ready[s], 1)
                        pe.wait_ge(rows_copied, s + 1)
                    for h in range(4):
                        for e in range(2):
                            o = 2 * s * BANK + h * 64
                            m = pe.matmul(ps[HALF[e], o:o + 64], CT[HALF[e], s, h, :], XX[HALF[e], s, 0, h, :], start=True, stop=True)
                    m.then_inc(y_done[s], 1)
                for s in streams:
                    pe.wait_ge(y_copied[s], n + 1)
                    for h in range(4):
                        for e in range(2):
                            o = (2 * s + 1) * BANK + h * 64
                            y, xt = ys[HALF[e], s, h, :], XX[HALF[e], s, 1, h, :]
                            pe.matmul(ps[HALF[e], o:o + 64], xt, y, start=True, stop=True)
                            m = pe.matmul(ps[HALF[e], o + 256:o + 320], y, xt, start=True, stop=True)
                    m.then_inc(z_done[s], 1)

            def with_state(bank, s, which, wide):
                for h in range(4):
                    for e in range(2):
                        o = ps[HALF[e], bank * BANK + h * 64:bank * BANK + (h + 1) * 64]
                        if sample:
                            for n in range(NB):
                                pe.matmul(o, wide[HALF[e], h, n, :], S8[HALF[e], h, n, :], start=(n == 0), stop=False)
                        else:
                            pe.matmul(o, arbk[HALF[e], s, h, which, :], S[HALF[e], s, h, :], start=True, stop=False)
                        m = pe.matmul(o, G[:, s, e, h, 64 * which:64 * which + 64], UV[:, s, e, h, :], start=False, stop=True)
                return m

            pe.wait_ge(masked, 2 * len(cs))
            if sample:
                pe.wait_ge(am_ready, 1)
            for s in streams:
                pe.wait_ge(started, 1)
                if s:
                    pe.wait_ge(s_ready, s)
                with_state(4, s, 0, AM).then_inc(p1_done, 1)
                pe.wait_ge(x_done[s], levels)
                pe.wait_ge(p1_copied, s + 1)
                for h in range(4):
                    for e in range(2):
                        m = pe.matmul(ps[HALF[e], 5 * BANK + h * 64:5 * BANK + (h + 1) * 64], XX[HALF[e], s, 1, h, :], p1[HALF[e], h, :], start=True, stop=True)
                m.then_inc(u_done, 1)
                pe.wait_ge(u_copied, s + 1)
                if sample:
                    pe.wait_ge(uvm_ready, 1)
                for h in range(4):
                    for e in range(2):
                        k = bkr[:, s, h, 64 * e:64 * e + 64]
                        if sample:
                            m = pe.matmul(ps[HALF[e], h * BANK:(h + 1) * BANK], k, UVm[:, :, e, h, :], start=True, stop=True)
                        else:
                            m = pe.matmul(ps[HALF[e], 7 * BANK + h * 64:7 * BANK + (h + 1) * 64], k, UV[:, s, e, h, :], start=True, stop=True)
                m.then_inc(st_done, 1)
                if s:
                    pe.wait_ge(out_copied, s)
                with_state(6, s, 1, RM).then_inc(out_done, 1)

        @block.scalar
        def _(act):
            for s in streams:
                act.wait_ge(rows[s], 1)
                act.copy(bkr[:, s, :, :], ps[:, 2 * s * BANK:(2 * s + 1) * BANK].rearrange("p (h t) -> p h t", h=4))
                for e in range(2):
                    o = (2 * s + 1) * BANK + e * 256
                    m = act.copy(UV[OTHER[e], s, e], ps[OTHER[e], o:o + 256].rearrange("p (h t) -> p h t", h=4))
                m.then_inc(rows_copied, 1)
            for n in range(levels):
                for s in streams:
                    act.wait_ge(y_done[s], n + 1)
                    if n:
                        act.wait_ge(z_done[s], n)
                    act.copy(ys[:, s], ps[:, 2 * s * BANK:2 * s * BANK + 256].rearrange("p (h t) -> p h t", h=4)).then_inc(y_copied[s], 1)
            for s in streams:
                act.wait_ge(p1_done, s + 1)
                if s:
                    act.wait_ge(u_done, s)
                act.copy(p1[:, :, :], ps[:, 4 * BANK:4 * BANK + 256].rearrange("p (h t) -> p h t", h=4)).then_inc(p1_copied, 1)
                act.wait_ge(u_done, s + 1)
                for e in range(2):
                    m = act.copy(UV[HALF[e], s, e], ps[HALF[e], 5 * BANK:5 * BANK + 256].rearrange("p (h t) -> p h t", h=4))
                m.then_inc(u_copied, 1)
                act.wait_ge(out_done, s + 1)
                act.copy(yo[:, s], ps[:, 6 * BANK:6 * BANK + 256].rearrange("p (h t) -> p h t", h=4)).then_inc(out_copied, 1)

        @block.vector
        def _(dve):
            step = Chain(dve, chain_sem)
            for e in range(2):
                dve.memset(UV[HALF[e], 0:len(cs), e], 0.0)
            for s in streams:
                for j in range(2):
                    for e in range(2):
                        m = dve.tensor_copy(XX[HALF[e], s, j], mid(cst["ident"][HALF[e], 64 * e:64 * e + 64], 4))
                m.then_inc(x_ready[s], 1)
            dve.sem_inc(started, 1)
            for s in streams:
                dve.wait_ge(gram[s], 1)
                for e in range(2):
                    o = (4 + 2 * s + e) * BANK
                    dve.tensor_tensor(G[:, s, e], ps[:, o:o + BANK].rearrange("p (h t) -> p h t", h=4), mid(masks[:, 0:P], 4), ALU.mult).then_inc(masked, 1)
                dve.wait_ge(masked, 2 * s + 2)
                for e in range(2):
                    m = dve.tensor_copy(AT[HALF[e], s], G[HALF[e], s, e, :, 0:64])
                step(m)
            if sample:
                dve.wait_ge(in0, 32)
                for which, dst in ((0, AM), (1, RM)):
                    for h in range(4):
                        m = dve.tensor_tensor(dst[:, h], mid(arbk[:, 0, h, which, :], NB), masks[:, P + 384:P + 384 + 512].rearrange("p (b t) -> p b t", b=NB), ALU.mult)
                m.then_inc(am_ready, 1)
            for n in range(levels):
                for s in streams:
                    if n:
                        dve.wait_ge(y_done[s], n)
                    dve.tensor_tensor(CT[:, s], AT[:, s], mid(masks[:, P + n * 64:P + (n + 1) * 64], 4), ALU.mult).then_inc(ct_ready[s], 1)
                for s in streams:
                    dve.wait_ge(z_done[s], n + 1)
                    if n:
                        dve.wait_ge(x_done[s], n)
                    else:
                        dve.wait_ge(x_ready[s], 1)
                    o = (2 * s + 1) * BANK
                    x = XX[:, s].rearrange("p j h t -> p (j h t)")
                    dve.tensor_tensor(x, x, ps[:, o:o + BANK], ALU.add).then_inc(x_done[s], 1)
            if sample:
                dve.wait_ge(u_copied, 1)
                for n in range(NB):
                    a = P + 384 + 512 + n
                    m = dve.tensor_scalar(UVm[:, n].rearrange("p e h d -> p (e h d)"), UV[:, 0].rearrange("p e h d -> p (e h d)"), masks[:, a:a + 1], None, ALU.mult)
                m.then_inc(uvm_ready, 1)
                dve.wait_ge(st_done, 1)
                dve.wait_ge(out_done, 1)
                for h in range(4):
                    m = dve.tensor_tensor(S8[:, h], S8[:, h], ps[:, h * BANK:(h + 1) * BANK].rearrange("p (b t) -> p b t", b=NB), ALU.add)
                step(m)
                for h in range(4):
                    dve.tensor_tensor(S8[:, h], S8[:, h], bc(wend[:, h, NCH:NCH + NB], 64), ALU.mult)
            else:
                for s in streams:
                    dve.wait_ge(st_done, s + 1)
                    if s:
                        dve.wait_ge(out_done, s)
                    step(dve.tensor_tensor(S[:, 1 - s], S[:, s], ps[:, 7 * BANK:7 * BANK + 256].rearrange("p (h t) -> p h t", h=4), ALU.add))
                    dve.tensor_tensor(S[:, 1 - s], S[:, 1 - s], wend[:, :, ds(cs[s], 1)].to_broadcast([P, 4, 64]), ALU.mult).then_inc(s_ready, 1)
                    dve.wait_ge(s_ready, s + 1)


def rwkv_scan(nc, ps, cst, l, wend, const_d, arbk_d, xmT, yr_d, vr_d, s_in, s_out):
    with Scope(nc) as sc:
        shapes = {"arbk": [2, 4, 4, CH], "vT": [2, 4, CH], "G": [2, 2, 4, P], "AT": [2, 4, CH], "CT": [2, 4, CH], "XX": [2, 2, 4, CH],
                  "ys": [2, 4, CH], "p1": [4, 64], "bkr": [2, 4, P], "UV": [2, 2, 4, 64], "yo": [2, 4, 64], "masks": [P + 384 + 512 + NB],
                  "S": [2, 4, 64], "AM": [4, NB, CH], "RM": [4, NB, CH], "S8": [4, NB, 64], "UVm": [NB, 2, 4, 64]}
        B = {n: sc.sb(f"rc_{n}", [P, *s]) for n, s in shapes.items()}
        masks, S, S8 = B["masks"], B["S"], B["S8"]
        with stage(nc, "loaded zeroed") as (block, loaded, zeroed):
            @block.sync
            def _(sp):
                o = 0
                for name in ("gmask", "lev", "seqt", "seqp"):
                    a, w = CO[name]
                    sp.dma_start(masks[:, o:o + w], const_d[:, a:a + w]).then_inc(loaded, 16)
                    o += w
                sp.dma_start(S8[:, :, :, :], s_in[l]).then_inc(loaded, 16)
                sp.wait_ge(loaded, 80)

            @block.vector
            def _(dve):
                dve.memset(S[:, 0], 0.0).then_inc(zeroed, 1)

        with nc.Fori(0, NCH // 2) as c:
            rwkv_chunks(nc, ps, cst, (2 * c, 2 * c + 1), False, B, wend, arbk_d, xmT, yr_d, vr_d)
        with stage(nc, "loaded") as (block, loaded):
            @block.sync
            def _(sp):
                a, w = CO["gmask_s"]
                sp.dma_start(masks[:, 0:P], const_d[:, a:a + w]).then_inc(loaded, 16)
                sp.wait_ge(loaded, 16)
        rwkv_chunks(nc, ps, cst, (NCH,), True, B, wend, arbk_d, xmT, yr_d, vr_d)
        with stage(nc, "stored") as (block, stored):
            @block.sync
            def _(sp):
                sp.dma_start(s_out[l, :, :, 0], S[:, 0]).then_inc(stored, 16)
                sp.dma_start(s_out[l, :, :, 1:NB + 1], S8[:, :, :, :]).then_inc(stored, 16)
                sp.wait_ge(stored, 32)


def rwkv_output(nc, ps, cst, l, mixT, xmT, rk_d, yr_d, vr_d, gb_d, gn_d, rk8_d):
    with Scope(nc) as sc:
        y, v, o, t1 = (sc.sb(f"ro_{n}", [P, 512]) for n in ("y", "v", "o", "t1"))
        rk = sc.sb("ro_rk", [P, 4, P])
        ga = sc.sb("ro_ga", [P, P])
        gb = sc.sb("ro_gb", [P, 512])
        gn = sc.sb("ro_gn", [P, 2, 512])
        rk8 = sc.sb("ro_rk8", [P, 4, 8])
        mean, var, bonus = (sc.sb(f"ro_{n}", [P, 8]) for n in ("mean", "var", "bonus"))
        with stage(nc, "loaded") as (block, loaded):
            @block.sync
            def _(sp):
                sp.dma_start(gb[:, :], gb_d[l]).then_inc(loaded, 16)
                for n in range(2):
                    sp.dma_start(gn[:, n], gn_d[l, n].partition_broadcast(P)).then_inc(loaded, 16)
                sp.dma_start(rk8[:, :, :], rk8_d[l]).then_inc(loaded, 16)
                sp.wait_ge(loaded, 64)

        def tile(t, m):
            with stage(nc, "y_in g_in sig g_done b_done chain centred var_ready rooted ready turned kept") as (
                    block, y_in, g_in, sig, g_done, b_done, chain_sem, centred, var_ready, rooted, ready, turned, kept):
                @block.sync
                def _(sp):
                    sp.dma_start(y[0:m, :], yr_d[ds(t * P, m), :]).then_inc(y_in, 16)
                    sp.dma_start(v[0:m, :], vr_d[ds(t * P, m), :]).then_inc(y_in, 16)
                    sp.dma_start(ga[:, 0:m], xmT[13, :, ds(t * P, m)]).then_inc(g_in, 16)
                    sp.dma_start(rk[:, :, 0:m], rk_d[:, :, ds(t * P, m)].rearrange("h p t -> p h t")).then_inc(g_in, 16)

                @block.scalar
                def _(act):
                    act.wait_ge(g_in, 32)
                    act.activation(ga[:, 0:m], ga[:, 0:m], ACT.Sigmoid).then_inc(sig, 1)
                    act.wait_ge(centred, 1)
                    act.activation(t1[0:m, :], y[0:m, :], ACT.Square).then_inc(sig, 1)
                    act.wait_ge(var_ready, 1)
                    act.activation(var[0:m, :], var[0:m, :], ACT.Sqrt).then_inc(rooted, 1)
                    act.wait_ge(turned, 1)
                    act.copy(mixT[:, 4:8, ds(t * P, m)], ps[:, 2 * BANK:3 * BANK].rearrange("p (h t) -> p h t", h=4)[:, :, 0:m]).then_inc(kept, 1)

                @block.tensor
                def _(pe):
                    pe.wait_ge(g_in, 32)
                    for hp in range(4):
                        mm = pe.matmul(ps[0:m, BANK:BANK + 8], rk[:, hp, 0:m], rk8[:, hp, :], start=(hp == 0), stop=(hp == 3))
                    mm.then_inc(b_done, 1)
                    pe.wait_ge(sig, 1)
                    pe.matmul(ps[0:m, 0:BANK], ga[:, 0:m], gb[:, :], start=True, stop=True).then_inc(g_done, 1)
                    pe.wait_ge(ready, 1)
                    for hp in range(4):
                        mm = pe.transpose(ps[:, 2 * BANK + hp * P:2 * BANK + hp * P + m], o[0:m, hp * P:(hp + 1) * P], cst["ident"][0:m, 0:m])
                    mm.then_inc(turned, 1)

                @block.vector
                def _(dve):
                    step = Chain(dve, chain_sem)

                    def hv(x):
                        return x[0:m, :].rearrange("p (h d) -> p h d", h=HH)

                    dve.wait_ge(y_in, 32)
                    step(dve.tensor_reduce(mean[0:m, :], hv(y), AX.X, ALU.add))
                    step(dve.tensor_scalar(mean[0:m, :], mean[0:m, :], 1.0 / HD, None, ALU.mult))
                    dve.tensor_tensor(hv(y), hv(y), bc(mean[0:m, :], HD), ALU.subtract).then_inc(centred, 1)
                    dve.wait_ge(b_done, 1)
                    step(dve.tensor_copy(bonus[0:m, :], ps[0:m, BANK:BANK + 8]))
                    dve.tensor_tensor(hv(v), hv(v), bc(bonus[0:m, :], HD), ALU.mult)
                    dve.wait_ge(sig, 2)
                    step(dve.tensor_reduce(var[0:m, :], hv(t1), AX.X, ALU.add))
                    dve.tensor_scalar(var[0:m, :], var[0:m, :], 1.0 / HD, 64e-5, ALU.mult, ALU.add).then_inc(var_ready, 1)
                    dve.wait_ge(rooted, 1)
                    step(dve.reciprocal(var[0:m, :], var[0:m, :]))
                    step(dve.tensor_tensor(hv(y), hv(y), bc(var[0:m, :], HD), ALU.mult))
                    step(dve.tensor_tensor(y[0:m, :], y[0:m, :], gn[0:m, 0, :], ALU.mult))
                    step(dve.tensor_tensor(y[0:m, :], y[0:m, :], gn[0:m, 1, :], ALU.add))
                    step(dve.tensor_tensor(y[0:m, :], y[0:m, :], v[0:m, :], ALU.add))
                    dve.wait_ge(g_done, 1)
                    dve.tensor_tensor(o[0:m, :], y[0:m, :], ps[0:m, 0:BANK], ALU.mult).then_inc(ready, 1)

        with nc.Fori(0, SEQ // P) as t:
            tile(t, P)
        tile(SEQ // P, NS)


def block_ranks(dve, step, sel, score, rows, g, nb, low, gt, eq, rank):
    a = score[0:rows].unsqueeze(2).to_broadcast([rows, g, nb, nb])
    b = bc(score[0:rows], nb)
    lo = low[0:rows].rearrange("p (s t) -> p s t", s=nb).unsqueeze(1).to_broadcast([rows, g, nb, nb])
    for n in range(g):
        dve.tensor_tensor(gt[0:rows, n], a[:, n], b[:, n], ALU.is_gt)
        m = dve.tensor_tensor(eq[0:rows, n], a[:, n], b[:, n], ALU.is_equal)
    step(m)
    for n in range(g):
        m = dve.tensor_tensor(eq[0:rows, n], eq[0:rows, n], lo[:, n], ALU.mult)
    step(m)
    step(dve.tensor_tensor(gt[0:rows], gt[0:rows], eq[0:rows], ALU.add))
    step(dve.tensor_reduce(rank[0:rows], gt[0:rows], AX.X, ALU.add))
    return dve.tensor_scalar(sel, rank[0:rows], 7.5, NEG, ALU.is_ge, ALU.mult)


class Compressor:

    def __init__(self, nc, sc):
        self.kvp = sc.sb("cp_kvp", [P, 4, 1024])
        self.kvc = sc.sb("cp_kvc", [P, 4, 4, P])
        self.kt = sc.sb("cp_kt", [P, 4, 512])
        self.w1 = sc.sb("cp_w1", [P, 2, 16, 256])
        self.w2 = sc.sb("cp_w2", [P, 2, 2, HD])
        self.pe_ = sc.sb("cp_pe", [P, 2, 16])
        self.bias = sc.sb("cp_bias", [P, 4])
        self.hid = sc.sb("cp_hid", [P, 2, 2, 2, 64])
        self.kc = sc.sb("cp_kc", [P, 64])
        self.vc = sc.sb("cp_vc", [64, 2, HD])

    def weights(self, nc, ps, l, w1_d, w2_d, pe_d):
        with stage(nc, "loaded bias_done zeroed") as (block, loaded, bias_done, zeroed):
            @block.sync
            def _(sp):
                for n in range(2):
                    sp.dma_start(self.w1[:, n], w1_d[l, n]).then_inc(loaded, 16)
                    sp.dma_start(self.w2[:, n], w2_d[l, n]).then_inc(loaded, 16)
                    sp.dma_start(self.pe_[:, n], pe_d[l, n]).then_inc(loaded, 16)

            @block.tensor
            def _(pe):
                pe.wait_ge(loaded, 96)
                for n in range(4):
                    for q in range(16):
                        m = pe.matmul(ps[:, n:n + 1], self.w1[:, n // 2, q, (n % 2) * P:(n % 2 + 1) * P],
                                      self.pe_[:, n // 2, q:q + 1], start=(q == 0), stop=(q == 15))
                m.then_inc(bias_done, 1)

            @block.vector
            def _(dve):
                dve.memset(self.hid[:, :, :, :, :], 0.0).then_inc(zeroed, 1)
                dve.wait_ge(bias_done, 1)
                dve.tensor_copy(self.bias[:, :], ps[:, 0:4])
                dve.wait_ge(zeroed, 1)

    def run(self, nc, ps, cst, loads, extra=None):
        with stage(nc, "loaded sorted_ turned odd_copied even_copied hidden hid_ready c_done") as (
                block, loaded, sorted_, turned, odd_copied, even_copied, hidden, hid_ready, c_done):
            count = []

            @block.sync
            def _(sp):
                count.append(loads(sp, loaded))
                sp.wait_ge(loaded, count[0])

            @block.tensor
            def _(pe):
                for kg in range(4):
                    pe.wait_ge(sorted_, 4)
                    for n in range(4):
                        m = pe.transpose(ps[:, kg * BANK + n * P:kg * BANK + (n + 1) * P], self.kvc[:, n, kg, :], cst["ident"])
                    m.then_inc(turned, 1)
                for kv in range(2):
                    pe.wait_ge(even_copied, kv + 1)
                    pe.wait_ge(odd_copied, kv + 1)
                    for half in range(2):
                        b = (4 + 2 * kv + half) * BANK
                        for q in range(16):
                            m = pe.matmul(ps[:, b:b + 126], self.w1[:, kv, q, half * P:(half + 1) * P],
                                          self.kt[:, 2 * kv:2 * kv + 2, q:q + 8 * 62 + 1:8], start=(q == 0), stop=(q == 15))
                        m.then_inc(hidden, 1)
                pe.wait_ge(hid_ready, 4)
                for g in range(2):
                    for half in range(2):
                        pe.matmul(ps[64 * g:64 * g + 64, 0:64], self.w2[:, 0, half, :], self.hid[:, 0, half, g, :], start=(half == 0), stop=(half == 1))
                for g in range(2):
                    for half in range(2):
                        m = pe.matmul(ps[0:64, BANK + g * 64:BANK + g * 64 + 64], self.hid[:, 1, half, g, :], self.w2[:, 1, half, :], start=(half == 0), stop=(half == 1))
                m.then_inc(c_done, 1)

            @block.vector
            def _(dve):
                dve.wait_ge(loaded, count[0])
                for n in range(4):
                    dve.tensor_copy(self.kvc[:, n].rearrange("p kg (e d) -> p e kg d", e=2),
                                    self.kvp[:, n].rearrange("p (e a kg d) -> p e a kg d", e=2, a=2, kg=4)[:, :, 0]).then_inc(sorted_, 1)
                for kg in range(1, 4, 2):
                    dve.wait_ge(turned, kg + 1)
                    dve.tensor_copy(self.kt[:, kg, :], ps[:, kg * BANK:(kg + 1) * BANK]).then_inc(odd_copied, 1)
                dve.wait_ge(c_done, 1)
                dve.tensor_copy(self.kc[:, :], ps[:, 0:64])
                dve.tensor_copy(self.vc[:, :, :], ps[0:64, BANK:BANK + P].rearrange("p (g d) -> p g d", g=2))

            @block.scalar
            def _(act):
                for kg in range(0, 4, 2):
                    act.wait_ge(turned, kg + 1)
                    act.copy(self.kt[:, kg, :], ps[:, kg * BANK:(kg + 1) * BANK]).then_inc(even_copied, 1)
                for n in range(4):
                    act.wait_ge(hidden, n + 1)
                    b = (4 + n) * BANK
                    act.activation(self.hid[:, n // 2, n % 2, :, 0:63], ps[:, b:b + 126].rearrange("p (g c) -> p g c", g=2),
                                   ACT.Silu, bias=self.bias[:, n:n + 1]).then_inc(hid_ready, 1)


def sample_attention(nc, ps, cst, l, cp, qT, cache, ptab, kvrows, winr, gs_d, os_d, state_win, const_d):
    with Scope(nc) as sc:
        q = sc.sb("sa_q", [P, R4, NQ])
        wk = sc.sb("sa_wk", [P, 2, 256])
        kn = sc.sb("sa_kn", [NQ, 512])
        wn = sc.sb("sa_wn", [NQ, 256])
        g3 = sc.sb("sa_g3", [64, 3, 8])
        ksT = sc.sb("sa_ksT", [P, 2, 512])
        wT = sc.sb("sa_wT", [P, 272])
        s = sc.sb("sa_s", [64, 1032])
        sw = sc.sb("sa_sw", [64, 264])
        pT = sc.sb("sa_pT", [P, 9, 64])
        pwT = sc.sb("sa_pwT", [P, 3, 64])
        pc = sc.sb("sa_pc", [64, 64])
        pcT = sc.sb("sa_pcT", [64, 64])
        pg = sc.sb("sa_pg", [64, 72])
        im = sc.sb("sa_im", [64, 17])
        im2 = sc.sb("sa_im2", [64, 1, 17])
        sel = sc.sb("sa_sel", [64, 1, 17])
        gt = sc.sb("sa_gt", [64, 1, 17, 17])
        eq = sc.sb("sa_eq", [64, 1, 17, 17])
        rank = sc.sb("sa_rank", [64, 1, 17])
        st = sc.sb("sa_st", [64, 16])
        o = sc.sb("sa_o", [64, HD])
        names = ("low17", "swin", "snew", "skeep", "sadd", "hsel", "same")
        off, w = {}, 0
        for n in names:
            off[n] = w
            w += CO[n][1]
        cm = sc.sb("sa_cm", [64, w])
        K = {n: cm[:, off[n]:off[n] + CO[n][1]] for n in names}
        with stage(nc, "loaded zeroed") as (block, loaded, zeroed):
            @block.sync
            def _(sp):
                for n in names:
                    a, ww = CO[n]
                    sp.dma_start(cm[:, off[n]:off[n] + ww], const_d[0:64, a:a + ww]).then_inc(loaded, 16)
                sp.wait_ge(loaded, 16 * len(names))

            @block.vector
            def _(dve):
                dve.memset(pg[:, :], 0.0).then_inc(zeroed, 1)

        with nc.Fori(0, NB) as b:
            def loads(sp, sem):
                for p in range(PAGES):
                    page = sp.value_load(ptab[0:1, ds(b * PAGES + p, 1)], min_val=0, max_val=NPHYS - 1)
                    sp.dma_start(cp.kvp[64 * (p % 2):64 * (p % 2) + 64, p // 2, :], cache[l, page]).then_inc(sem, 16)
                sp.dma_start(wk[:, :, :], state_win[l, b].rearrange("(h p) n -> p h n", p=P)).then_inc(sem, 16)
                sp.dma_start(kn[:, :], kvrows[l, ds(SEQ + b * NQ, NQ), :]).then_inc(sem, 16)
                sp.dma_start(wn[:, :], winr[ds(SEQ + b * NQ, NQ), :]).then_inc(sem, 16)
                for gr in range(8):
                    src = gs_d[ds(b * NQ, NQ), :].rearrange("q (c h) -> q c h", c=3)
                    sp.dma_start(g3[gr * 8:gr * 8 + 8, :, :], src).then_inc(sem, 16)
                return 16 * (PAGES + 11)

            cp.run(nc, ps, cst, loads)
            with stage(nc, "q_ready turned k_copied c_scored s_scored w_scored c_masked c_exp c_ready c_turned c_copied c_out imp_ready imp_done s_masked s_exp s_turned s_copied s_out w_masked w_exp w_turned w_copied w_out chain out_ready stored") as (
                    block, q_ready, turned, k_copied, c_scored, s_scored, w_scored, c_masked, c_exp, c_ready, c_turned, c_copied, c_out, imp_ready, imp_done,
                    s_masked, s_exp, s_turned, s_copied, s_out, w_masked, w_exp, w_turned, w_copied, w_out, chain_sem, out_ready, stored):
                @block.sync
                def _(sp):
                    sp.wait_ge(out_ready, 1)
                    for g in range(2):
                        for r in range(R4):
                            row = g * 32 + r * 8
                            sp.dma_start(os_d[ds(b * NQ, NQ), r * P + g * HD:r * P + (g + 1) * HD], o[row:row + 8, :]).then_inc(stored, 16)
                    sp.wait_ge(stored, 128)

                @block.tensor
                def _(pe):
                    for e in range(2):
                        for n in range(4):
                            m = pe.transpose(ps[:, e * BANK + n * P:e * BANK + (n + 1) * P], cp.kvp[:, n, e * 512 + 256:e * 512 + 384], cst["ident"])
                    m.then_inc(turned, 1)
                    for n in range(2):
                        pe.transpose(ps[:, 2 * BANK + n * P:2 * BANK + (n + 1) * P], wk[:, n, 0:P], cst["ident"])
                    pe.transpose(ps[:, 2 * BANK + 256:2 * BANK + 264], wn[:, 0:P], cst["ident"][0:8, 0:8])
                    pe.transpose(ps[:, 2 * BANK + 264:2 * BANK + 272], kn[:, 256:384], cst["ident"][0:8, 0:8]).then_inc(turned, 1)
                    pe.wait_ge(q_ready, 1)
                    for g in range(2):
                        ql = q[64 * g:64 * g + 64, :, :].rearrange("p r t -> p (r t)")
                        m = pe.matmul(ps[32 * g:32 * g + 32, 3 * BANK:3 * BANK + 64], ql, cp.kc[64 * g:64 * g + 64, :], start=True, stop=True)
                    m.then_inc(c_scored, 1)
                    pe.wait_ge(k_copied, 2)
                    for g in range(2):
                        ql = q[64 * g:64 * g + 64, :, :].rearrange("p r t -> p (r t)")
                        rows = slice(32 * g, 32 * g + 32)
                        for e in range(2):
                            pe.matmul(ps[rows, (4 + e) * BANK:(5 + e) * BANK], ql, ksT[64 * g:64 * g + 64, e, :], start=True, stop=True)
                        pe.matmul(ps[rows, 6 * BANK:6 * BANK + 8], ql, wT[64 * g:64 * g + 64, 264:272], start=True, stop=True)
                        m = pe.matmul(ps[rows, 7 * BANK:7 * BANK + 264], ql, wT[64 * g:64 * g + 64, 0:264], start=True, stop=True)
                    m.then_inc(s_scored, 1)
                    pe.wait_ge(c_ready, 1)
                    pe.transpose(ps[0:64, 2 * BANK:2 * BANK + 64], pc[:, :], cst["ident"][0:64, 0:64]).then_inc(c_turned, 1)
                    pe.wait_ge(imp_ready, 1)
                    pe.matmul(ps[0:64, 0:17], K["same"], im[:, :], start=True, stop=True).then_inc(imp_done, 1)
                    pe.wait_ge(c_copied, 1)
                    for g in range(2):
                        m = pe.matmul(ps[32 * g:32 * g + 32, 3 * BANK + 64:3 * BANK + 128], pcT[0:63, 32 * g:32 * g + 32], cp.vc[0:63, g, :], start=True, stop=True)
                    m.then_inc(c_out, 1)
                    pe.wait_ge(w_exp, 1)
                    for n in range(2):
                        pe.transpose(ps[:, BANK + n * 64:BANK + n * 64 + 64], sw[:, n * P:(n + 1) * P], cst["ident"][0:64, 0:64])
                    pe.transpose(ps[0:8, BANK + 128:BANK + 192], sw[:, 256:264], cst["ident"][0:64, 0:64]).then_inc(w_turned, 1)
                    pe.wait_ge(w_copied, 1)
                    for g in range(2):
                        oo = ps[32 * g:32 * g + 32, 7 * BANK:7 * BANK + 64]
                        for n in range(2):
                            pe.matmul(oo, pwT[:, n, 32 * g:32 * g + 32], wk[:, n, P + g * HD:P + (g + 1) * HD], start=(n == 0), stop=False)
                        m = pe.matmul(oo, pwT[0:8, 2, 32 * g:32 * g + 32], wn[:, P + g * HD:P + (g + 1) * HD], start=False, stop=True)
                    m.then_inc(w_out, 1)
                    pe.wait_ge(s_exp, 1)
                    for n in range(8):
                        pe.transpose(ps[:, n * 64:n * 64 + 64], s[:, n * P:(n + 1) * P], cst["ident"][0:64, 0:64])
                    pe.transpose(ps[0:8, BANK + 192:BANK + 256], s[:, 1024:1032], cst["ident"][0:64, 0:64]).then_inc(s_turned, 1)
                    pe.wait_ge(s_copied, 1)
                    for g in range(2):
                        oo = ps[32 * g:32 * g + 32, 4 * BANK:4 * BANK + 64]
                        for n in range(8):
                            e, pp = n // 4, n % 4
                            v = cp.kvp[:, pp, e * 512 + 384 + g * HD:e * 512 + 384 + (g + 1) * HD]
                            pe.matmul(oo, pT[:, n, 32 * g:32 * g + 32], v, start=(n == 0), stop=False)
                        m = pe.matmul(oo, pT[0:8, 8, 32 * g:32 * g + 32], kn[:, 384 + g * HD:384 + (g + 1) * HD], start=False, stop=True)
                    m.then_inc(s_out, 1)

                @block.scalar
                def _(act):
                    act.wait_ge(turned, 1)
                    act.copy(ksT[:, :, :], ps[:, 0:1024].rearrange("p (e n) -> p e n", e=2)).then_inc(k_copied, 1)
                    act.wait_ge(turned, 2)
                    act.copy(wT[:, :], ps[:, 2 * BANK:2 * BANK + 272]).then_inc(k_copied, 1)
                    act.wait_ge(c_masked, 1)
                    act.activation(pc[:, :], pc[:, :], ACT.Exp, bias=st[:, 1:2], scale=SCALE).then_inc(c_exp, 1)
                    act.wait_ge(c_turned, 1)
                    act.copy(pcT[:, :], ps[0:64, 2 * BANK:2 * BANK + 64]).then_inc(c_copied, 1)
                    act.wait_ge(w_masked, 1)
                    act.activation(sw[:, :], sw[:, :], ACT.Exp, bias=st[:, 5:6], scale=SCALE, accum_out=st[:, 6:7]).then_inc(w_exp, 1)
                    act.wait_ge(w_turned, 1)
                    act.copy(pwT[:, 0:2, :], ps[:, BANK:BANK + 128].rearrange("p (n t) -> p n t", n=2))
                    act.copy(pwT[0:8, 2, :], ps[0:8, BANK + 128:BANK + 192]).then_inc(w_copied, 1)
                    act.wait_ge(s_masked, 1)
                    act.activation(s[:, :], s[:, :], ACT.Exp, bias=st[:, 9:10], scale=SCALE, accum_out=st[:, 10:11]).then_inc(s_exp, 1)
                    act.wait_ge(s_turned, 1)
                    act.copy(pT[:, 0:8, :], ps[:, 0:512].rearrange("p (n t) -> p n t", n=8))
                    act.copy(pT[0:8, 8, :], ps[0:8, BANK + 192:BANK + 256]).then_inc(s_copied, 1)

                @block.vector
                def _(dve):
                    step = Chain(dve, chain_sem)
                    dve.tensor_copy(q[:, :, :], qT[:, :, ds(SEQ + b * NQ, NQ)]).then_inc(q_ready, 1)
                    dve.wait_ge(c_scored, 1)
                    step(dve.tensor_copy(pc[:, 0:63], ps[0:64, 3 * BANK:3 * BANK + 63]))
                    dve.memset(pc[:, 63:64], NEG)
                    step(dve.tensor_reduce(st[:, 0:1], pc[:, 0:63], AX.X, ALU.max))
                    step(dve.tensor_scalar(st[:, 1:2], st[:, 0:1], -SCALE, None, ALU.mult))
                    dve.sem_inc(c_masked, 1)
                    dve.wait_ge(c_exp, 1)
                    step(dve.tensor_reduce(st[:, 2:3], pc[:, 0:63], AX.X, ALU.add))
                    step(dve.reciprocal(st[:, 3:4], st[:, 2:3]))
                    step(dve.tensor_scalar(pc[:, :], pc[:, :], st[:, 3:4], None, ALU.mult))
                    dve.sem_inc(c_ready, 1)
                    step(dve.tensor_copy(pg[:, 1:65], pc[:, :]))
                    step(dve.tensor_reduce(im[:, :], pg[:, 1:69].rearrange("p (s c) -> p s c", c=4), AX.X, ALU.add))
                    step(dve.tensor_tensor(im[:, :], im[:, :], pg[:, 0:65:4], ALU.add))
                    dve.sem_inc(imp_ready, 1)
                    dve.wait_ge(s_scored, 1)
                    step(dve.tensor_tensor(sw[:, :], ps[0:64, 7 * BANK:7 * BANK + 264], K["swin"], ALU.add))
                    step(dve.tensor_reduce(st[:, 4:5], sw[:, :], AX.X, ALU.max))
                    step(dve.tensor_scalar(st[:, 5:6], st[:, 4:5], -SCALE, None, ALU.mult))
                    dve.sem_inc(w_masked, 1)
                    dve.wait_ge(imp_done, 1)
                    step(dve.tensor_tensor(im2[:, 0, :], ps[0:64, 0:17], K["skeep"], ALU.mult))
                    step(dve.tensor_tensor(im2[:, 0, :], im2[:, 0, :], K["sadd"], ALU.add))
                    step(block_ranks(dve, step, sel[:, :, :], im2, 64, 1, 17, K["low17"], gt, eq, rank))
                    for e in range(2):
                        dve.tensor_tensor(s[:, e * 512:(e + 1) * 512].rearrange("p (s t) -> p s t", s=16),
                                          ps[0:64, (4 + e) * BANK:(5 + e) * BANK].rearrange("p (s t) -> p s t", s=16),
                                          bc(sel[:, 0, 0:16], 32), ALU.add)
                    step(dve.scalar_tensor_tensor(out=s[:, 1024:1032], in0=ps[0:64, 6 * BANK:6 * BANK + 8], scalar=sel[:, 0, 16:17], in1=K["snew"], op0=ALU.add, op1=ALU.add))
                    step(dve.tensor_reduce(st[:, 8:9], s[:, :], AX.X, ALU.max))
                    step(dve.tensor_scalar(st[:, 9:10], st[:, 8:9], -SCALE, None, ALU.mult))
                    dve.sem_inc(s_masked, 1)
                    dve.wait_ge(w_exp, 1)
                    dve.reciprocal(st[:, 7:8], st[:, 6:7])
                    dve.wait_ge(s_exp, 1)
                    step(dve.reciprocal(st[:, 11:12], st[:, 10:11]))
                    step(dve.tensor_tensor(g3[:, :, :], g3[:, :, :], K["hsel"].rearrange("p (a b) -> p a b", a=1).to_broadcast([64, 3, 8]), ALU.mult))
                    step(dve.tensor_reduce(st[:, 12:15], g3[:, :, :], AX.X, ALU.add))
                    dve.tensor_tensor(st[:, 13:14], st[:, 13:14], st[:, 11:12], ALU.mult)
                    step(dve.tensor_tensor(st[:, 14:15], st[:, 14:15], st[:, 7:8], ALU.mult))
                    dve.wait_ge(c_out, 1)
                    step(dve.tensor_scalar(o[:, :], ps[0:64, 3 * BANK + 64:3 * BANK + 128], st[:, 12:13], None, ALU.mult))
                    dve.wait_ge(s_out, 1)
                    dve.wait_ge(w_out, 1)
                    step(dve.scalar_tensor_tensor(out=o[:, :], in0=ps[0:64, 4 * BANK:4 * BANK + 64], scalar=st[:, 13:14], in1=o[:, :], op0=ALU.mult, op1=ALU.add))
                    dve.scalar_tensor_tensor(out=o[:, :], in0=ps[0:64, 7 * BANK:7 * BANK + 64], scalar=st[:, 14:15], in1=o[:, :], op0=ALU.mult, op1=ALU.add).then_inc(out_ready, 1)


def prompt_compressed(nc, ps, cst, t, cp, qT, gate, mixT, selm, bufs, K):
    qt, s, sg, pT, m8, pgb, im, gt, eq, rank = bufs
    with stage(nc, "q_ready scored masked exped chain p_ready turned copied out_done") as (
            block, q_ready, scored, masked, exped, chain_sem, p_ready, turned, copied, out_done):
        sv = s[:, :].rearrange("p (h c) -> p h c", h=HH)

        @block.tensor
        def _(pe):
            pe.wait_ge(q_ready, 1)
            for h in range(HH):
                r, g = h // 2, h % 2
                b = 4 * g * BANK + r * 64
                m = pe.matmul(ps[:, b:b + 64], qt[64 * g:64 * g + 64, r, :], cp.kc[64 * g:64 * g + 64, :], start=True, stop=True)
            m.then_inc(scored, 1)
            pe.wait_ge(p_ready, 1)
            for h in range(HH):
                m = pe.transpose(ps[0:64, BANK + h * P:BANK + (h + 1) * P], sg[:, h * 64:(h + 1) * 64], cst["ident"])
            m.then_inc(turned, 1)
            pe.wait_ge(copied, 1)
            for g in range(2):
                m = pe.matmul(ps[:, (5 + g) * BANK:(6 + g) * BANK], cp.vc[:, :, :].rearrange("p g d -> p (g d)"), pT[:, g:HH:2, :], start=True, stop=True)
            m.then_inc(out_done, 1)

        @block.scalar
        def _(act):
            act.wait_ge(masked, 1)
            act.activation(s[:, :], s[:, :], ACT.Exp, scale=SCALE).then_inc(exped, 1)
            act.wait_ge(turned, 1)
            act.copy(pT[:, :, :], ps[0:64, BANK:3 * BANK].rearrange("p (h t) -> p h t", h=HH)).then_inc(copied, 1)
            act.wait_ge(out_done, 1)
            for g in range(2):
                hf = slice(64 * g, 64 * g + 64)
                act.copy(mixT[hf, 0:4, ds(t * P, P)], ps[hf, (5 + g) * BANK:(6 + g) * BANK].rearrange("p (r t) -> p r t", r=R4))

        @block.vector
        def _(dve):
            step = Chain(dve, chain_sem)
            dve.tensor_copy(qt[:, :, :], qT[:, :, ds(t * P, P)]).then_inc(q_ready, 1)
            dve.wait_ge(scored, 1)
            for g in range(2):
                m = dve.tensor_tensor(sv[:, g:HH:2], ps[:, 4 * g * BANK:4 * g * BANK + 256].rearrange("p (r c) -> p r c", r=R4),
                                      K["cadd"][:, ds(t * 64, 64)].unsqueeze(1).to_broadcast([P, R4, 64]), ALU.add)
            step(m)
            step(dve.tensor_reduce(m8[:, :], sv, AX.X, ALU.max))
            dve.tensor_tensor(sv, sv, bc(m8[:, :], 64), ALU.subtract).then_inc(masked, 1)
            dve.wait_ge(exped, 1)
            step(dve.tensor_tensor(sv, sv, K["cvalid"][:, ds(t * 64, 64)].unsqueeze(1).to_broadcast([P, HH, 64]), ALU.mult))
            step(dve.tensor_reduce(m8[:, :], sv, AX.X, ALU.add))
            step(dve.tensor_scalar(m8[:, :], m8[:, :], 1e-30, None, ALU.max))
            step(dve.reciprocal(m8[:, :], m8[:, :]))
            step(dve.tensor_tensor(sv, sv, bc(m8[:, :], 64), ALU.mult))
            dve.tensor_tensor(sg[:, :].rearrange("p (h c) -> p h c", h=HH), sv, bc(gate[:, ds(t * 24, 8)], 64), ALU.mult).then_inc(p_ready, 1)
            for g in range(2):
                m = dve.tensor_reduce(pgb[:, g, 1:65], s[:, :].rearrange("p (r g c) -> p g c r", r=R4, g=2)[:, g], AX.X, ALU.add)
            step(m)
            step(dve.tensor_reduce(im[:, :, :], pgb[:, :, 1:65].rearrange("p g (s c) -> p g s c", c=4), AX.X, ALU.add))
            step(dve.tensor_tensor(im[:, :, :], im[:, :, :], pgb[:, :, 0:61:4], ALU.add))
            step(dve.tensor_tensor(im[:, :, :], im[:, :, :], K["keep"][:, ds(t * 16, 16)].unsqueeze(1).to_broadcast([P, 2, 16]), ALU.mult))
            step(dve.tensor_tensor(im[:, :, :], im[:, :, :], K["add"][:, ds(t * 16, 16)].unsqueeze(1).to_broadcast([P, 2, 16]), ALU.add))
            block_ranks(dve, step, selm[:, ds(t, 1)].rearrange("p a g s -> p (a g) s"), im, P, 2, 16, K["low16"], gt, eq, rank)


def prompt_attention(nc, ps, cst, r, qT, ksT, kwT, vs, vw, gate, mixT, selm, bufs, K):
    qz, s, pT, st, gr = bufs
    jobs = [(t, g, br) for t in range(SEQ // P) for g in range(2) for br in range(2)]

    def keys(job):
        t, g, br = job
        first = max(0, t - 2) if br else 0
        return first, t + 1 - first

    with stage(nc, "q_ready scored added maxed exped normed turned copied out_done summed gates_in chain") as (
            block, q_ready, scored, added, maxed, exped, normed, turned, copied, out_done, summed, gates_in, chain_sem):
        @block.tensor
        def _(pe):
            pe.wait_ge(q_ready, 1)

            def scores(j):
                t, g, br = jobs[j]
                first, n = keys(jobs[j])
                if j >= 2:
                    pe.wait_ge(added, j - 1)
                kT = kwT if br else ksT
                for a in range(0, n * P, BANK):
                    w = min(BANK, n * P - a)
                    o = br * 2 * BANK + a
                    m = pe.matmul(ps[:, o:o + w], qz[:, g, t * P:(t + 1) * P],
                                  kT[:, first * P + a:first * P + a + w], start=True, stop=True)
                m.then_inc(scored, 1)

            def values(j):
                t, g, br = jobs[j]
                first, n = keys(jobs[j])
                pe.wait_ge(copied, j + 1)
                if g == 0 and br == 0 and t >= 2:
                    pe.wait_ge(summed, t - 1)
                v = vw if br else vs
                o = (6 + t % 2) * BANK + g * P
                for a in range(n):
                    m = pe.matmul(ps[:, o:o + P], v[:, (first + a) * P:(first + a + 1) * P], pT[:, j % 2, a, :],
                                  start=(a == 0 and br == 0), stop=(a == n - 1 and br == 1))
                m.then_inc(out_done, 1)

            scores(0)
            scores(1)
            for j, job in enumerate(jobs):
                first, n = keys(job)
                if j + 2 < len(jobs):
                    scores(j + 2)
                pe.wait_ge(normed, j + 1)
                if j:
                    pe.wait_ge(copied, j)
                for a in range(n):
                    m = pe.transpose(ps[:, 4 * BANK + a * P:4 * BANK + (a + 1) * P], s[:, j % 3, a * P:(a + 1) * P], cst["ident"])
                m.then_inc(turned, 1)
                if j:
                    values(j - 1)
            values(len(jobs) - 1)

        @block.scalar
        def _(act):
            def exp(j):
                w = keys(jobs[j])[1] * P
                act.wait_ge(maxed, j + 1)
                act.activation(s[:, j % 3, 0:w], s[:, j % 3, 0:w], ACT.Exp, bias=st[:, j % 3, 2:3], scale=SCALE,
                               accum_out=st[:, j % 3, 3:4]).then_inc(exped, 1)

            exp(0)
            for j, job in enumerate(jobs):
                if j + 1 < len(jobs):
                    exp(j + 1)
                w = keys(job)[1] * P
                act.wait_ge(turned, j + 1)
                if j >= 2:
                    act.wait_ge(out_done, j - 1)
                act.copy(pT[:, j % 2].rearrange("p a t -> p (a t)")[:, 0:w], ps[:, 4 * BANK:4 * BANK + w]).then_inc(copied, 1)

        @block.vector
        def _(dve):
            step = Chain(dve, chain_sem)
            dve.tensor_copy(gr[:, :, :, :], gate[:, 0:24 * 8].rearrange("p (t c r g) -> p t c r g", t=8, c=3, r=R4)[:, :, :, ds(r, 1), :].rearrange("p t c a g -> p t c (a g)")).then_inc(gates_in, 1)
            for g in range(2):
                hf = slice(64 * g, 64 * g + 64)
                m = dve.tensor_copy(qz[hf, g, :], qT[hf, ds(r, 1), 0:SEQ].rearrange("p a t -> p (a t)"))
            m.then_inc(q_ready, 1)
            dve.wait_ge(gates_in, 1)

            def mask(j):
                t, g, br = jobs[j]
                first, n = keys(jobs[j])
                dve.wait_ge(scored, j + 1)
                if j >= 3:
                    dve.wait_ge(turned, j - 2)
                a = br * 2 * BANK
                w = n * P
                sj, sm = s[:, j % 3, :], st[:, j % 3, :]
                if br:
                    dve.tensor_tensor_reduce(out=sj[:, 0:w], in0=ps[:, a:a + w], in1=K["band"][:, 384 - w:384], scale=1.0, scalar=-3e38,
                                             op0=ALU.add, op1=ALU.max, accum_out=sm[:, 0:1]).then_inc(added, 1)
                    dve.wait_ge(added, j + 1)
                    dve.tensor_scalar(sm[:, 2:3], sm[:, 0:1], -SCALE, None, ALU.mult).then_inc(maxed, 1)
                    return
                if n > 1:
                    dve.tensor_tensor_reduce(out=sj[:, 0:w - P].rearrange("p (s d) -> p s d", d=64), in0=ps[:, a:a + w - P].rearrange("p (s d) -> p s d", d=64),
                                             in1=bc(selm[:, t, g, 0:2 * t], 64), scale=1.0, scalar=-3e38,
                                             op0=ALU.add, op1=ALU.max, accum_out=sm[:, 0:1])
                dve.tensor_tensor_reduce(out=sj[:, w - P:w], in0=ps[:, a + w - P:a + w], in1=K["causal"], scale=1.0, scalar=-3e38,
                                         op0=ALU.add, op1=ALU.max, accum_out=sm[:, 1:2]).then_inc(added, 1)
                dve.wait_ge(added, j + 1)
                most = sm[:, 0:1] if n > 1 else sm[:, 1:2]
                dve.tensor_scalar(sm[:, 2:3], most, sm[:, 1:2], -SCALE, ALU.max, ALU.mult).then_inc(maxed, 1)

            def finish(t):
                dve.wait_ge(out_done, 4 * t + 4)
                for g in range(2):
                    hf = slice(64 * g, 64 * g + 64)
                    o = mixT[hf, ds(r, 1), t * P:(t + 1) * P].rearrange("p a t -> p (a t)")
                    b = (6 + t % 2) * BANK + g * P
                    m = dve.tensor_tensor(o, o, ps[hf, b:b + P], ALU.add)
                m.then_inc(summed, 1)

            mask(0)
            for j, job in enumerate(jobs):
                t, g, br = job
                w = keys(job)[1] * P
                if j + 1 < len(jobs):
                    mask(j + 1)
                dve.wait_ge(exped, j + 1)
                step(dve.reciprocal(st[:, j % 3, 4:5], st[:, j % 3, 3:4]))
                dve.tensor_scalar(s[:, j % 3, 0:w], s[:, j % 3, 0:w], st[:, j % 3, 4:5], gr[:, t, 1 + br, g:g + 1], ALU.mult, ALU.mult).then_inc(normed, 1)
                if j % 4 == 1 and t:
                    finish(t - 1)
            finish(SEQ // P - 1)


def sample_out(nc, ps, cst, os_d, mixT):
    with Scope(nc) as sc, stage(nc, "loaded turned kept") as (block, loaded, turned, kept):
        os_ = sc.sb("no_os", [NS, 512])

        @block.sync
        def _(sp):
            sp.dma_start(os_[:, :], os_d).then_inc(loaded, 16)

        @block.tensor
        def _(pe):
            pe.wait_ge(loaded, 16)
            for r in range(R4):
                m = pe.transpose(ps[:, r * NS:(r + 1) * NS], os_[:, r * P:(r + 1) * P], cst["ident"][0:NS, 0:NS])
            m.then_inc(turned, 1)

        @block.scalar
        def _(act):
            act.wait_ge(turned, 1)
            act.copy(mixT[:, 0:4, SEQ:NT], ps[:, 0:R4 * NS].rearrange("p (r t) -> p r t", r=R4)).then_inc(kept, 1)


FPART = 8


def residual_product(nc, ps, l, k0, kt, xh, xl, w_d, xres):
    with Scope(nc) as sc, stage(nc, "pool_hold w_hi w_ready w_in0 w_in1 x_in0 x_in1 products added banks_read stored0 stored1 sp_hold") as (
            block, pool_hold, w_hi, w_ready, w0, w1, x0, x1, products, added, banks_read, st0, st1, sp_hold):
        w_in, x_in, stored = (w0, w1), (x0, x1), (st0, st1)
        wt = sc.sb("rs_w", [P, 2, kt, P])
        wh = sc.sb("rs_wh", [P, 2, kt, P], F32R)
        wl = sc.sb("rs_wl", [P, 2, kt, P], F32R)
        xr = sc.sb("rs_x", [P, 2, NT])

        @block.sync
        def _(sp):
            def load_w(n, u):
                sp.dma_start(wt[:, u], w_d[l, n, :, k0:k0 + kt, :]).then_inc(w_in[u], 16)

            def load_x(n, u):
                sp.dma_start(xr[:, u, :], xres[n]).then_inc(x_in[u], 16)

            for u in range(2):
                load_w(u, u)
            for u in range(2):
                load_x(u, u)
            with sp.Fori(0, KD // 2 - 1) as i:
                for u in range(2):
                    sp.wait_ge(added, 2 * i + u + 1)
                    sp.sem_inc(sp_hold, 1)
                    sp.dma_start(xres[2 * i + u], xr[:, u, :]).then_inc(stored[u], 16)
                    load_w(2 * i + u + 2, u)
                    sp.wait_ge(stored[u], 16 * i + 16)
                    sp.sem_inc(sp_hold, 1)
                    load_x(2 * i + u + 2, u)
            for u in range(2):
                sp.wait_ge(added, KD - 1 + u)
                sp.dma_start(xres[KD - 2 + u], xr[:, u, :]).then_inc(stored[u], 16)
            for u in range(2):
                sp.wait_ge(stored[u], 16 * (KD // 2))

        @block.tensor
        def _(pe):
            with pe.Fori(0, KD // 2) as i:
                for u in range(2):
                    pe.wait_ge(banks_read, 2 * i + u + 1)
                    product3(pe, ps, 3 * u, wh[:, u], wl[:, u], xh, xl, kt, w_ready,
                             lambda c: kt // CHUNK * (2 * i + u) + c).then_inc(products, 1)

        @block.gpsimd
        def _(pool):
            with pool.Fori(0, KD // 2) as i:
                for u in range(2):
                    pool.wait_ge(w_in[u], 16 * i + 16)
                    pool.sem_inc(pool_hold, 1)
                    split_weights(pool, wt[:, u], wh[:, u], wl[:, u], kt, w_hi, w_ready, lambda c: kt // CHUNK * (2 * i + u) + c)

        @block.vector
        def _(dve):
            dve.sem_inc(banks_read, 2)
            with dve.Fori(0, KD // 2) as i:
                for u in range(2):
                    dve.wait_ge(x_in[u], 16 * i + 16)
                    dve.wait_ge(products, 2 * i + u + 1)
                    for n, (o, w) in enumerate(GROUPS):
                        b = (3 * u + n) * BANK
                        m = dve.tensor_tensor(xr[:, u, o:o + w], xr[:, u, o:o + w], ps[:, b:b + w], ALU.add)
                    m.then_inc(added, 1)
                    dve.wait_ge(added, 2 * i + u + 1)
                    dve.sem_inc(banks_read, 1)


def split_features(nc, hi, lo, x):
    with stage(nc, "hi_ready split") as (block, hi_ready, split):
        @block.scalar
        def _(act):
            for k in range(KD):
                act.copy(hi[:, k, :], x[:, k, :]).then_inc(hi_ready, 1)

        @block.vector
        def _(dve):
            for k in range(KD):
                dve.wait_ge(hi_ready, k + 1)
                dve.tensor_tensor(lo[:, k, :], x[:, k, :], f32(hi[:, k, :]), ALU.subtract).then_inc(split, 1)


def ffn_up(nc, ps, l, f0, nf, xh, xl, hh, hl, wg_d, wu_d, conv_d, cstate_d, conv_out):
    with Scope(nc) as sc, stage(nc, "pool_hold w_hi w_ready gate_used up_used h_hi h_split w_in0 w_in1 gate_done up_done gate_copied conv_done silu_done h_done ext_free gate_free h_free sent0 sent1 chain zeroed sp_hold") as (
            block, pool_hold, w_hi, w_ready, gate_used, up_used, h_hi, h_split, w0, w1, gate_done, up_done, gate_copied, conv_done, silu_done, h_done, ext_free, gate_free, h_free, sent0, sent1, chain_sem, zeroed, sp_hold):
        w_in, sent = (w0, w1), (sent0, sent1)
        wt = sc.sb("fu_w", [P, 2, 2, KD, P])
        wh = sc.sb("fu_wh", [P, 2, KD, P], F32R)
        wl = sc.sb("fu_wl", [P, 2, KD, P], F32R)
        steps = KD // CHUNK
        cw = sc.sb("fu_cw", [P, 2, 4])
        cst_ = sc.sb("fu_cst", [P, 2, NB, 2])
        ge = sc.sb("fu_ge", [P, SEQ + 2])
        gs = sc.sb("fu_gs", [P, NB, NQ + 2])
        c = sc.sb("fu_c", [P, NT])
        h = sc.sb("fu_h", [P, NT])
        co = sc.sb("fu_co", [P, 2, NB + 1, 2])

        @block.sync
        def _(sp):
            def load(f, u):
                sp.dma_start(wt[:, u, 0], wg_d[l, f]).then_inc(w_in[u], 16)
                sp.dma_start(wt[:, u, 1], wu_d[l, f]).then_inc(w_in[u], 16)
                sp.dma_start(cw[:, u, :], conv_d[l, f]).then_inc(w_in[u], 16)
                sp.dma_start(cst_[:, u], cstate_d[l, f]).then_inc(w_in[u], 16)

            def store(f, u):
                sp.dma_start(conv_out[l, f], co[:, u].rearrange("p b e -> p (b e)")).then_inc(sent[u], 16)

            sp.sem_inc(sent[0], 16)
            sp.sem_inc(sent[1], 16)
            load(f0, 0)
            load(f0 + 1, 1)
            with sp.Fori(0, nf // 2 - 1) as i:
                for u in range(2):
                    sp.wait_ge(conv_done, 2 * i + u + 1)
                    sp.sem_inc(sp_hold, 1)
                    store(f0 + 2 * i + u, u)
                    sp.wait_ge(up_done, 2 * i + u + 1)
                    sp.sem_inc(sp_hold, 1)
                    load(f0 + 2 * i + u + 2, u)
            for u in range(2):
                sp.wait_ge(conv_done, nf - 1 + u)
                store(f0 + nf - 2 + u, u)
            for u in range(2):
                sp.wait_ge(sent[u], 16 * (nf // 2 + 1))

        @block.tensor
        def _(pe):
            pe.sem_inc(gate_used, 1)
            pe.sem_inc(up_used, 1)
            with pe.Fori(0, nf // 2) as i:
                for u in range(2):
                    for half, (free, done, used) in enumerate(((gate_free, gate_done, gate_used), (h_free, up_done, up_used))):
                        pe.wait_ge(free, 2 * i + u + 1)
                        product3(pe, ps, 3 * half, wh[:, half], wl[:, half], xh, xl, KD, w_ready,
                                 lambda c: 2 * steps * (2 * i + u) + steps * half + c).then_inc(done, 1)
                        pe.wait_ge(done, 2 * i + u + 1)
                        pe.sem_inc(used, 1)

        @block.gpsimd
        def _(pool):
            with pool.Fori(0, nf // 2) as i:
                for u in range(2):
                    pool.wait_ge(w_in[u], 64 * i + 64)
                    pool.sem_inc(pool_hold, 1)
                    for half, used in enumerate((gate_used, up_used)):
                        pool.wait_ge(used, 2 * i + u + 1)
                        pool.sem_inc(pool_hold, 1)
                        split_weights(pool, wt[:, u, half], wh[:, half], wl[:, half], KD, w_hi, w_ready,
                                      lambda c: 2 * steps * (2 * i + u) + steps * half + c)

        @block.scalar
        def _(act):
            act.sem_inc(gate_free, 1)
            with act.Fori(0, nf // 2) as i:
                for u in range(2):
                    act.wait_ge(gate_done, 2 * i + u + 1)
                    act.wait_ge(ext_free, 2 * i + u + 1)
                    act.copy(ge[:, 2:386], ps[:, 0:384])
                    act.copy(ge[:, 386:770], ps[:, BANK:BANK + 384])
                    act.copy(ge[:, 770:1026], ps[:, 2 * BANK:2 * BANK + 256])
                    act.copy(gs[:, :, 2:NQ + 2], ps[:, 2 * BANK + 256:2 * BANK + 320].rearrange("p (b q) -> p b q", b=NB)).then_inc(gate_copied, 1)
                    act.wait_ge(gate_copied, 2 * i + u + 1)
                    act.sem_inc(gate_free, 1)
                    act.wait_ge(conv_done, 2 * i + u + 1)
                    act.activation(c[:, :], c[:, :], ACT.Silu).then_inc(silu_done, 1)
                    act.wait_ge(h_done, 2 * i + u + 1)
                    act.copy(hh[:, ds(2 * i + u, 1), :].rearrange("p a t -> p (a t)"), h[:, :]).then_inc(h_hi, 1)

        @block.vector
        def _(dve):
            dve.memset(ge[:, 0:2], 0.0).then_inc(zeroed, 1)
            dve.wait_ge(zeroed, 1)
            dve.sem_inc(ext_free, 1)
            dve.sem_inc(h_free, 1)
            csam = c[:, SEQ:NT].rearrange("p (b q) -> p b q", b=NB)
            with dve.Fori(0, nf // 2) as i:
                for u in range(2):
                    dve.wait_ge(w_in[u], 64 * i + 64)
                    dve.wait_ge(gate_copied, 2 * i + u + 1)
                    dve.wait_ge(sent[u], 16 * i + 16)
                    dve.tensor_copy(co[:, u, 0, :], ge[:, SEQ:SEQ + 2])
                    dve.tensor_copy(co[:, u, 1:NB + 1, :], gs[:, :, NQ:NQ + 2])
                    dve.tensor_copy(gs[:, :, 0:2], cst_[:, u]).then_inc(chain_sem, 1)
                    dve.wait_ge(chain_sem, 3 * (2 * i + u) + 1)
                    dve.tensor_scalar(c[:, 0:SEQ], ge[:, 0:SEQ], cw[:, u, 0:1], cw[:, u, 3:4], ALU.mult, ALU.add)
                    dve.tensor_scalar(csam, gs[:, :, 0:NQ], cw[:, u, 0:1], cw[:, u, 3:4], ALU.mult, ALU.add).then_inc(chain_sem, 1)
                    dve.wait_ge(chain_sem, 3 * (2 * i + u) + 2)
                    dve.scalar_tensor_tensor(out=c[:, 0:SEQ], in0=ge[:, 1:SEQ + 1], scalar=cw[:, u, 1:2], in1=c[:, 0:SEQ], op0=ALU.mult, op1=ALU.add)
                    dve.scalar_tensor_tensor(out=csam, in0=gs[:, :, 1:NQ + 1], scalar=cw[:, u, 1:2], in1=csam, op0=ALU.mult, op1=ALU.add).then_inc(chain_sem, 1)
                    dve.wait_ge(chain_sem, 3 * (2 * i + u) + 3)
                    dve.scalar_tensor_tensor(out=c[:, 0:SEQ], in0=ge[:, 2:SEQ + 2], scalar=cw[:, u, 2:3], in1=c[:, 0:SEQ], op0=ALU.mult, op1=ALU.add)
                    dve.scalar_tensor_tensor(out=csam, in0=gs[:, :, 2:NQ + 2], scalar=cw[:, u, 2:3], in1=csam, op0=ALU.mult, op1=ALU.add).then_inc(conv_done, 1)
                    dve.wait_ge(conv_done, 2 * i + u + 1)
                    dve.sem_inc(ext_free, 1)
                    dve.wait_ge(silu_done, 2 * i + u + 1)
                    dve.wait_ge(up_done, 2 * i + u + 1)
                    for n, (o, w) in enumerate(GROUPS):
                        m = dve.tensor_tensor(h[:, o:o + w], c[:, o:o + w], ps[:, (3 + n) * BANK:(3 + n) * BANK + w], ALU.mult)
                    m.then_inc(h_done, 1)
                    dve.wait_ge(h_done, 2 * i + u + 1)
                    dve.sem_inc(h_free, 1)
                    dve.wait_ge(h_hi, 2 * i + u + 1)
                    high, low = (a[:, ds(2 * i + u, 1), :].rearrange("p a t -> p (a t)") for a in (hh, hl))
                    dve.tensor_tensor(low, h[:, :], f32(high), ALU.subtract).then_inc(h_split, 1)


def trunk(nc, A, O, X, upto=99):
    with ExitStack() as top:
        pst = top.enter_context(nc.psum_tensor("ps", [P, 8 * BANK], F32))
        ps = pst[:, :]
        cbuf = top.enter_context(nc.sbuf_tensor("cbuf", [P, 3 * P], F32))
        ptab = top.enter_context(nc.sbuf_tensor("ptab", [1, NB * PAGES], I32))
        cst = {n: cbuf[:, i * P:(i + 1) * P] for i, n in enumerate(("ident", "ones", "blk"))}
        xres = X["xres"]
        with stage(nc, "loaded") as (block, loaded):
            @block.sync
            def _(sp):
                sp.dma_start(cbuf[:, :], A["const"][:, 0:3 * P]).then_inc(loaded, 16)
                sp.dma_start(ptab[:, :], A["page_table"]).then_inc(loaded, 16)
                for k in range(KD):
                    sp.dma_start(xres[k], A["xT"][k]).then_inc(loaded, 16)
                sp.wait_ge(loaded, 16 * (KD + 2))

        with nc.Fori(0, L_RUN) as l:
            with Scope(nc) as mixed:
                qT = mixed.sb("qT", [P, R4, NTP])
                ksT, kwT, vs, vw = (mixed.sb(n, [P, NTP]) for n in ("ksT", "kwT", "vs", "vw"))
                gate = mixed.sb("gate", [P, TT * 24])
                with Scope(nc) as sc:
                    xh = sc.sb("xh", [P, KD, NTP], F32R)
                    xl = sc.sb("xl", [P, KD, NTP], F32R)
                    with Scope(nc) as sn:
                        zero = sn.sb("zero", [P, NTP - NT])
                        with stage(nc, "zeroed padded") as (block, zeroed, padded):
                            @block.vector
                            def _(dve):
                                dve.memset(zero[:, :], 0.0).then_inc(zeroed, 1)
                                dve.wait_ge(zeroed, 1)
                                dve.tensor_copy(xh[:, :, NT:NTP], mid(zero[:, :], KD))
                                dve.tensor_copy(xl[:, :, NT:NTP], mid(zero[:, :], KD)).then_inc(padded, 1)
                        load_norm(nc, ps, cst, xres, A["norm_mix"][l], sn.sb("xn", [P, KD, NT]), hi=xh, lo=xl)
                    if upto < 2:
                        return
                    with Scope(nc) as sn:
                        w = sn.sb("wn", [P, KD, WN])
                        tmp = (sn.sb("np_xt", [P, KD, P]), sn.sb("np_kv", [P, 768]), sn.sb("np_q", [P, 512]), sn.sb("np_q2", [P, 512]),
                               sn.sb("np_tb", [P, 4, 256]), sn.sb("np_cs", [P, 64]))
                        with stage(nc, "loaded") as (block, loaded):
                            @block.sync
                            def _(sp):
                                for k in range(KD):
                                    sp.dma_start(w[:, k, :], A["w_nsa"][l, k]).then_inc(loaded, 16)
                                sp.wait_ge(loaded, 16 * KD)
                        with nc.Fori(0, TT) as t:
                            nsa_projection(nc, ps, cst, l, t, xh, xl, w, None, qT, ksT, kwT, vs, vw, gate, O["kvrows"], X["winr"], A["rope"], tmp)
                    if upto < 3:
                        return
                    rwkv_projection(nc, ps, cst, l, xh, xl, A["w_rw"], A["shift_in"], A["mu"][l], X["xmT"], O["shift"])
                if upto < 4:
                    return
                mixT = mixed.sb("mixT", [P, KD, NT])
                with Scope(nc) as sc:
                    wend = sc.sb("wend", [P, 4, NCH + NB])
                    rwkv_features(nc, ps, cst, l, X["xmT"], A["lora"][l], A["rvec"][l], X["arbk"], X["rk"], wend, A["const"])
                    if upto < 5:
                        return
                    rwkv_scan(nc, ps, cst, l, wend, A["const"], X["arbk"], X["xmT"], X["yr"], X["vr"], A["wkv_in"], O["wkv"])
                    if upto < 6:
                        return
                    rwkv_output(nc, ps, cst, l, mixT, X["xmT"], X["rk"], X["yr"], X["vr"], A["g_b"], A["gn"], A["rk8"])
                if upto < 7:
                    return
                with Scope(nc) as sc:
                    cp = Compressor(nc, sc)
                    with stage(nc, "stored") as (block, stored):
                        @block.sync
                        def _(sp):
                            sp.dma_start(O["win_p"][l], X["winr"][SEQ - 256:SEQ, :]).then_inc(stored, 16)
                            sp.dma_start(O["win_s"][l, :, 0:256 - NQ, :], A["state_win"][l, :, NQ:256, :]).then_inc(stored, 16)
                            sp.dma_start(O["win_s"][l, :, 256 - NQ:256, :], X["winr"][SEQ:NT, :].rearrange("(b q) n -> b q n", b=NB)).then_inc(stored, 16)
                            sp.dma_start(X["gs"], gate[0:NS, 24 * (TT - 1):24 * TT]).then_inc(stored, 16)
                            sp.wait_ge(stored, 64)
                    cp.weights(nc, ps, l, A["w1"], A["w2"], A["pe"])
                    sample_attention(nc, ps, cst, l, cp, qT, A["cache"], ptab, O["kvrows"], X["winr"], X["gs"], X["os"], A["state_win"], A["const"])
                    if upto < 8:
                        return

                    def prompt_rows(sp, sem):
                        for n in range(4):
                            sp.dma_start(cp.kvp[:, n, :], O["kvrows"][l, n * 256:(n + 1) * 256, :].rearrange("(p e) n -> p (e n)", e=2)).then_inc(sem, 16)
                        return 64

                    cp.run(nc, ps, cst, prompt_rows)
                    selm = sc.sb("selm", [P, 8, 2, 16])
                    names = ("cvalid", "cadd", "keep", "add", "causal", "band", "low16")
                    off, w = {}, 0
                    for n in names:
                        off[n] = w
                        w += CO[n][1]
                    km = sc.sb("km", [P, w])
                    K = {n: km[:, off[n]:off[n] + CO[n][1]] for n in names}
                    pgb = sc.sb("pc_pgb", [P, 2, 66])
                    with stage(nc, "loaded zeroed") as (block, loaded, zeroed):
                        @block.sync
                        def _(sp):
                            for n in names:
                                a, ww = CO[n]
                                sp.dma_start(km[:, off[n]:off[n] + ww], A["const"][:, a:a + ww]).then_inc(loaded, 16)
                            sp.wait_ge(loaded, 16 * len(names))

                        @block.vector
                        def _(dve):
                            dve.memset(pgb[:, :, :], 0.0).then_inc(zeroed, 1)
                    with Scope(nc) as s2:
                        bufs = (s2.sb("pc_qt", [P, R4, P]), s2.sb("pc_s", [P, 512]), s2.sb("pc_sg", [P, 512]), s2.sb("pc_pT", [64, HH, P]), s2.sb("pc_m8", [P, 8]), pgb,
                                s2.sb("pc_im", [P, 2, 16]), s2.sb("pc_gt", [P, 2, 16, 16]), s2.sb("pc_eq", [P, 2, 16, 16]), s2.sb("pc_rank", [P, 2, 16]))
                        with nc.Fori(0, SEQ // P) as t:
                            prompt_compressed(nc, ps, cst, t, cp, qT, gate, mixT, selm, bufs, K)
                    if upto < 9:
                        return
                    with Scope(nc) as s2:
                        bufs = (s2.sb("pa_qz", [P, 2, SEQ]), s2.sb("pa_s", [P, 3, SEQ]), s2.sb("pa_pT", [P, 2, 8, P]), s2.sb("pa_st", [P, 3, 5]), s2.sb("pa_gr", [P, 8, 3, 2]))
                        with stage(nc, "zeroed") as (block, zeroed):
                            @block.vector
                            def _(dve):
                                dve.memset(bufs[0][64:128, 0, :], 0.0)
                                dve.memset(bufs[0][0:64, 1, :], 0.0).then_inc(zeroed, 1)
                        with nc.Fori(0, R4) as r:
                            prompt_attention(nc, ps, cst, r, qT, ksT, kwT, vs, vw, gate, mixT, selm, bufs, K)
                    sample_out(nc, ps, cst, X["os"], mixT)
                if upto < 10:
                    return
                mixh = mixed.sb("mixh", [P, KD, NT], F32R)
                mixl = mixed.sb("mixl", [P, KD, NT], F32R)
                split_features(nc, mixh, mixl, mixT)
                residual_product(nc, ps, l, 0, KD, mixh, mixl, A["w_out"], xres)
            if upto < 11:
                return
            with Scope(nc) as sc:
                xh = sc.sb("xh2", [P, KD, NT], F32R)
                xl = sc.sb("xl2", [P, KD, NT], F32R)
                with Scope(nc) as sn:
                    load_norm(nc, ps, cst, xres, A["norm_ffn"][l], sn.sb("xn2", [P, KD, NT]), hi=xh, lo=xl)
                hh = sc.sb("hh", [P, FPART, NT], F32R)
                hl = sc.sb("hl", [P, FPART, NT], F32R)
                for f0 in range(0, FF, FPART):
                    nf = min(FPART, FF - f0)
                    ffn_up(nc, ps, l, f0, nf, xh, xl, hh, hl, A["w_gate"], A["w_up"], A["conv_w"], A["conv_in"], O["conv"])
                    residual_product(nc, ps, l, f0, nf, hh, hl, A["w_down"], xres)
        with Scope(nc) as sc:
            xf = sc.sb("xf", [P, KD, NT])
            load_norm(nc, ps, cst, xres, A["norm_final"], xf, store=O["yT"])


QPERM = np.arange(512).reshape(2, 4, 64).transpose(1, 0, 2).reshape(-1)
GPERM = np.arange(24).reshape(2, 4, 3).transpose(2, 1, 0).reshape(-1)
RPERM = np.concatenate([np.arange(0, 512), np.arange(576, 1088), np.arange(1088, 1600),
                        np.arange(512, 576), np.arange(1600, 1664), np.arange(1664, 1792)])

SPERM = np.arange(512).reshape(4, 2, 64).transpose(1, 0, 2).reshape(-1)


def tiles(v, n):
    return np.ascontiguousarray(v.reshape(v.shape[0], n, P).transpose(0, 2, 1))


def layout(i):
    c = np.ascontiguousarray
    a = {"const": constants(), "rope": rope_tables()}
    x = np.concatenate([i["x_prompt"].reshape(SEQ, D), i["x_sample"].reshape(NS, D)])
    a["xT"] = c(x.T.reshape(KD, P, NT))
    a["page_table"] = c(i["page_table"].reshape(1, NB * PAGES))
    a["cache"] = c(i["cache_kv"].reshape(L, NPHYS, 64, 1024))
    a["state_win"] = c(i["state_win"].reshape(L, NB, 256, 256))
    w = i["w_in"]
    nsa = np.concatenate([QPERM, np.arange(512, 1280), 1280 + GPERM])
    a["w_nsa"] = c(w[:, :, nsa].reshape(L, KD, P, WN))
    a["w_rw"] = c(w[:, :, 1304 + RPERM].reshape(L, KD, P, FR, P).transpose(0, 3, 2, 1, 4))
    a["mu"] = tiles(i["rw_mu"][:, RPERM], FR)
    a["shift_in"] = c(i["state_shift"][:, :, RPERM].reshape(L, NB, FR, P).transpose(0, 2, 3, 1))
    a["lora"] = c(np.concatenate([i["rw_w_b"], i["rw_a_b"]], 1))
    a["rvec"] = c(np.stack([tiles(i[n], 4) for n in ("rw_w0", "rw_a0", "rw_k_k", "rw_k_a")], 2))
    a["g_b"] = c(i["rw_g_b"][:, :, SPERM])
    a["gn"] = c(np.stack([i["rw_gn_w"], i["rw_gn_b"]], 1)[:, :, SPERM])
    rk8 = np.zeros((L, P, 4, 8), np.float32)
    for h in range(HH):
        rk8[:, 64 * (h % 2):64 * (h % 2) + 64, h // 2, h % 2 * 4 + h // 2] = i["rw_r_k"][:, h]
    a["rk8"] = rk8
    a["wkv_in"] = c(i["state_wkv"].reshape(L, NB, 4, 2, HD, HD).transpose(0, 3, 5, 2, 1, 4).reshape(L, P, 4, NB, HD))
    a["w1"] = c(i["cmp_w1"].reshape(L, 2, 16, P, 256).transpose(0, 1, 3, 2, 4))
    a["w2"] = c(i["cmp_w2"].reshape(L, 2, 2, P, HD).transpose(0, 1, 3, 2, 4))
    a["pe"] = c(i["cmp_pe"].reshape(L, 2, 16, P).transpose(0, 1, 3, 2))
    wo = i["w_out"][:, np.concatenate([QPERM, 512 + SPERM]), :]
    a["w_out"] = c(wo.reshape(L, KD, P, KD, P).transpose(0, 3, 2, 1, 4))
    for n, k in (("w_gate", "ffn_w_gate"), ("w_up", "ffn_w_up")):
        z = np.zeros((L, D, FF * P), np.float32)
        z[:, :, :2752] = i[k]
        a[n] = c(z.reshape(L, KD, P, FF, P).transpose(0, 3, 2, 1, 4))
    z = np.zeros((L, FF * P, D), np.float32)
    z[:, :2752] = i["ffn_w_down"]
    a["w_down"] = c(z.reshape(L, FF, P, KD, P).transpose(0, 3, 2, 1, 4))
    z = np.zeros((L, FF * P, 4), np.float32)
    z[:, :2752, 0:3] = i["ffn_conv_w"].transpose(0, 2, 1)
    z[:, :2752, 3] = i["ffn_conv_b"]
    a["conv_w"] = z.reshape(L, FF, P, 4)
    z = np.zeros((L, FF * P, NB, 2), np.float32)
    z[:, :2752] = i["state_conv"].transpose(0, 3, 1, 2)
    a["conv_in"] = z.reshape(L, FF, P, NB, 2)
    a["norm_mix"] = tiles(i["norm_mix"], KD)
    a["norm_ffn"] = tiles(i["norm_ffn"], KD)
    a["norm_final"] = tiles(i["norm_final"][None], KD)[0]
    return a


OUTS = {"yT": (KD, P, NT), "kvrows": (L, NTP, 512), "win_p": (L, 256, 256), "win_s": (L, NB, 256, 256),
        "wkv": (L, P, 4, NB + 1, HD), "shift": (L, FR, P, NB + 1), "conv": (L, FF, P, 2 * (NB + 1))}
SCRATCH = {"xres": (KD, P, NT), "winr": (NTP, 256), "xmT": (FR, P, NT), "arbk": (NCH + 1, P, 4, 4 * CH),
           "rk": (4, P, NT), "yr": (NT, 512), "vr": (NT, 512), "gs": (NS, 24), "os": (NS, 512)}


def build(nc, arrays, upto=99):
    A = {n: nc.dram_tensor(f"in_{n}", a.shape, mybir.dt.from_np(a.dtype), kind="ExternalInput").ap() for n, a in arrays.items()}
    O = {n: nc.dram_tensor(f"out_{n}", s, F32, kind="ExternalOutput").ap() for n, s in OUTS.items()}
    X = {n: nc.dram_tensor(f"scr_{n}", s, F32, kind="Internal").ap() for n, s in SCRATCH.items()}
    trunk(nc, A, O, X, upto)


def unlay(o):
    y = o["yT"].reshape(D, NT).T
    kv = o["kvrows"]
    rp = np.argsort(RPERM)
    wkv = o["wkv"].reshape(L, 2, HD, 4, NB + 1, HD).transpose(0, 4, 3, 1, 5, 2).reshape(L, NB + 1, HH, HD, HD)
    sh = o["shift"].reshape(L, FR * P, NB + 1)[:, rp].transpose(0, 2, 1)
    cv = o["conv"].reshape(L, FF * P, NB + 1, 2)[:, :2752].transpose(0, 2, 3, 1)
    c = np.ascontiguousarray
    return (c(y[:SEQ].reshape(1, SEQ, D)), c(y[SEQ:].reshape(NB, NQ, D)),
            c(kv[:, :SEQ].reshape(L, 1, SEQ, 4, 2, HD)), c(kv[:, SEQ:NT].reshape(L, NB, NQ, 4, 2, HD)),
            o["win_p"].reshape(L, 1, 256, 2, 2, HD), o["win_s"].reshape(L, NB, 256, 2, 2, HD),
            c(wkv[:, 0:1]), c(wkv[:, 1:]), c(sh[:, 0:1]), c(sh[:, 1:]), c(cv[:, 0:1]), c(cv[:, 1:]))


def kernel(**inputs):
    import concourse.bacc as bacc
    from concourse.bass_utils import run_bass_kernel_spmd as run

    arrays = layout({k: np.asarray(v) for k, v in inputs.items()})
    nc = bacc.Bacc("TRN2", target_bir_lowering=False, num_devices=1)
    build(nc, arrays)
    r = run(nc, [{f"in_{n}": a for n, a in arrays.items()}], core_ids=[0])
    return unlay({n: r.results[0][f"out_{n}"] for n in OUTS})
```

```python
from contextlib import ExitStack, contextmanager
import itertools
import math

import numpy as np
import concourse.bass as bass
from concourse import mybir

F32 = mybir.dt.float32
F32R = mybir.dt.float32r
I32 = mybir.dt.int32
ALU = mybir.AluOpType
ACT = mybir.ActivationFunctionType
AX = mybir.AxisListType

P = 128
D = 1024
KD = D // P
L = 2
SEQ = 1024
NB = 8
NQ = 8
NS = NB * NQ
NT = SEQ + NS
NTP = SEQ + P
TT = NTP // P
HD = 64
HH = 8
R4 = 4
WN = 1304
FR = 14
FF = 22
PAGES = 8
NPHYS = 80
CH = 64
NCH = SEQ // CH
SCALE = HD ** -0.5
NEG = -1e30
GROUPS = [(0, 384), (384, 384), (768, 320)]
BANK = 512
E05 = math.exp(-0.5)

_W = [("ident", P), ("ones", P), ("blk", P), ("gmask", P), ("gmask_s", P), ("lev", 6 * CH),
      ("restart", NT), ("cvalid", 8 * 64), ("cadd", 8 * 64), ("keep", 8 * 16), ("add", 8 * 16),
      ("causal", P), ("band", 384), ("low16", 256), ("low17", 289), ("swin", 264), ("snew", 8),
      ("skeep", 17), ("sadd", 17), ("hsel", 8), ("same", 64), ("seqt", NB * CH), ("seqp", NB)]
CO, _o = {}, 0
for _n, _w in _W:
    CO[_n] = (_o, _w)
    _o += _w
CW = _o


def constants():
    c = np.zeros((P, CW), np.float32)

    def put(name, a):
        o, w = CO[name]
        a = np.asarray(a, np.float32).reshape(a.shape[0], -1)
        c[:a.shape[0], o:o + w] = a

    p = np.arange(P)
    put("ident", np.eye(P))
    put("ones", np.ones((P, P)))
    put("blk", p[:, None] // 64 == p[None, :] // 64)
    s, t = p % 64, p % 64
    strict = np.concatenate([(s[:, None] < t[None, :64]), (s[:, None] <= t[None, :64])], 1)
    same = s[:, None] // NQ == (p % 64)[None, :] // NQ
    put("gmask", strict)
    put("gmask_s", strict & same)
    a = np.arange(CH)
    lev = []
    for n in range(6):
        w = 1 << n
        lev.append((a[None, :] // (2 * w) == a[:, None] // (2 * w)) & (a[None, :] // w % 2 == 1) & (a[:, None] // w % 2 == 0))
    put("lev", np.tile(np.stack(lev, 1), (2, 1, 1)))
    r = np.ones(NT)
    r[0:SEQ:CH] = 0
    r[SEQ::NQ] = 0
    put("restart", np.tile(r, (P, 1)))
    q = np.arange(8)[None, :, None] * P + p[:, None, None]
    cc = np.arange(64)[None, None, :]
    valid = (cc < 63) & (16 * cc + 31 <= q)
    put("cvalid", valid)
    put("cadd", np.where(valid, 0, NEG))
    b = np.arange(16)[None, None, :]
    cur = q // 64
    forced = (b == 0) | ((b <= cur) & (b > cur - 2))
    future = b * 64 > q
    put("keep", ~(forced | future))
    put("add", np.where(forced, 1e9, np.where(future, -1e9, 0)))
    put("causal", np.where(p[None, :] > p[:, None], NEG, 0))
    k = np.arange(384)[None, :] - 256
    put("band", np.where((k <= p[:, None]) & (k > p[:, None] - 256), 0, NEG))
    for n in (16, 17):
        i = np.arange(n)
        put(f"low{n}", np.tile((i[None, None, :] < i[None, :, None]), (P, 1, 1)))
    q = (np.arange(64) % NQ)[:, None]
    k = np.arange(264)[None, :]
    put("swin", np.where((k > q) & (k <= 256 + q), 0, NEG))
    put("snew", np.where(np.arange(8)[None, :] <= q, 0, NEG))
    b = np.arange(17)[None, :] + 0 * q
    f = (b == 0) | (b >= 15)
    put("skeep", ~f)
    put("sadd", np.where(f, 1e9, 0))
    i = np.arange(64)
    put("hsel", (2 * (i // 8 % 4) + i // 32)[:, None] == np.arange(8)[None, :])
    put("same", (i[:, None] // 32 == i[None, :] // 32) & (i[:, None] % 8 == i[None, :] % 8))
    put("seqt", np.tile((a[None, None, :] // NQ == np.arange(NB)[None, :, None]), (P, 1, 1)))
    put("seqp", (p % 64)[:, None] // NQ == np.arange(NB)[None, :])
    return c


def rope_tables():
    pos = np.arange(NTP)
    pos[SEQ:] = SEQ + (pos[SEQ:] - SEQ) % NQ
    inv = (np.float32(10000.0) ** (-np.arange(32, dtype=np.float32) / 32)).astype(np.float32)
    ang = pos.astype(np.float32)[:, None] * inv[None, :]
    return np.concatenate([np.cos(ang), np.sin(ang)], 1).astype(np.float32).reshape(TT, P, 64)


class Chain:

    def __init__(self, eng, sem):
        self.eng, self.sem, self.n = eng, sem, 0

    def __call__(self, ins):
        ins.then_inc(self.sem, 1)
        self.n += 1
        self.eng.wait_ge(self.sem, self.n)


def clear(sp, sems):
    nums = sorted(s.num for s in sems)
    first = nums[0]
    for n, after in zip(nums, nums[1:] + [None]):
        if after != n + 1:
            sp.sem_clear(range(first, n + 1))
            first = after


@contextmanager
def stage(nc, names, used=()):
    with ExitStack() as es:
        sems = [es.enter_context(nc.semaphore(n)) for n in names.split()]
        with nc.Block() as block:
            yield (block, *sems)
        clear(nc.sync, [*sems, *used])
        nc.all_engine_barrier()


_NUMBER = itertools.count()


class Scope(ExitStack):

    def __init__(self, nc):
        super().__init__()
        self.nc = nc

    def sb(self, name, shape, dt=F32):
        return self.enter_context(self.nc.sbuf_tensor(f"{name}_{next(_NUMBER)}", shape, dt))


def ds(start, size):
    return bass.ds(start, size)


def bc(ap, n):
    return ap.unsqueeze(len(ap.shape)).to_broadcast([*ap.shape, n])


def mid(ap, n):
    return ap.unsqueeze(1).to_broadcast([ap.shape[0], n, ap.shape[1]])


def f32(ap):
    return ap.bitcast(F32)



NSA_TILES = 3
CHUNK = 2


def split_weights(pool, w, hi, lo, kt, hi_ready, ready, count):
    for c in range(kt // CHUNK):
        k = slice(c * CHUNK, (c + 1) * CHUNK)
        pool.tensor_copy(hi[:, k, :], w[:, k, :]).then_inc(hi_ready, 1)
        pool.wait_ge(hi_ready, count(c) + 1)
        pool.tensor_tensor(lo[:, k, :], w[:, k, :], f32(hi[:, k, :]), ALU.subtract).then_inc(ready, 1)


def product3(pe, ps, bank, wh, wl, xh, xl, kt, ready, count):
    for k in range(kt):
        if k % CHUNK == 0:
            pe.wait_ge(ready, count(k // CHUNK) + 1)
        for j, (w, x) in enumerate(((wh, xh), (wh, xl), (wl, xh))):
            for n, (o, c) in enumerate(GROUPS):
                b = (bank + n) * BANK
                m = pe.matmul(ps[:, b:b + c], w[:, k, :], x[:, k, o:o + c], start=(k == 0 and j == 0), stop=(k == kt - 1 and j == 2))
    return m


def load_norm(nc, ps, cst, xres, gain, xn, store=None, hi=None, lo=None):
    with Scope(nc) as sc, stage(nc, "gain_in squared summed rooted root_chain scaled normed stored hi_ready split " + " ".join(f"x_in{k}" for k in range(KD))) as (
            block, gain_in, squared, summed, rooted, chain_sem, scaled, normed, stored, hi_ready, split, *x_in):
        sq = sc.sb("n_sq", [P, 2, NT])
        rs = sc.sb("n_rs", [P, NT])
        g = sc.sb("n_g", [P, KD])

        @block.sync
        def _(sp):
            for k in range(KD):
                sp.dma_start(xn[:, k, 0:NT], xres[k]).then_inc(x_in[k], 16)
            sp.dma_start(g[:, :], gain).then_inc(gain_in, 16)
            if store is not None:
                sp.wait_ge(normed, KD)
                for k in range(KD):
                    sp.dma_start(store[k], xn[:, k, 0:NT]).then_inc(stored, 16)
                sp.wait_ge(stored, 16 * KD)

        @block.scalar
        def _(act):
            for k in range(KD):
                act.wait_ge(x_in[k], 16)
                if k >= 2:
                    act.wait_ge(summed, k - 1)
                act.activation(sq[:, k % 2, :], xn[:, k, 0:NT], ACT.Square).then_inc(squared, 1)
            act.wait_ge(scaled, 1)
            act.activation(rs[:, :], rs[:, :], ACT.Sqrt).then_inc(rooted, 1)
            if hi is not None:
                for k in range(KD):
                    act.wait_ge(normed, k + 1)
                    act.copy(hi[:, k, 0:NT], xn[:, k, 0:NT]).then_inc(hi_ready, 1)

        @block.tensor
        def _(pe):
            for k in range(KD):
                pe.wait_ge(squared, k + 1)
                for n, (o, w) in enumerate(GROUPS):
                    m = pe.matmul(ps[:, n * BANK:n * BANK + w], cst["ones"], sq[:, k % 2, o:o + w],
                                  start=(k == 0), stop=(k == KD - 1))
                m.then_inc(summed, 1)

        @block.vector
        def _(dve):
            dve.wait_ge(summed, KD)
            for n, (o, w) in enumerate(GROUPS):
                m = dve.tensor_scalar(rs[:, o:o + w], ps[:, n * BANK:n * BANK + w], 1.0 / D, 1e-6, ALU.mult, ALU.add)
            m.then_inc(scaled, 1)
            dve.wait_ge(rooted, 1)
            dve.reciprocal(rs[:, :], rs[:, :]).then_inc(chain_sem, 1)
            dve.wait_ge(chain_sem, 1)
            dve.wait_ge(gain_in, 16)
            for k in range(KD + 1):
                if k < KD:
                    dve.scalar_tensor_tensor(out=xn[:, k, 0:NT], in0=xn[:, k, 0:NT], scalar=g[:, k:k + 1],
                                             in1=rs[:, :], op0=ALU.mult, op1=ALU.mult).then_inc(normed, 1)
                if hi is not None and k > 0:
                    dve.wait_ge(hi_ready, k)
                    dve.tensor_tensor(lo[:, k - 1, 0:NT], xn[:, k - 1, 0:NT], f32(hi[:, k - 1, 0:NT]), ALU.subtract).then_inc(split, 1)


def nsa_projection(nc, ps, cst, l, t0, xh, xl, w, qT, ksT, kwT, vs, vw, gate, kvrows, winr, rope_d, tmp):
    xt2, kv2, q_2, q2_2, tb, cs3 = tmp
    TS = range(NSA_TILES)
    with stage(nc, "cs_loaded x_copied proj copied chain rotated tiled turned kept stored0 stored1") as (
            block, cs_loaded, x_copied, proj, copied, chain_sem, rotated, tiled, turned, kept, stored0, stored1):
        stored = (stored0, stored1)

        @block.sync
        def _(sp):
            for j in TS:
                sp.dma_start(cs3[:, j, :], rope_d[t0 + j]).then_inc(cs_loaded, 16)
            for j in TS:
                kv = kv2[:, j % 2, :]
                sp.wait_ge(rotated, 4 * j + 2)
                sp.dma_start(kvrows[l, ds((t0 + j) * P, P), :], kv[:, 0:512]).then_inc(stored[j % 2], 16)
                sp.dma_start(winr[ds((t0 + j) * P, P), :], kv[:, 512:768]).then_inc(stored[j % 2], 16)
            for u in range(2):
                sp.wait_ge(stored[u], 32 * len(TS[u::2]))

        @block.tensor
        def _(pe):
            def turn(j):
                kv, q2 = kv2[:, j % 2, :], q2_2[:, j % 2, :]
                pe.wait_ge(rotated, 4 * j + 2)
                if j:
                    pe.wait_ge(kept, j)
                pe.transpose(ps[:, 4 * BANK:4 * BANK + P], kv[:, 256:384], cst["ident"])
                pe.transpose(ps[:, 4 * BANK + P:4 * BANK + 2 * P], kv[:, 512:640], cst["ident"]).then_inc(turned, 1)
                pe.wait_ge(rotated, 4 * j + 4)
                for r in range(R4):
                    m = pe.transpose(ps[:, 3 * BANK + r * P:3 * BANK + (r + 1) * P], q2[:, r * P:(r + 1) * P], cst["ident"])
                m.then_inc(turned, 1)

            for j in TS:
                pe.wait_ge(x_copied, j + 1)
                for n, (o, c) in enumerate([(512, 512), (1024, 280), (0, 512)]):
                    if j:
                        pe.wait_ge(copied, 3 * (j - 1) + n + 1)
                    for k in range(KD):
                        m = pe.matmul(ps[:, n * BANK:n * BANK + c], xt2[:, j % 2, k, :], w[:, k, o:o + c],
                                      start=(k == 0), stop=(k == KD - 1))
                    m.then_inc(proj, 1)
                    if j and n == 1:
                        turn(j - 1)
            turn(NSA_TILES - 1)

        @block.scalar
        def _(act):
            def keep(j):
                t = t0 + j
                act.wait_ge(turned, 2 * j + 1)
                act.copy(ksT[:, ds(t * P, P)], ps[:, 4 * BANK:4 * BANK + P])
                act.copy(kwT[:, ds(t * P, P)], ps[:, 4 * BANK + P:4 * BANK + 2 * P])
                act.wait_ge(turned, 2 * j + 2)
                act.copy(qT[:, :, ds(t * P, P)], ps[:, 3 * BANK:4 * BANK].rearrange("p (r t) -> p r t", r=R4)).then_inc(kept, 1)

            for j in TS:
                kv, q = kv2[:, j % 2, :], q_2[:, j % 2, :]
                act.wait_ge(proj, 3 * j + 1)
                if j >= 2:
                    act.wait_ge(tiled, j - 1)
                    act.wait_ge(kept, j - 1)
                    act.wait_ge(stored[j % 2], 32 * (j // 2))
                act.copy(kv[:, 0:512], ps[:, 0:512]).then_inc(copied, 1)
                act.wait_ge(proj, 3 * j + 2)
                act.activation(gate[:, ds((t0 + j) * 24, 24)], ps[:, BANK + 256:BANK + 280], ACT.Sigmoid)
                act.copy(kv[:, 512:768], ps[:, BANK:BANK + 256]).then_inc(copied, 1)
                if j:
                    keep(j - 1)
                act.wait_ge(proj, 3 * j + 3)
                act.copy(q[:, :], ps[:, 2 * BANK:3 * BANK]).then_inc(copied, 1)
            keep(NSA_TILES - 1)

        @block.vector
        def _(dve):
            step = Chain(dve, chain_sem)
            dve.wait_ge(cs_loaded, 16 * NSA_TILES)

            def take(j):
                t = t0 + j
                if j >= 2:
                    dve.wait_ge(proj, 3 * (j - 1))
                dve.tensor_tensor(xt2[:, j % 2], f32(xh[:, :, ds(t * P, P)]), f32(xl[:, :, ds(t * P, P)]), ALU.add).then_inc(x_copied, 1)

            take(0)
            take(1)
            for j in TS:
                t = t0 + j
                kv, q, q2, cs = kv2[:, j % 2, :], q_2[:, j % 2, :], q2_2[:, j % 2, :], cs3[:, j, :]

                def rotate(x1, x2, o1, o2, shape, tmps):
                    dims = list(shape)
                    cos, sin = cs[:, 0:32], cs[:, 32:64]
                    for d in dims[:-1]:
                        cos, sin = cos.unsqueeze(1), sin.unsqueeze(1)
                    cos, sin = cos.to_broadcast([P, *dims]), sin.to_broadcast([P, *dims])
                    ta, tc, td, te = tmps
                    dve.tensor_tensor(ta, x1, cos, ALU.mult)
                    dve.tensor_tensor(tc, x2, sin, ALU.mult)
                    dve.tensor_tensor(td, x2, cos, ALU.mult)
                    step(dve.tensor_tensor(te, x1, sin, ALU.mult))
                    dve.tensor_tensor(o1, ta, tc, ALU.subtract).then_inc(rotated, 1)
                    m = dve.tensor_tensor(o2, td, te, ALU.add)
                    m.then_inc(rotated, 1)

                dve.wait_ge(copied, 3 * j + 2)
                kh = kv.rearrange("p (a k g e d) -> p a k g e d", a=3, k=2, g=2, e=2)[:, :, 0]
                tk = [tb[:, n, 0:192].rearrange("p (a g d) -> p a g d", a=3, g=2) for n in range(4)]
                rotate(kh[:, :, :, 0, :], kh[:, :, :, 1, :], kh[:, :, :, 0, :], kh[:, :, :, 1, :], (3, 2, 32), tk)
                dve.tensor_copy(vs[:, ds(t * P, P)], kv[:, 384:512])
                dve.tensor_copy(vw[:, ds(t * P, P)], kv[:, 640:768])
                dve.wait_ge(copied, 3 * j + 3)
                dve.wait_ge(rotated, 4 * j + 2)
                if j >= 2:
                    dve.wait_ge(kept, j - 1)
                qh, q2h = (a.rearrange("p (h e d) -> p h e d", h=8, e=2) for a in (q, q2))
                tq = [tb[:, n, :].rearrange("p (h d) -> p h d", h=8) for n in range(4)]
                rotate(qh[:, :, 0, :], qh[:, :, 1, :], q2h[:, :, 0, :], q2h[:, :, 1, :], (8, 32), tq)
                dve.wait_ge(rotated, 4 * j + 4)
                dve.sem_inc(tiled, 1)
                if j + 2 < NSA_TILES:
                    take(j + 2)


def rwkv_projection(nc, ps, cst, l, xh, xl, w_rw, shift_in, mu_d, xmT, shift_out):
    with Scope(nc) as sc, stage(nc, "w_in0 w_in1 w_hi w_ready pool_hold s_in0 s_in1 mu_in done raw mixed raw_read sent0 sent1 chain zeroed sp_hold") as (
            block, w0, w1, w_hi, w_ready, pool_hold, s0, s1, mu_in, products, raw_ready, mixed, raw_read, sent0, sent1, chain_sem, zeroed, sp_hold):
        w_in, s_in, sent = (w0, w1), (s0, s1), (sent0, sent1)
        wt = sc.sb("rp_w", [P, 2, KD, P])
        wh = sc.sb("rp_wh", [P, 2, KD, P], F32R)
        wl = sc.sb("rp_wl", [P, 2, KD, P], F32R)
        raw = sc.sb("rp_raw", [P, 2, SEQ + 1])
        rsm = sc.sb("rp_rsm", [P, 2, NB, NQ + 1])
        shi = sc.sb("rp_shi", [P, 2, NB])
        xm = sc.sb("rp_xm", [P, 2, NT])
        sho = sc.sb("rp_sho", [P, 2, NB + 1])
        mu = sc.sb("rp_mu", [P, FR])
        muc = sc.sb("rp_muc", [P, 2])

        @block.sync
        def _(sp):
            def load(f, u):
                sp.dma_start(wt[:, u], w_rw[l, f]).then_inc(w_in[u], 16)
                sp.dma_start(shi[:, u, :], shift_in[l, f]).then_inc(s_in[u], 16)

            def store(f, u):
                sp.dma_start(xmT[f], xm[:, u, :]).then_inc(sent[u], 16)
                sp.dma_start(shift_out[l, f], sho[:, u, :]).then_inc(sent[u], 16)

            sp.sem_inc(sent[0], 32)
            sp.sem_inc(sent[1], 32)
            load(0, 0)
            load(1, 1)
            sp.dma_start(mu[:, :], mu_d).then_inc(mu_in, 16)
            with sp.Fori(0, FR // 2 - 1) as i:
                for u in range(2):
                    sp.wait_ge(mixed, 2 * i + u + 1)
                    sp.sem_inc(sp_hold, 1)
                    store(2 * i + u, u)
                    load(2 * i + u + 2, u)
            for u in range(2):
                sp.wait_ge(mixed, FR - 1 + u)
                store(FR - 2 + u, u)
            for u in range(2):
                sp.wait_ge(sent[u], 32 * (FR // 2 + 1))

        @block.gpsimd
        def _(pool):
            with pool.Fori(0, FR // 2) as i:
                for u in range(2):
                    pool.wait_ge(w_in[u], 16 * i + 16)
                    pool.sem_inc(pool_hold, 1)
                    split_weights(pool, wt[:, u], wh[:, u], wl[:, u], KD, w_hi, w_ready, lambda c: KD // CHUNK * (2 * i + u) + c)

        @block.tensor
        def _(pe):
            with pe.Fori(0, FR // 2) as i:
                for u in range(2):
                    pe.wait_ge(raw_ready, 2 * i + u + 1)
                    product3(pe, ps, 3 * u, wh[:, u], wl[:, u], xh, xl, KD, w_ready,
                             lambda c: KD // CHUNK * (2 * i + u) + c).then_inc(products, 1)

        @block.scalar
        def _(act):
            act.sem_inc(raw_ready, 2)
            with act.Fori(0, FR // 2) as i:
                for u in range(2):
                    act.wait_ge(products, 2 * i + u + 1)
                    act.wait_ge(raw_read, 2 * i + u + 1)
                    b = 3 * u * BANK
                    act.copy(raw[:, u, 1:385], ps[:, b:b + 384])
                    act.copy(raw[:, u, 385:769], ps[:, b + BANK:b + BANK + 384])
                    act.copy(raw[:, u, 769:1025], ps[:, b + 2 * BANK:b + 2 * BANK + 256])
                    act.copy(rsm[:, u, :, 1:NQ + 1],
                             ps[:, b + 2 * BANK + 256:b + 2 * BANK + 320].rearrange("p (b q) -> p b q", b=NB)).then_inc(raw_ready, 1)

        @block.vector
        def _(dve):
            dve.memset(raw[:, :, 0:1], 0.0).then_inc(zeroed, 1)
            dve.wait_ge(zeroed, 1)
            dve.sem_inc(raw_read, 2)
            dve.wait_ge(mu_in, 16)
            with dve.Fori(0, FR // 2) as i:
                for u in range(2):
                    dve.wait_ge(raw_ready, 2 * i + u + 3)
                    dve.wait_ge(s_in[u], 16 * i + 16)
                    dve.wait_ge(sent[u], 32 * i + 32)
                    dve.tensor_copy(rsm[:, u, :, 0], shi[:, u, :])
                    dve.tensor_copy(muc[:, u:u + 1], mu[:, ds(2 * i + u, 1)]).then_inc(chain_sem, 1)
                    dve.wait_ge(chain_sem, 2 * (2 * i + u) + 1)
                    dve.tensor_copy(sho[:, u, 0:1], raw[:, u, SEQ:SEQ + 1])
                    dve.tensor_copy(sho[:, u, 1:NB + 1], rsm[:, u, :, NQ])
                    xs = xm[:, u, SEQ:NT].rearrange("p (b q) -> p b q", b=NB)
                    dve.tensor_tensor(xm[:, u, 0:SEQ], raw[:, u, 0:SEQ], raw[:, u, 1:SEQ + 1], ALU.subtract)
                    dve.tensor_tensor(xs, rsm[:, u, :, 0:NQ], rsm[:, u, :, 1:NQ + 1], ALU.subtract).then_inc(chain_sem, 1)
                    dve.wait_ge(chain_sem, 2 * (2 * i + u) + 2)
                    dve.scalar_tensor_tensor(out=xm[:, u, 0:SEQ], in0=xm[:, u, 0:SEQ], scalar=muc[:, u:u + 1],
                                             in1=raw[:, u, 1:SEQ + 1], op0=ALU.mult, op1=ALU.add)
                    dve.scalar_tensor_tensor(out=xs, in0=xs, scalar=muc[:, u:u + 1], in1=rsm[:, u, :, 1:NQ + 1],
                                             op0=ALU.mult, op1=ALU.add).then_inc(mixed, 1)
                    dve.wait_ge(mixed, 2 * i + u + 1)
                    dve.sem_inc(raw_read, 1)


def rwkv_features(nc, ps, cst, l, xmT, lora_d, vec_d, arbk_d, rk_d, wend, const_d):
    with Scope(nc) as sc:
        wa = sc.sb("rf_wa", [P, NT])
        restart = sc.sb("rf_restart", [P, NT])
        vec = sc.sb("rf_vec", [P, 4, 4])
        vc = sc.sb("rf_vc", [P, 4])
        lora = sc.sb("rf_lora", [P, P])
        r, k, sw, a, ld, w, wp, wi, kk, t1 = (sc.sb(f"rf_{n}", [P, NT]) for n in
                                              ("r", "k", "sw", "a", "ld", "w", "wp", "wi", "kk", "t1"))
        rk = sc.sb("rf_rk", [P, NT])
        out = sc.sb("rf_out", [P, NCH + 1, 4, CH])
        kept = sc.enter_context(nc.semaphore("outputs_kept"))
        with stage(nc, "loaded tanned") as (block, loaded, tanned):
            @block.sync
            def _(sp):
                sp.sem_inc(kept, 32)
                sp.dma_start(wa[:, :], xmT[12]).then_inc(loaded, 16)
                sp.dma_start(vec[:, :, :], vec_d).then_inc(loaded, 16)
                sp.dma_start(restart[:, :], const_d[:, CO["restart"][0]:CO["restart"][0] + NT]).then_inc(loaded, 16)
                sp.wait_ge(loaded, 48)

            @block.scalar
            def _(act):
                act.wait_ge(loaded, 48)
                act.activation(wa[0:64, :], wa[0:64, :], ACT.Tanh).then_inc(tanned, 1)

        with nc.Fori(0, 4) as hp, stage(nc, "out_free r_in lora_in vec_ready z_done gates_ready chain cum_ready prev_ready decays sq_ready sq_done sum_ready rooted ready") as (
                block, out_free, r_in, lora_in, vec_ready, z_done, gates_ready, chain_sem, cum_ready, prev_ready, decays, sq_ready, sq_done, sum_ready, rooted, ready):

            @block.sync
            def _(sp):
                sp.dma_start(lora[:, :], lora_d[:, ds(hp * P, P)]).then_inc(lora_in, 16)
                sp.dma_start(r[:, :], xmT[hp]).then_inc(r_in, 16)
                sp.dma_start(k[:, :], xmT[hp + 4]).then_inc(r_in, 16)
                sp.wait_ge(kept, 32)
                sp.sem_clear(kept)
                sp.sem_inc(out_free, 1)
                sp.wait_ge(ready, 1)
                sp.dma_start(arbk_d[:, :, hp].rearrange("c p n -> p c n"), out[:, :, :, :].rearrange("p c a t -> p c (a t)")).then_inc(kept, 16)
                sp.dma_start(rk_d[hp], rk[:, :]).then_inc(kept, 16)

            @block.tensor
            def _(pe):
                pe.wait_ge(lora_in, 16)
                for half in range(2):
                    for n, (o, c) in enumerate(GROUPS):
                        b = (3 * half + n) * BANK
                        m = pe.matmul(ps[:, b:b + c], lora[64 * half:64 * half + 64, :], wa[64 * half:64 * half + 64, o:o + c], start=True, stop=True)
                    m.then_inc(z_done, 1)
                pe.wait_ge(sq_ready, 1)
                pe.wait_ge(gates_ready, 1)
                for n, (o, c) in enumerate(GROUPS):
                    m = pe.matmul(ps[:, n * BANK:n * BANK + c], cst["blk"], t1[:, o:o + c], start=True, stop=True)
                m.then_inc(sq_done, 1)

            @block.scalar
            def _(act):
                act.wait_ge(vec_ready, 1)
                for half, dst in enumerate((sw, a)):
                    act.wait_ge(z_done, half + 1)
                    for n, (o, c) in enumerate(GROUPS):
                        b = (3 * half + n) * BANK
                        m = act.activation(dst[:, o:o + c], ps[:, b:b + c], ACT.Sigmoid, bias=vc[:, half:half + 1])
                    m.then_inc(gates_ready, 1)
                act.wait_ge(cum_ready, 1)
                act.activation(w[:, :], wp[:, :], ACT.Exp)
                act.activation(wi[:, :], wp[:, :], ACT.Exp, scale=-1.0).then_inc(decays, 1)
                act.wait_ge(prev_ready, 1)
                act.activation(ld[:, :], ld[:, :], ACT.Exp).then_inc(decays, 1)
                act.wait_ge(sum_ready, 1)
                act.activation(t1[:, :], t1[:, :], ACT.Sqrt).then_inc(rooted, 1)

            @block.vector
            def _(dve):
                step = Chain(dve, chain_sem)
                for n in range(4):
                    m = dve.tensor_copy(vc[:, n:n + 1], vec[:, n, ds(hp, 1)])
                m.then_inc(vec_ready, 1)
                dve.wait_ge(vec_ready, 1)
                dve.wait_ge(r_in, 32)
                step(dve.tensor_scalar(kk[:, :], k[:, :], vc[:, 2:3], None, ALU.mult))
                dve.tensor_tensor(t1[:, :], kk[:, :], kk[:, :], ALU.mult).then_inc(sq_ready, 1)
                dve.wait_ge(gates_ready, 1)
                step(dve.tensor_scalar(ld[:, :], sw[:, :], -E05, None, ALU.mult))
                step(dve.tensor_tensor_scan(wp[:, :], restart[:, :], ld[:, :], 0.0, ALU.mult, ALU.add))
                dve.tensor_tensor(ld[:, :], wp[:, :], ld[:, :], ALU.subtract).then_inc(prev_ready, 1)
                dve.sem_inc(cum_ready, 1)
                dve.wait_ge(gates_ready, 2)
                step(dve.tensor_scalar(sw[:, :], a[:, :], 1.0, vc[:, 3:4], ALU.subtract, ALU.mult))
                step(dve.scalar_tensor_tensor(out=sw[:, :], in0=sw[:, :], scalar=1.0, in1=k[:, :], op0=ALU.add, op1=ALU.mult))
                dve.wait_ge(out_free, 1)
                dve.tensor_tensor(rk[:, :], r[:, :], sw[:, :], ALU.mult)
                dve.wait_ge(sq_done, 1)
                for n, (o, c) in enumerate(GROUPS):
                    m = dve.tensor_scalar(t1[:, o:o + c], ps[:, n * BANK:n * BANK + c], 1e-24, None, ALU.max)
                m.then_inc(sum_ready, 1)
                dve.wait_ge(rooted, 1)
                step(dve.reciprocal(t1[:, :], t1[:, :]))
                step(dve.tensor_tensor(kk[:, :], kk[:, :], t1[:, :], ALU.mult))
                dve.wait_ge(decays, 2)

                def parts(x):
                    return x[:, :].rearrange("p (c t) -> p c t", t=CH)

                step(dve.tensor_tensor(out[:, :, 1, :], parts(r), parts(w), ALU.mult))
                dve.scalar_tensor_tensor(out=out[:, :, 0, :], in0=parts(kk), scalar=-1.0, in1=parts(ld), op0=ALU.mult, op1=ALU.mult)
                for e in range(2):
                    hf = slice(64 * e, 64 * e + 64)
                    m = dve.tensor_tensor(out[hf, :, 3 - e, :], parts(sw)[hf], parts(wi)[hf], ALU.mult)
                step(m)
                step(dve.tensor_tensor(kk[:, :], kk[:, :], a[:, :], ALU.mult))
                for e in range(2):
                    hf = slice(64 * e, 64 * e + 64)
                    dve.tensor_tensor(out[hf, :, 2 + e, :], parts(kk)[hf], parts(wi)[hf], ALU.mult)
                dve.tensor_copy(wend[:, ds(hp, 1), 0:NCH], w[:, CH - 1:SEQ:CH].unsqueeze(1))
                dve.tensor_copy(wend[:, ds(hp, 1), NCH:NCH + NB], w[:, SEQ + NQ - 1:NT:NQ].unsqueeze(1)).then_inc(ready, 1)
        with stage(nc, "through", (kept,)) as (block, through):
            @block.sync
            def _(sp):
                sp.wait_ge(kept, 32)
                sp.sem_inc(through, 1)


def load_chunks(sp, cs, B, u, arbk_d, xmT, rows_in):
    for s in range(len(cs)):
        sp.dma_start(B["arbk"][:, u, s], arbk_d[cs[s]].rearrange("p h (a t) -> p h a t", a=4)).then_inc(rows_in[u], 16)
        sp.dma_start(B["vT"][:, u, s], xmT[8:12, :, ds(cs[s] * CH, CH)].rearrange("h p t -> p h t")).then_inc(rows_in[u], 16)


def rwkv_chunks(nc, ps, cst, cs, following, u, sample, B, wend, arbk_d, xmT, yr_d, vr_d, rows_in, kept, before):
    levels = 3 if sample else 6
    streams = range(len(cs))
    arbk, vT, G, AT, CT, XX, ys, p1, bkr, UV, yo, masks, S, AM, RM, S8, UVm = (B[n] for n in (
        "arbk", "vT", "G", "AT", "CT", "XX", "ys", "p1", "bkr", "UV", "yo", "masks", "S", "AM", "RM", "S8", "UVm"))
    arbk, vT = arbk[:, u], vT[:, u]
    HALF = (slice(0, 64), slice(64, 128))
    OTHER = (slice(64, 128), slice(0, 64))
    with stage(nc, "in0 in1 gram0 gram1 masked rows0 rows1 rows_copied started x_ready0 x_ready1 ct_ready0 ct_ready1 y_done0 y_done1 "
                   "y_copied0 y_copied1 z_done0 z_done1 x_done0 x_done1 am_ready p1_done p1_copied u_done u_copied st_done s_ready "
                   "out_done out_copied uvm_ready chain stored yo_free", (rows_in[u], kept[1 - u])) as (
            block, in0, in1, gram0, gram1, masked, rows0, rows1, rows_copied, started, xr0, xr1, ct0, ct1, yd0, yd1, yc0, yc1, zd0, zd1,
            xd0, xd1, am_ready, p1_done, p1_copied, u_done, u_copied, st_done, s_ready, out_done, out_copied, uvm_ready, chain_sem, stored, yo_free):
        in_, gram, rows, x_ready, ct_ready = (in0, in1), (gram0, gram1), (rows0, rows1), (xr0, xr1), (ct0, ct1)
        y_done, y_copied, z_done, x_done = (yd0, yd1), (yc0, yc1), (zd0, zd1), (xd0, xd1)

        @block.sync
        def _(sp):
            sp.wait_ge(rows_in[u], 32 * len(cs))
            for s in streams:
                sp.sem_inc(in_[s], 1)
            if following:
                load_chunks(sp, following, B, 1 - u, arbk_d, xmT, rows_in)
            for s in streams:
                sp.wait_ge(rows_copied, s + 1)
                for e in range(2):
                    sp.dma_start(vr_d[ds(cs[s] * CH, CH), 256 * e:256 * e + 256], UV[OTHER[e], s, e].rearrange("p h d -> p (h d)")).then_inc(stored, 16)
            sp.wait_ge(kept[1 - u], 32 * before)
            sp.sem_inc(yo_free, 1)
            for s in streams:
                sp.wait_ge(out_copied, s + 1)
                for e in range(2):
                    sp.dma_start(yr_d[ds(cs[s] * CH, CH), 256 * e:256 * e + 256], yo[HALF[e], s].rearrange("p h d -> p (h d)")).then_inc(kept[u], 16)
            sp.wait_ge(stored, 32 * len(cs))

        @block.tensor
        def _(pe):
            for s in streams:
                pe.wait_ge(in_[s], 1)
                for e in range(2):
                    for h in range(4):
                        bk = arbk[HALF[e], s, h, 2:4, :].rearrange("p a t -> p (a t)")
                        ar = arbk[HALF[e], s, h, 0:2, :].rearrange("p a t -> p (a t)")
                        o = (4 + 2 * s + e) * BANK + h * P
                        m = pe.matmul(ps[:, o:o + P], bk, ar, start=True, stop=True)
                m.then_inc(gram[s], 1)
                for h in range(4):
                    o = 2 * s * BANK + h * P
                    pe.transpose(ps[:, o:o + P], arbk[:, s, h, 2:4, :].rearrange("p a t -> p (a t)"), cst["ident"])
                for h in range(4):
                    for e in range(2):
                        o = (2 * s + 1) * BANK + e * 256 + h * 64
                        m = pe.matmul(ps[OTHER[e], o:o + 64], vT[:, s, h, :], cst["ident"][:, 64 * e:64 * e + 64], start=True, stop=True)
                m.then_inc(rows[s], 1)
            for n in range(levels):
                for s in streams:
                    pe.wait_ge(ct_ready[s], n + 1)
                    if n:
                        pe.wait_ge(x_done[s], n)
                    else:
                        pe.wait_ge(x_ready[s], 1)
                        pe.wait_ge(rows_copied, s + 1)
                    for h in range(4):
                        for e in range(2):
                            o = 2 * s * BANK + h * 64
                            m = pe.matmul(ps[HALF[e], o:o + 64], CT[HALF[e], s, h, :], XX[HALF[e], s, 0, h, :], start=True, stop=True)
                    m.then_inc(y_done[s], 1)
                for s in streams if n else ():
                    pe.wait_ge(y_copied[s], n)
                    for h in range(4):
                        for e in range(2):
                            o = (2 * s + 1) * BANK + h * 64
                            y, xt = ys[HALF[e], s, h, :], XX[HALF[e], s, 1, h, :]
                            if n < levels - 1:
                                pe.matmul(ps[HALF[e], o:o + 64], xt, y, start=True, stop=True)
                            m = pe.matmul(ps[HALF[e], o + 256:o + 320], y, xt, start=True, stop=True)
                    m.then_inc(z_done[s], 1)

            def with_state(bank, s, which, wide):
                for h in range(4):
                    for e in range(2):
                        o = ps[HALF[e], bank * BANK + h * 64:bank * BANK + (h + 1) * 64]
                        if sample:
                            for n in range(NB):
                                pe.matmul(o, wide[HALF[e], h, n, :], S8[HALF[e], h, n, :], start=(n == 0), stop=False)
                        else:
                            pe.matmul(o, arbk[HALF[e], s, h, which, :], S[HALF[e], s, h, :], start=True, stop=False)
                        m = pe.matmul(o, G[:, s, e, h, 64 * which:64 * which + 64], UV[:, s, e, h, :], start=False, stop=True)
                return m

            pe.wait_ge(masked, 2 * len(cs))
            if sample:
                pe.wait_ge(am_ready, 1)
            for s in streams:
                pe.wait_ge(started, 1)
                if s:
                    pe.wait_ge(s_ready, s)
                with_state(4, s, 0, AM).then_inc(p1_done, 1)
                pe.wait_ge(x_done[s], levels)
                pe.wait_ge(p1_copied, s + 1)
                for h in range(4):
                    for e in range(2):
                        m = pe.matmul(ps[HALF[e], 5 * BANK + h * 64:5 * BANK + (h + 1) * 64], XX[HALF[e], s, 1, h, :], p1[HALF[e], h, :], start=True, stop=True)
                m.then_inc(u_done, 1)
                pe.wait_ge(u_copied, s + 1)
                if sample:
                    pe.wait_ge(uvm_ready, 1)
                for h in range(4):
                    for e in range(2):
                        k = bkr[:, s, h, 64 * e:64 * e + 64]
                        if sample:
                            m = pe.matmul(ps[HALF[e], h * BANK:(h + 1) * BANK], k, UVm[:, :, e, h, :], start=True, stop=True)
                        else:
                            m = pe.matmul(ps[HALF[e], 7 * BANK + h * 64:7 * BANK + (h + 1) * 64], k, UV[:, s, e, h, :], start=True, stop=True)
                m.then_inc(st_done, 1)
                if s:
                    pe.wait_ge(out_copied, s)
                with_state(6, s, 1, RM).then_inc(out_done, 1)

        @block.scalar
        def _(act):
            for s in streams:
                act.wait_ge(rows[s], 1)
                act.copy(bkr[:, s, :, :], ps[:, 2 * s * BANK:(2 * s + 1) * BANK].rearrange("p (h t) -> p h t", h=4))
                for e in range(2):
                    o = (2 * s + 1) * BANK + e * 256
                    m = act.copy(UV[OTHER[e], s, e], ps[OTHER[e], o:o + 256].rearrange("p (h t) -> p h t", h=4))
                m.then_inc(rows_copied, 1)
            for n in range(1, levels):
                for s in streams:
                    act.wait_ge(y_done[s], n + 1)
                    if n > 1:
                        act.wait_ge(z_done[s], n - 1)
                    act.copy(ys[:, s], ps[:, 2 * s * BANK:2 * s * BANK + 256].rearrange("p (h t) -> p h t", h=4)).then_inc(y_copied[s], 1)
            for s in streams:
                act.wait_ge(p1_done, s + 1)
                if s:
                    act.wait_ge(u_done, s)
                act.copy(p1[:, :, :], ps[:, 4 * BANK:4 * BANK + 256].rearrange("p (h t) -> p h t", h=4)).then_inc(p1_copied, 1)
                act.wait_ge(u_done, s + 1)
                for e in range(2):
                    m = act.copy(UV[HALF[e], s, e], ps[HALF[e], 5 * BANK:5 * BANK + 256].rearrange("p (h t) -> p h t", h=4))
                m.then_inc(u_copied, 1)
                act.wait_ge(out_done, s + 1)
                if not s:
                    act.wait_ge(yo_free, 1)
                act.copy(yo[:, s], ps[:, 6 * BANK:6 * BANK + 256].rearrange("p (h t) -> p h t", h=4)).then_inc(out_copied, 1)

        @block.vector
        def _(dve):
            step = Chain(dve, chain_sem)
            for e in range(2):
                dve.memset(UV[HALF[e], 0:len(cs), e], 0.0)
            for s in streams:
                for j in range(2):
                    for e in range(2):
                        m = dve.tensor_copy(XX[HALF[e], s, j], mid(cst["ident"][HALF[e], 64 * e:64 * e + 64], 4))
                m.then_inc(x_ready[s], 1)
            dve.sem_inc(started, 1)
            for s in streams:
                dve.wait_ge(gram[s], 1)
                for e in range(2):
                    o = (4 + 2 * s + e) * BANK
                    dve.tensor_tensor(G[:, s, e], ps[:, o:o + BANK].rearrange("p (h t) -> p h t", h=4), mid(masks[:, 0:P], 4), ALU.mult).then_inc(masked, 1)
                dve.wait_ge(masked, 2 * s + 2)
                for e in range(2):
                    m = dve.tensor_copy(AT[HALF[e], s], G[HALF[e], s, e, :, 0:64])
                step(m)
            if sample:
                dve.wait_ge(in0, 1)
                for which, dst in ((0, AM), (1, RM)):
                    for h in range(4):
                        m = dve.tensor_tensor(dst[:, h], mid(arbk[:, 0, h, which, :], NB), masks[:, P + 384:P + 384 + 512].rearrange("p (b t) -> p b t", b=NB), ALU.mult)
                m.then_inc(am_ready, 1)
            for n in range(levels):
                for s in streams:
                    if n:
                        dve.wait_ge(y_done[s], n)
                        dve.wait_ge(x_done[s], 1)
                    dve.tensor_tensor(CT[:, s], AT[:, s], mid(masks[:, P + n * 64:P + (n + 1) * 64], 4), ALU.mult).then_inc(ct_ready[s], 1)
                for s in streams:
                    if n == 0:
                        dve.wait_ge(x_ready[s], 1)
                        dve.wait_ge(ct_ready[s], 1)
                        dve.wait_ge(y_done[s], 1)
                        dve.tensor_tensor(XX[:, s, 1], XX[:, s, 1], CT[:, s], ALU.add)
                        dve.tensor_tensor(XX[:, s, 0], XX[:, s, 0], ps[:, 2 * s * BANK:2 * s * BANK + 256].rearrange("p (h t) -> p h t", h=4), ALU.add).then_inc(x_done[s], 1)
                        continue
                    dve.wait_ge(z_done[s], n)
                    dve.wait_ge(x_done[s], n)
                    o = (2 * s + 1) * BANK
                    j = 0 if n < levels - 1 else 1
                    x = XX[:, s, j:].rearrange("p j h t -> p (j h t)")
                    dve.tensor_tensor(x, x, ps[:, o + 256 * j:o + BANK], ALU.add).then_inc(x_done[s], 1)
            if sample:
                dve.wait_ge(u_copied, 1)
                for n in range(NB):
                    a = P + 384 + 512 + n
                    m = dve.tensor_scalar(UVm[:, n].rearrange("p e h d -> p (e h d)"), UV[:, 0].rearrange("p e h d -> p (e h d)"), masks[:, a:a + 1], None, ALU.mult)
                m.then_inc(uvm_ready, 1)
                dve.wait_ge(st_done, 1)
                dve.wait_ge(out_done, 1)
                for h in range(4):
                    m = dve.tensor_tensor(S8[:, h], S8[:, h], ps[:, h * BANK:(h + 1) * BANK].rearrange("p (b t) -> p b t", b=NB), ALU.add)
                step(m)
                for h in range(4):
                    dve.tensor_tensor(S8[:, h], S8[:, h], bc(wend[:, h, NCH:NCH + NB], 64), ALU.mult)
            else:
                for s in streams:
                    dve.wait_ge(st_done, s + 1)
                    if s:
                        dve.wait_ge(out_done, s)
                    step(dve.tensor_tensor(S[:, 1 - s], S[:, s], ps[:, 7 * BANK:7 * BANK + 256].rearrange("p (h t) -> p h t", h=4), ALU.add))
                    dve.tensor_tensor(S[:, 1 - s], S[:, 1 - s], wend[:, :, ds(cs[s], 1)].to_broadcast([P, 4, 64]), ALU.mult).then_inc(s_ready, 1)
                    dve.wait_ge(s_ready, s + 1)


def rwkv_scan(nc, ps, cst, l, wend, const_d, arbk_d, xmT, yr_d, vr_d, s_in, s_out):
    with Scope(nc) as sc:
        shapes = {"arbk": [2, 2, 4, 4, CH], "vT": [2, 2, 4, CH], "G": [2, 2, 4, P], "AT": [2, 4, CH], "CT": [2, 4, CH], "XX": [2, 2, 4, CH],
                  "ys": [2, 4, CH], "p1": [4, 64], "bkr": [2, 4, P], "UV": [2, 2, 4, 64], "yo": [2, 4, 64], "masks": [P + 384 + 512 + NB],
                  "S": [2, 4, 64], "AM": [4, NB, CH], "RM": [4, NB, CH], "S8": [4, NB, 64], "UVm": [NB, 2, 4, 64]}
        B = {n: sc.sb(f"rc_{n}", [P, *s]) for n, s in shapes.items()}
        masks, S, S8 = B["masks"], B["S"], B["S8"]
        rows_in, kept = ([sc.enter_context(nc.semaphore(f"{n}{u}")) for u in range(2)] for n in ("rows_in", "y_kept"))
        with stage(nc, "loaded zeroed") as (block, loaded, zeroed):
            @block.sync
            def _(sp):
                load_chunks(sp, (0, 1), B, 0, arbk_d, xmT, rows_in)
                sp.sem_inc(kept[1], 64)
                o = 0
                for name in ("gmask", "lev", "seqt", "seqp"):
                    a, w = CO[name]
                    sp.dma_start(masks[:, o:o + w], const_d[:, a:a + w]).then_inc(loaded, 16)
                    o += w
                sp.dma_start(S8[:, :, :, :], s_in[l]).then_inc(loaded, 16)
                sp.wait_ge(loaded, 80)

            @block.vector
            def _(dve):
                dve.memset(S[:, 0], 0.0).then_inc(zeroed, 1)

        def pair(c, u, following):
            rwkv_chunks(nc, ps, cst, (2 * c, 2 * c + 1), following, u, False, B, wend, arbk_d, xmT, yr_d, vr_d, rows_in, kept, 2)

        with nc.Fori(0, NCH // 4 - 1) as c:
            for u in range(2):
                pair(2 * c + u, u, (4 * c + 2 * u + 2, 4 * c + 2 * u + 3))
        pair(NCH // 2 - 2, 0, (NCH - 2, NCH - 1))
        pair(NCH // 2 - 1, 1, (NCH,))
        with stage(nc, "loaded") as (block, loaded):
            @block.sync
            def _(sp):
                a, w = CO["gmask_s"]
                sp.dma_start(masks[:, 0:P], const_d[:, a:a + w]).then_inc(loaded, 16)
                sp.wait_ge(loaded, 16)
        rwkv_chunks(nc, ps, cst, (NCH,), None, 0, True, B, wend, arbk_d, xmT, yr_d, vr_d, rows_in, kept, 2)
        with stage(nc, "stored", (kept[0],)) as (block, stored):
            @block.sync
            def _(sp):
                sp.dma_start(s_out[l, :, :, 0], S[:, 0]).then_inc(stored, 16)
                sp.dma_start(s_out[l, :, :, 1:NB + 1], S8[:, :, :, :]).then_inc(stored, 16)
                sp.wait_ge(stored, 32)
                sp.wait_ge(kept[0], 32)


def rwkv_output(nc, ps, cst, l, mixT, xmT, rk_d, yr_d, vr_d, gb_d, gn_d, rk8_d):
    J = 4
    with Scope(nc) as sc:
        y, v, o = (sc.sb(f"ro_{n}", [P, J, 512]) for n in ("y", "v", "o"))
        rk = sc.sb("ro_rk", [P, 4, J * P])
        ga = sc.sb("ro_ga", [P, J * P])
        gb = sc.sb("ro_gb", [P, 512])
        gn = sc.sb("ro_gn", [P, 2, 512])
        rk8 = sc.sb("ro_rk8", [P, 4, 8])
        mean, var, bonus = (sc.sb(f"ro_{n}", [P, J, 8]) for n in ("mean", "var", "bonus"))
        with stage(nc, "loaded") as (block, loaded):
            @block.sync
            def _(sp):
                sp.dma_start(gb[:, :], gb_d[l]).then_inc(loaded, 16)
                for n in range(2):
                    sp.dma_start(gn[:, n], gn_d[l, n].partition_broadcast(P)).then_inc(loaded, 16)
                sp.dma_start(rk8[:, :, :], rk8_d[l]).then_inc(loaded, 16)
                sp.wait_ge(loaded, 64)

        def tiles(token, nt, m):
            with stage(nc, "y_in g_in sig g_done b_done bonus_ready bonused chain centred squared var_ready rooted ready turned kept") as (
                    block, y_in, g_in, sig, g_done, b_done, bonus_ready, bonused, chain_sem, centred, squared, var_ready, rooted, ready, turned, kept):
                tokens = ds(token, nt * m)

                def hv(x):
                    return x[0:m, 0:nt, :].rearrange("p j (h d) -> p (j h) d", h=HH)

                def per_head(x):
                    return x[0:m, 0:nt, :].rearrange("p j h -> p (j h)")

                @block.sync
                def _(sp):
                    sp.dma_start(y[0:m, 0:nt, :], yr_d[tokens, :].rearrange("(j p) n -> p j n", p=m)).then_inc(y_in, 16)
                    sp.dma_start(ga[:, 0:nt * m], xmT[13, :, tokens]).then_inc(g_in, 16)
                    sp.dma_start(rk[:, :, 0:nt * m], rk_d[:, :, tokens].rearrange("h p t -> p h t")).then_inc(g_in, 16)
                    sp.dma_start(v[0:m, 0:nt, :], vr_d[tokens, :].rearrange("(j p) n -> p j n", p=m)).then_inc(y_in, 16)

                @block.tensor
                def _(pe):
                    pe.wait_ge(g_in, 32)
                    for j in range(nt):
                        for hp in range(4):
                            mm = pe.matmul(ps[0:m, 4 * BANK + 8 * j:4 * BANK + 8 * j + 8], rk[:, hp, j * m:(j + 1) * m], rk8[:, hp, :], start=(hp == 0), stop=(hp == 3))
                    mm.then_inc(b_done, 1)
                    pe.wait_ge(sig, 1)
                    for j in range(nt):
                        mm = pe.matmul(ps[0:m, j * BANK:(j + 1) * BANK], ga[:, j * m:(j + 1) * m], gb[:, :], start=True, stop=True)
                    mm.then_inc(g_done, 1)
                    for j in range(nt):
                        pe.wait_ge(ready, j + 1)
                        for hp in range(4):
                            c = (4 + j) * BANK + hp * P
                            mm = pe.transpose(ps[:, c:c + m], o[0:m, j, hp * P:(hp + 1) * P], cst["ident"][0:m, 0:m])
                        mm.then_inc(turned, 1)

                @block.gpsimd
                def _(pool):
                    pool.wait_ge(y_in, 32)
                    pool.wait_ge(bonus_ready, 1)
                    pool.tensor_tensor(hv(v), hv(v), bc(per_head(bonus), HD), ALU.mult).then_inc(bonused, 1)

                @block.scalar
                def _(act):
                    act.wait_ge(g_in, 32)
                    act.activation(ga[:, 0:nt * m], ga[:, 0:nt * m], ACT.Sigmoid).then_inc(sig, 1)
                    act.wait_ge(b_done, 1)
                    act.copy(per_head(bonus), ps[0:m, 4 * BANK:4 * BANK + 8 * nt]).then_inc(bonus_ready, 1)
                    act.wait_ge(centred, 1)
                    act.activation(hv(o), hv(y), ACT.Square).then_inc(squared, 1)
                    act.wait_ge(var_ready, 1)
                    act.activation(per_head(var), per_head(var), ACT.Sqrt).then_inc(rooted, 1)
                    for j in range(nt):
                        act.wait_ge(turned, j + 1)
                        c = (4 + j) * BANK
                        act.copy(mixT[:, 4:8, ds(token + j * m, m)], ps[:, c:c + BANK].rearrange("p (h t) -> p h t", h=4)[:, :, 0:m]).then_inc(kept, 1)

                @block.vector
                def _(dve):
                    step = Chain(dve, chain_sem)
                    dve.wait_ge(y_in, 32)
                    step(dve.tensor_reduce(per_head(mean), hv(y), AX.X, ALU.add))
                    step(dve.tensor_scalar(per_head(mean), per_head(mean), 1.0 / HD, None, ALU.mult))
                    dve.tensor_tensor(hv(y), hv(y), bc(per_head(mean), HD), ALU.subtract).then_inc(centred, 1)
                    dve.wait_ge(squared, 1)
                    step(dve.tensor_reduce(per_head(var), hv(o), AX.X, ALU.add))
                    dve.tensor_scalar(per_head(var), per_head(var), 1.0 / HD, 64e-5, ALU.mult, ALU.add).then_inc(var_ready, 1)
                    dve.wait_ge(rooted, 1)
                    step(dve.reciprocal(per_head(var), per_head(var)))
                    step(dve.tensor_tensor(hv(y), hv(y), bc(per_head(var), HD), ALU.mult))
                    yj = y[0:m, 0:nt, :]
                    step(dve.tensor_tensor(yj, yj, mid(gn[0:m, 0, :], nt), ALU.mult))
                    step(dve.tensor_tensor(yj, yj, mid(gn[0:m, 1, :], nt), ALU.add))
                    dve.wait_ge(bonused, 1)
                    step(dve.tensor_tensor(yj, yj, v[0:m, 0:nt, :], ALU.add))
                    dve.wait_ge(g_done, 1)
                    for j in range(nt):
                        dve.tensor_tensor(o[0:m, j, :], y[0:m, j, :], ps[0:m, j * BANK:(j + 1) * BANK], ALU.mult).then_inc(ready, 1)

        with nc.Fori(0, SEQ // (J * P)) as t:
            tiles(t * J * P, J, P)
        tiles(SEQ, 1, NS)


def block_ranks(dve, step, sel, score, rows, g, nb, low, gt, eq, rank):
    a = score[0:rows].unsqueeze(2).to_broadcast([rows, g, nb, nb])
    b = bc(score[0:rows], nb)
    lo = low[0:rows].rearrange("p (s t) -> p s t", s=nb).unsqueeze(1).to_broadcast([rows, g, nb, nb])
    for n in range(g):
        dve.tensor_tensor(gt[0:rows, n], a[:, n], b[:, n], ALU.is_gt)
        m = dve.tensor_tensor(eq[0:rows, n], a[:, n], b[:, n], ALU.is_equal)
    step(m)
    for n in range(g):
        m = dve.tensor_tensor(eq[0:rows, n], eq[0:rows, n], lo[:, n], ALU.mult)
    step(m)
    step(dve.tensor_tensor(gt[0:rows], gt[0:rows], eq[0:rows], ALU.add))
    step(dve.tensor_reduce(rank[0:rows], gt[0:rows], AX.X, ALU.add))
    return dve.tensor_scalar(sel, rank[0:rows], 7.5, NEG, ALU.is_ge, ALU.mult)


class Compressor:

    def __init__(self, nc, sc):
        self.kvp = sc.sb("cp_kvp", [P, 2, 4, 1024])
        self.kvc = sc.sb("cp_kvc", [P, 4, 4, P])
        self.kt = sc.sb("cp_kt", [P, 4, 512])
        self.w1 = sc.sb("cp_w1", [P, 2, 16, 256])
        self.w2 = sc.sb("cp_w2", [P, 2, 2, HD])
        self.pe_ = sc.sb("cp_pe", [P, 2, 16])
        self.bias = sc.sb("cp_bias", [P, 4])
        self.hid = sc.sb("cp_hid", [P, 2, 2, 2, 64])
        self.kc = sc.sb("cp_kc", [P, 64])
        self.vc = sc.sb("cp_vc", [64, 2, HD])

    def weights(self, nc, ps, l, w1_d, w2_d, pe_d):
        with stage(nc, "loaded bias_done zeroed") as (block, loaded, bias_done, zeroed):
            @block.sync
            def _(sp):
                for n in range(2):
                    sp.dma_start(self.w1[:, n], w1_d[l, n]).then_inc(loaded, 16)
                    sp.dma_start(self.w2[:, n], w2_d[l, n]).then_inc(loaded, 16)
                    sp.dma_start(self.pe_[:, n], pe_d[l, n]).then_inc(loaded, 16)

            @block.tensor
            def _(pe):
                pe.wait_ge(loaded, 96)
                for n in range(4):
                    for q in range(16):
                        m = pe.matmul(ps[:, n:n + 1], self.w1[:, n // 2, q, (n % 2) * P:(n % 2 + 1) * P],
                                      self.pe_[:, n // 2, q:q + 1], start=(q == 0), stop=(q == 15))
                m.then_inc(bias_done, 1)

            @block.vector
            def _(dve):
                dve.memset(self.hid[:, :, :, :, :], 0.0).then_inc(zeroed, 1)
                dve.wait_ge(bias_done, 1)
                dve.tensor_copy(self.bias[:, :], ps[:, 0:4])
                dve.wait_ge(zeroed, 1)

    def run(self, nc, ps, cst, u, before, after=None, used=()):
        kvp = self.kvp[:, u]
        with stage(nc, "loaded sorted_ turned odd_copied even_copied hidden hid_ready c_done", used) as (
                block, loaded, sorted_, turned, odd_copied, even_copied, hidden, hid_ready, c_done):
            @block.sync
            def _(sp):
                before(sp)
                sp.sem_inc(loaded, 1)
                if after is not None:
                    after(sp)

            @block.tensor
            def _(pe):
                for kg in range(4):
                    pe.wait_ge(sorted_, 4)
                    for n in range(4):
                        m = pe.transpose(ps[:, kg * BANK + n * P:kg * BANK + (n + 1) * P], self.kvc[:, n, kg, :], cst["ident"])
                    m.then_inc(turned, 1)
                for kv in range(2):
                    pe.wait_ge(even_copied, kv + 1)
                    pe.wait_ge(odd_copied, kv + 1)
                    for half in range(2):
                        b = (4 + 2 * kv + half) * BANK
                        for q in range(16):
                            m = pe.matmul(ps[:, b:b + 126], self.w1[:, kv, q, half * P:(half + 1) * P],
                                          self.kt[:, 2 * kv:2 * kv + 2, q:q + 8 * 62 + 1:8], start=(q == 0), stop=(q == 15))
                        m.then_inc(hidden, 1)
                pe.wait_ge(hid_ready, 4)
                for g in range(2):
                    for half in range(2):
                        pe.matmul(ps[64 * g:64 * g + 64, 0:64], self.w2[:, 0, half, :], self.hid[:, 0, half, g, :], start=(half == 0), stop=(half == 1))
                for g in range(2):
                    for half in range(2):
                        m = pe.matmul(ps[0:64, BANK + g * 64:BANK + g * 64 + 64], self.hid[:, 1, half, g, :], self.w2[:, 1, half, :], start=(half == 0), stop=(half == 1))
                m.then_inc(c_done, 1)

            @block.vector
            def _(dve):
                dve.wait_ge(loaded, 1)
                for n in range(4):
                    dve.tensor_copy(self.kvc[:, n].rearrange("p kg (e d) -> p e kg d", e=2),
                                    kvp[:, n].rearrange("p (e a kg d) -> p e a kg d", e=2, a=2, kg=4)[:, :, 0]).then_inc(sorted_, 1)
                for kg in range(1, 4, 2):
                    dve.wait_ge(turned, kg + 1)
                    dve.tensor_copy(self.kt[:, kg, :], ps[:, kg * BANK:(kg + 1) * BANK]).then_inc(odd_copied, 1)
                dve.wait_ge(c_done, 1)
                dve.tensor_copy(self.kc[:, :], ps[:, 0:64])
                dve.tensor_copy(self.vc[:, :, :], ps[0:64, BANK:BANK + P].rearrange("p (g d) -> p g d", g=2))

            @block.scalar
            def _(act):
                for kg in range(0, 4, 2):
                    act.wait_ge(turned, kg + 1)
                    act.copy(self.kt[:, kg, :], ps[:, kg * BANK:(kg + 1) * BANK]).then_inc(even_copied, 1)
                for n in range(4):
                    act.wait_ge(hidden, n + 1)
                    b = (4 + n) * BANK
                    act.activation(self.hid[:, n // 2, n % 2, :, 0:63], ps[:, b:b + 126].rearrange("p (g c) -> p g c", g=2),
                                   ACT.Silu, bias=self.bias[:, n:n + 1]).then_inc(hid_ready, 1)


def sample_attention(nc, ps, cst, l, cp, qT, cache, ptab, kvrows, winr, gs_d, os_d, state_win, const_d):
    with Scope(nc) as sc:
        q = sc.sb("sa_q", [P, R4, NQ])
        wk2 = sc.sb("sa_wk", [P, 2, 2, 256])
        kn2 = sc.sb("sa_kn", [NQ, 2, 512])
        wn2 = sc.sb("sa_wn", [NQ, 2, 256])
        gates = sc.sb("sa_gates", [64, NB, 24])
        g3 = sc.sb("sa_g3", [64, 3, 8])
        ksT = sc.sb("sa_ksT", [P, 2, 512])
        wT = sc.sb("sa_wT", [P, 272])
        s = sc.sb("sa_s", [64, 1032])
        sw = sc.sb("sa_sw", [64, 264])
        pT = sc.sb("sa_pT", [P, 9, 64])
        pwT = sc.sb("sa_pwT", [P, 3, 64])
        pc = sc.sb("sa_pc", [64, 64])
        pcT = sc.sb("sa_pcT", [64, 64])
        pg = sc.sb("sa_pg", [64, 72])
        im = sc.sb("sa_im", [64, 17])
        im2 = sc.sb("sa_im2", [64, 1, 17])
        sel = sc.sb("sa_sel", [64, 1, 17])
        gt = sc.sb("sa_gt", [64, 1, 17, 17])
        eq = sc.sb("sa_eq", [64, 1, 17, 17])
        rank = sc.sb("sa_rank", [64, 1, 17])
        st = sc.sb("sa_st", [64, 16])
        o2 = sc.sb("sa_o", [64, 2, HD])
        names = ("low17", "swin", "snew", "skeep", "sadd", "hsel", "same")
        off, w = {}, 0
        for n in names:
            off[n] = w
            w += CO[n][1]
        cm = sc.sb("sa_cm", [64, w])
        K = {n: cm[:, off[n]:off[n] + CO[n][1]] for n in names}
        row_sems = [sc.enter_context(nc.semaphore(f"rows_in{u}")) for u in range(2)]
        kept = sc.enter_context(nc.semaphore("o_kept"))
        ROWS_IN = 16 * (PAGES + 3)

        def load_rows(sp, b, u):
            pages = [sp.value_load(ptab[0:1, ds(b * PAGES + p, 1)], min_val=0, max_val=NPHYS - 1) for p in range(PAGES)]
            for p, page in enumerate(pages):
                sp.dma_start(cp.kvp[64 * (p % 2):64 * (p % 2) + 64, u, p // 2, :], cache[l, page]).then_inc(row_sems[u], 16)
            sp.dma_start(wk2[:, u], state_win[l, b].rearrange("(h p) n -> p h n", p=P)).then_inc(row_sems[u], 16)
            sp.dma_start(kn2[:, u, :], kvrows[l, ds(SEQ + b * NQ, NQ), :]).then_inc(row_sems[u], 16)
            sp.dma_start(wn2[:, u, :], winr[ds(SEQ + b * NQ, NQ), :]).then_inc(row_sems[u], 16)

        with stage(nc, "loaded zeroed") as (block, loaded, zeroed):
            @block.sync
            def _(sp):
                load_rows(sp, 0, 0)
                sp.sem_inc(kept, 16)
                for n in names:
                    a, ww = CO[n]
                    sp.dma_start(cm[:, off[n]:off[n] + ww], const_d[0:64, a:a + ww]).then_inc(loaded, 16)
                for gr in range(8):
                    sp.dma_start(gates[gr * 8:gr * 8 + 8, :, :], gs_d.rearrange("(b q) n -> q b n", b=NB)).then_inc(loaded, 16)
                sp.wait_ge(loaded, 16 * (len(names) + 8))

            @block.vector
            def _(dve):
                dve.memset(pg[:, :], 0.0).then_inc(zeroed, 1)

        def sequence(b, u, more):
            wk, kn, wn, o, kvp = wk2[:, u], kn2[:, u], wn2[:, u], o2[:, u], cp.kvp[:, u]

            def rows_there(sp):
                sp.wait_ge(row_sems[u], ROWS_IN)
                sp.wait_ge(kept, 16)

            def next_rows(sp):
                load_rows(sp, b + 1, 1 - u)

            cp.run(nc, ps, cst, u, rows_there, next_rows if more else None, used=(row_sems[u], kept))
            with stage(nc, "q_ready turned k_copied c_scored s_scored w_scored c_masked c_exp c_ready c_turned c_copied c_out imp_ready imp_done s_masked s_exp s_turned s_copied s_out w_masked w_exp w_turned w_copied w_out chain out_ready") as (
                    block, q_ready, turned, k_copied, c_scored, s_scored, w_scored, c_masked, c_exp, c_ready, c_turned, c_copied, c_out, imp_ready, imp_done,
                    s_masked, s_exp, s_turned, s_copied, s_out, w_masked, w_exp, w_turned, w_copied, w_out, chain_sem, out_ready):
                @block.sync
                def _(sp):
                    sp.wait_ge(out_ready, 1)
                    sp.dma_start(os_d[b], o).then_inc(kept, 16)

                @block.tensor
                def _(pe):
                    for e in range(2):
                        for n in range(4):
                            m = pe.transpose(ps[:, e * BANK + n * P:e * BANK + (n + 1) * P], kvp[:, n, e * 512 + 256:e * 512 + 384], cst["ident"])
                    m.then_inc(turned, 1)
                    for n in range(2):
                        pe.transpose(ps[:, 2 * BANK + n * P:2 * BANK + (n + 1) * P], wk[:, n, 0:P], cst["ident"])
                    pe.transpose(ps[:, 2 * BANK + 256:2 * BANK + 264], wn[:, 0:P], cst["ident"][0:8, 0:8])
                    pe.transpose(ps[:, 2 * BANK + 264:2 * BANK + 272], kn[:, 256:384], cst["ident"][0:8, 0:8]).then_inc(turned, 1)
                    pe.wait_ge(q_ready, 1)
                    for g in range(2):
                        ql = q[64 * g:64 * g + 64, :, :].rearrange("p r t -> p (r t)")
                        m = pe.matmul(ps[32 * g:32 * g + 32, 3 * BANK:3 * BANK + 64], ql, cp.kc[64 * g:64 * g + 64, :], start=True, stop=True)
                    m.then_inc(c_scored, 1)
                    pe.wait_ge(k_copied, 2)
                    for g in range(2):
                        ql = q[64 * g:64 * g + 64, :, :].rearrange("p r t -> p (r t)")
                        rows = slice(32 * g, 32 * g + 32)
                        for e in range(2):
                            pe.matmul(ps[rows, (4 + e) * BANK:(5 + e) * BANK], ql, ksT[64 * g:64 * g + 64, e, :], start=True, stop=True)
                        pe.matmul(ps[rows, 6 * BANK:6 * BANK + 8], ql, wT[64 * g:64 * g + 64, 264:272], start=True, stop=True)
                        m = pe.matmul(ps[rows, 7 * BANK:7 * BANK + 264], ql, wT[64 * g:64 * g + 64, 0:264], start=True, stop=True)
                    m.then_inc(s_scored, 1)
                    pe.wait_ge(c_ready, 1)
                    pe.transpose(ps[0:64, 2 * BANK:2 * BANK + 64], pc[:, :], cst["ident"][0:64, 0:64]).then_inc(c_turned, 1)
                    pe.wait_ge(imp_ready, 1)
                    pe.matmul(ps[0:64, 0:17], K["same"], im[:, :], start=True, stop=True).then_inc(imp_done, 1)
                    pe.wait_ge(c_copied, 1)
                    for g in range(2):
                        m = pe.matmul(ps[32 * g:32 * g + 32, 3 * BANK + 64:3 * BANK + 128], pcT[0:63, 32 * g:32 * g + 32], cp.vc[0:63, g, :], start=True, stop=True)
                    m.then_inc(c_out, 1)
                    pe.wait_ge(w_exp, 1)
                    for n in range(2):
                        pe.transpose(ps[:, BANK + n * 64:BANK + n * 64 + 64], sw[:, n * P:(n + 1) * P], cst["ident"][0:64, 0:64])
                    pe.transpose(ps[0:8, BANK + 128:BANK + 192], sw[:, 256:264], cst["ident"][0:64, 0:64]).then_inc(w_turned, 1)
                    pe.wait_ge(w_copied, 1)
                    for g in range(2):
                        oo = ps[32 * g:32 * g + 32, 7 * BANK:7 * BANK + 64]
                        for n in range(2):
                            pe.matmul(oo, pwT[:, n, 32 * g:32 * g + 32], wk[:, n, P + g * HD:P + (g + 1) * HD], start=(n == 0), stop=False)
                        m = pe.matmul(oo, pwT[0:8, 2, 32 * g:32 * g + 32], wn[:, P + g * HD:P + (g + 1) * HD], start=False, stop=True)
                    m.then_inc(w_out, 1)
                    pe.wait_ge(s_exp, 1)
                    for n in range(8):
                        pe.transpose(ps[:, n * 64:n * 64 + 64], s[:, n * P:(n + 1) * P], cst["ident"][0:64, 0:64])
                    pe.transpose(ps[0:8, BANK + 192:BANK + 256], s[:, 1024:1032], cst["ident"][0:64, 0:64]).then_inc(s_turned, 1)
                    pe.wait_ge(s_copied, 1)
                    for g in range(2):
                        oo = ps[32 * g:32 * g + 32, 4 * BANK:4 * BANK + 64]
                        for n in range(8):
                            e, pp = n // 4, n % 4
                            v = kvp[:, pp, e * 512 + 384 + g * HD:e * 512 + 384 + (g + 1) * HD]
                            pe.matmul(oo, pT[:, n, 32 * g:32 * g + 32], v, start=(n == 0), stop=False)
                        m = pe.matmul(oo, pT[0:8, 8, 32 * g:32 * g + 32], kn[:, 384 + g * HD:384 + (g + 1) * HD], start=False, stop=True)
                    m.then_inc(s_out, 1)

                @block.scalar
                def _(act):
                    act.wait_ge(turned, 1)
                    act.copy(ksT[:, :, :], ps[:, 0:1024].rearrange("p (e n) -> p e n", e=2)).then_inc(k_copied, 1)
                    act.wait_ge(turned, 2)
                    act.copy(wT[:, :], ps[:, 2 * BANK:2 * BANK + 272]).then_inc(k_copied, 1)
                    act.wait_ge(c_masked, 1)
                    act.activation(pc[:, :], pc[:, :], ACT.Exp, bias=st[:, 1:2], scale=SCALE).then_inc(c_exp, 1)
                    act.wait_ge(c_turned, 1)
                    act.copy(pcT[:, :], ps[0:64, 2 * BANK:2 * BANK + 64]).then_inc(c_copied, 1)
                    act.wait_ge(w_masked, 1)
                    act.activation(sw[:, :], sw[:, :], ACT.Exp, bias=st[:, 5:6], scale=SCALE, accum_out=st[:, 6:7]).then_inc(w_exp, 1)
                    act.wait_ge(w_turned, 1)
                    act.copy(pwT[:, 0:2, :], ps[:, BANK:BANK + 128].rearrange("p (n t) -> p n t", n=2))
                    act.copy(pwT[0:8, 2, :], ps[0:8, BANK + 128:BANK + 192]).then_inc(w_copied, 1)
                    act.wait_ge(s_masked, 1)
                    act.activation(s[:, :], s[:, :], ACT.Exp, bias=st[:, 9:10], scale=SCALE, accum_out=st[:, 10:11]).then_inc(s_exp, 1)
                    act.wait_ge(s_turned, 1)
                    act.copy(pT[:, 0:8, :], ps[:, 0:512].rearrange("p (n t) -> p n t", n=8))
                    act.copy(pT[0:8, 8, :], ps[0:8, BANK + 192:BANK + 256]).then_inc(s_copied, 1)

                @block.vector
                def _(dve):
                    step = Chain(dve, chain_sem)
                    dve.tensor_copy(q[:, :, :], qT[:, :, ds(SEQ + b * NQ, NQ)]).then_inc(q_ready, 1)
                    step(dve.tensor_copy(g3[:, :, :], gates[:, ds(b, 1), :].rearrange("p a (c h) -> p (a c) h", c=3)))
                    dve.wait_ge(c_scored, 1)
                    step(dve.tensor_copy(pc[:, 0:63], ps[0:64, 3 * BANK:3 * BANK + 63]))
                    dve.memset(pc[:, 63:64], NEG)
                    step(dve.tensor_reduce(st[:, 0:1], pc[:, 0:63], AX.X, ALU.max))
                    step(dve.tensor_scalar(st[:, 1:2], st[:, 0:1], -SCALE, None, ALU.mult))
                    dve.sem_inc(c_masked, 1)
                    dve.wait_ge(c_exp, 1)
                    step(dve.tensor_reduce(st[:, 2:3], pc[:, 0:63], AX.X, ALU.add))
                    step(dve.reciprocal(st[:, 3:4], st[:, 2:3]))
                    step(dve.tensor_scalar(pc[:, :], pc[:, :], st[:, 3:4], None, ALU.mult))
                    dve.sem_inc(c_ready, 1)
                    step(dve.tensor_copy(pg[:, 1:65], pc[:, :]))
                    step(dve.tensor_reduce(im[:, :], pg[:, 1:69].rearrange("p (s c) -> p s c", c=4), AX.X, ALU.add))
                    step(dve.tensor_tensor(im[:, :], im[:, :], pg[:, 0:65:4], ALU.add))
                    dve.sem_inc(imp_ready, 1)
                    dve.wait_ge(s_scored, 1)
                    step(dve.tensor_tensor(sw[:, :], ps[0:64, 7 * BANK:7 * BANK + 264], K["swin"], ALU.add))
                    step(dve.tensor_reduce(st[:, 4:5], sw[:, :], AX.X, ALU.max))
                    step(dve.tensor_scalar(st[:, 5:6], st[:, 4:5], -SCALE, None, ALU.mult))
                    dve.sem_inc(w_masked, 1)
                    dve.wait_ge(imp_done, 1)
                    step(dve.tensor_tensor(im2[:, 0, :], ps[0:64, 0:17], K["skeep"], ALU.mult))
                    step(dve.tensor_tensor(im2[:, 0, :], im2[:, 0, :], K["sadd"], ALU.add))
                    step(block_ranks(dve, step, sel[:, :, :], im2, 64, 1, 17, K["low17"], gt, eq, rank))
                    for e in range(2):
                        dve.tensor_tensor(s[:, e * 512:(e + 1) * 512].rearrange("p (s t) -> p s t", s=16),
                                          ps[0:64, (4 + e) * BANK:(5 + e) * BANK].rearrange("p (s t) -> p s t", s=16),
                                          bc(sel[:, 0, 0:16], 32), ALU.add)
                    step(dve.scalar_tensor_tensor(out=s[:, 1024:1032], in0=ps[0:64, 6 * BANK:6 * BANK + 8], scalar=sel[:, 0, 16:17], in1=K["snew"], op0=ALU.add, op1=ALU.add))
                    step(dve.tensor_reduce(st[:, 8:9], s[:, :], AX.X, ALU.max))
                    step(dve.tensor_scalar(st[:, 9:10], st[:, 8:9], -SCALE, None, ALU.mult))
                    dve.sem_inc(s_masked, 1)
                    dve.wait_ge(w_exp, 1)
                    dve.reciprocal(st[:, 7:8], st[:, 6:7])
                    dve.wait_ge(s_exp, 1)
                    step(dve.reciprocal(st[:, 11:12], st[:, 10:11]))
                    step(dve.tensor_tensor(g3[:, :, :], g3[:, :, :], K["hsel"].rearrange("p (a b) -> p a b", a=1).to_broadcast([64, 3, 8]), ALU.mult))
                    step(dve.tensor_reduce(st[:, 12:15], g3[:, :, :], AX.X, ALU.add))
                    dve.tensor_tensor(st[:, 13:14], st[:, 13:14], st[:, 11:12], ALU.mult)
                    step(dve.tensor_tensor(st[:, 14:15], st[:, 14:15], st[:, 7:8], ALU.mult))
                    dve.wait_ge(c_out, 1)
                    step(dve.tensor_scalar(o, ps[0:64, 3 * BANK + 64:3 * BANK + 128], st[:, 12:13], None, ALU.mult))
                    dve.wait_ge(s_out, 1)
                    dve.wait_ge(w_out, 1)
                    step(dve.scalar_tensor_tensor(out=o, in0=ps[0:64, 4 * BANK:4 * BANK + 64], scalar=st[:, 13:14], in1=o, op0=ALU.mult, op1=ALU.add))
                    dve.scalar_tensor_tensor(out=o, in0=ps[0:64, 7 * BANK:7 * BANK + 64], scalar=st[:, 14:15], in1=o, op0=ALU.mult, op1=ALU.add).then_inc(out_ready, 1)

        with nc.Fori(0, NB // 2 - 1) as i:
            for u in range(2):
                sequence(2 * i + u, u, True)
        for u in range(2):
            sequence(NB - 2 + u, u, u == 0)
        with stage(nc, "through", used=(kept,)) as (block, through):
            @block.sync
            def _(sp):
                sp.wait_ge(kept, 16)
                sp.sem_inc(through, 1)


def prompt_compressed(nc, ps, cst, t, cp, qT, gate, mixT, selm, bufs, K):
    J = 2
    TURNED, OUT = (1, 6), ((3, 5), (0, 4))
    qt, s, sg, pT, m8, pgb, im, gt, eq, rank = bufs
    with stage(nc, "q_ready scored masked exped chain p_ready turned copied out_done") as (
            block, q_ready, scored, masked, exped, chain_sem, p_ready, turned, copied, out_done):
        sv = s[:, :, :].rearrange("p j (h c) -> p j h c", h=HH)

        @block.tensor
        def _(pe):
            pe.wait_ge(q_ready, 1)
            for j in range(J):
                for h in range(HH):
                    r, g = h // 2, h % 2
                    b = 4 * g * BANK + j * 256 + r * 64
                    m = pe.matmul(ps[:, b:b + 64], qt[64 * g:64 * g + 64, r, j * P:(j + 1) * P], cp.kc[64 * g:64 * g + 64, :], start=True, stop=True)
            m.then_inc(scored, 1)
            pe.wait_ge(p_ready, 1)
            for j in range(J):
                for h in range(HH):
                    c = TURNED[j] * BANK + h * P
                    m = pe.transpose(ps[0:64, c:c + P], sg[:, j, h * 64:(h + 1) * 64], cst["ident"])
                m.then_inc(turned, 1)
            for j in range(J):
                pe.wait_ge(copied, j + 1)
                for g in range(2):
                    c = OUT[j][g] * BANK
                    m = pe.matmul(ps[:, c:c + BANK], cp.vc[:, :, :].rearrange("p g d -> p (g d)"), pT[:, j, g:HH:2, :], start=True, stop=True)
                m.then_inc(out_done, 1)

        @block.scalar
        def _(act):
            act.wait_ge(masked, 1)
            act.activation(s[:, :, :], s[:, :, :], ACT.Exp, scale=SCALE).then_inc(exped, 1)
            for j in range(J):
                act.wait_ge(turned, j + 1)
                c = TURNED[j] * BANK
                act.copy(pT[:, j, :, :], ps[0:64, c:c + 2 * BANK].rearrange("p (h t) -> p h t", h=HH)).then_inc(copied, 1)
            for j in range(J):
                act.wait_ge(out_done, j + 1)
                for g in range(2):
                    hf, c = slice(64 * g, 64 * g + 64), OUT[j][g] * BANK
                    act.copy(mixT[hf, 0:4, ds((t + j) * P, P)], ps[hf, c:c + BANK].rearrange("p (r t) -> p r t", r=R4))

        @block.vector
        def _(dve):
            step = Chain(dve, chain_sem)

            def of_tiles(name, w, n):
                return K[name][:, ds(t * w, J * w)].rearrange("p (j c) -> p j c", j=J).unsqueeze(2).to_broadcast([P, J, n, w])

            dve.tensor_copy(qt[:, :, :], qT[:, :, ds(t * P, J * P)]).then_inc(q_ready, 1)
            dve.wait_ge(scored, 1)
            for g in range(2):
                m = dve.tensor_tensor(sv[:, :, g:HH:2], ps[:, 4 * g * BANK:(4 * g + 1) * BANK].rearrange("p (j r c) -> p j r c", j=J, r=R4),
                                      of_tiles("cadd", 64, R4), ALU.add)
            step(m)
            step(dve.tensor_reduce(m8[:, :, :], sv, AX.X, ALU.max))
            dve.tensor_tensor(sv, sv, bc(m8[:, :, :], 64), ALU.subtract).then_inc(masked, 1)
            dve.wait_ge(exped, 1)
            step(dve.tensor_tensor(sv, sv, of_tiles("cvalid", 64, HH), ALU.mult))
            step(dve.tensor_reduce(m8[:, :, :], sv, AX.X, ALU.add))
            step(dve.tensor_scalar(m8[:, :, :], m8[:, :, :], 1e-30, None, ALU.max))
            step(dve.reciprocal(m8[:, :, :], m8[:, :, :]))
            step(dve.tensor_tensor(sv, sv, bc(m8[:, :, :], 64), ALU.mult))
            gates = gate[:, ds(t * 24, J * 24)].rearrange("p (j c) -> p j c", j=J)[:, :, 0:8]
            dve.tensor_tensor(sg[:, :, :].rearrange("p j (h c) -> p j h c", h=HH), sv, bc(gates, 64), ALU.mult).then_inc(p_ready, 1)
            for g in range(2):
                m = dve.tensor_reduce(pgb[:, g:2 * J:2, 1:65], s[:, :, :].rearrange("p j (r g c) -> p g j c r", r=R4, g=2)[:, g], AX.X, ALU.add)
            step(m)
            step(dve.tensor_reduce(im[:, :, :], pgb[:, :, 1:65].rearrange("p g (s c) -> p g s c", c=4), AX.X, ALU.add))
            step(dve.tensor_tensor(im[:, :, :], im[:, :, :], pgb[:, :, 0:61:4], ALU.add))
            imj = im[:, :, :].rearrange("p (j g) s -> p j g s", j=J)
            step(dve.tensor_tensor(imj, imj, of_tiles("keep", 16, 2), ALU.mult))
            step(dve.tensor_tensor(imj, imj, of_tiles("add", 16, 2), ALU.add))
            block_ranks(dve, step, selm[:, ds(t, J)].rearrange("p a g s -> p (a g) s"), im, P, 2 * J, 16, K["low16"], gt, eq, rank)


def prompt_attention(nc, ps, cst, r, qT, ksT, kwT, vs, vw, gate, mixT, selm, bufs, K):
    qz, s, pT, st, gr = bufs
    jobs = [(t, g, br) for t in range(SEQ // P) for g in range(2) for br in range(2)]

    def keys(job):
        t, g, br = job
        first = max(0, t - 2) if br else 0
        return first, t + 1 - first

    with stage(nc, "q_ready scored added maxed exped normed turned copied out_done summed gates_in chain") as (
            block, q_ready, scored, added, maxed, exped, normed, turned, copied, out_done, summed, gates_in, chain_sem):
        @block.tensor
        def _(pe):
            pe.wait_ge(q_ready, 1)

            def scores(j):
                t, g, br = jobs[j]
                first, n = keys(jobs[j])
                if j >= 2:
                    pe.wait_ge(added, j - 1)
                kT = kwT if br else ksT
                for a in range(0, n * P, BANK):
                    w = min(BANK, n * P - a)
                    o = br * 2 * BANK + a
                    m = pe.matmul(ps[:, o:o + w], qz[:, g, t * P:(t + 1) * P],
                                  kT[:, first * P + a:first * P + a + w], start=True, stop=True)
                m.then_inc(scored, 1)

            def values(j):
                t, g, br = jobs[j]
                first, n = keys(jobs[j])
                pe.wait_ge(copied, j + 1)
                if g == 0 and br == 0 and t >= 2:
                    pe.wait_ge(summed, t - 1)
                v = vw if br else vs
                o = (6 + t % 2) * BANK + g * P
                for a in range(n):
                    m = pe.matmul(ps[:, o:o + P], v[:, (first + a) * P:(first + a + 1) * P], pT[:, j % 2, a, :],
                                  start=(a == 0 and br == 0), stop=(a == n - 1 and br == 1))
                m.then_inc(out_done, 1)

            scores(0)
            scores(1)
            for j, job in enumerate(jobs):
                first, n = keys(job)
                if j + 2 < len(jobs):
                    scores(j + 2)
                pe.wait_ge(normed, j + 1)
                if j:
                    pe.wait_ge(copied, j)
                for a in range(n):
                    m = pe.transpose(ps[:, 4 * BANK + a * P:4 * BANK + (a + 1) * P], s[:, j % 3, a * P:(a + 1) * P], cst["ident"])
                m.then_inc(turned, 1)
                if j:
                    values(j - 1)
            values(len(jobs) - 1)

        @block.scalar
        def _(act):
            def exp(j):
                w = keys(jobs[j])[1] * P
                act.wait_ge(maxed, j + 1)
                act.activation(s[:, j % 3, 0:w], s[:, j % 3, 0:w], ACT.Exp, bias=st[:, j % 3, 2:3], scale=SCALE,
                               accum_out=st[:, j % 3, 3:4]).then_inc(exped, 1)

            exp(0)
            for j, job in enumerate(jobs):
                if j + 1 < len(jobs):
                    exp(j + 1)
                w = keys(job)[1] * P
                act.wait_ge(turned, j + 1)
                if j >= 2:
                    act.wait_ge(out_done, j - 1)
                act.copy(pT[:, j % 2].rearrange("p a t -> p (a t)")[:, 0:w], ps[:, 4 * BANK:4 * BANK + w]).then_inc(copied, 1)

        @block.vector
        def _(dve):
            step = Chain(dve, chain_sem)
            dve.tensor_copy(gr[:, :, :, :], gate[:, 0:24 * 8].rearrange("p (t c r g) -> p t c r g", t=8, c=3, r=R4)[:, :, :, ds(r, 1), :].rearrange("p t c a g -> p t c (a g)")).then_inc(gates_in, 1)
            for g in range(2):
                hf = slice(64 * g, 64 * g + 64)
                m = dve.tensor_copy(qz[hf, g, :], qT[hf, ds(r, 1), 0:SEQ].rearrange("p a t -> p (a t)"))
            m.then_inc(q_ready, 1)
            dve.wait_ge(gates_in, 1)

            def mask(j):
                t, g, br = jobs[j]
                first, n = keys(jobs[j])
                dve.wait_ge(scored, j + 1)
                if j >= 3:
                    dve.wait_ge(turned, j - 2)
                a = br * 2 * BANK
                w = n * P
                sj, sm = s[:, j % 3, :], st[:, j % 3, :]
                if br:
                    dve.tensor_tensor_reduce(out=sj[:, 0:w], in0=ps[:, a:a + w], in1=K["band"][:, 384 - w:384], scale=1.0, scalar=-3e38,
                                             op0=ALU.add, op1=ALU.max, accum_out=sm[:, 0:1]).then_inc(added, 1)
                    dve.wait_ge(added, j + 1)
                    dve.tensor_scalar(sm[:, 2:3], sm[:, 0:1], -SCALE, None, ALU.mult).then_inc(maxed, 1)
                    return
                if n > 1:
                    dve.tensor_tensor_reduce(out=sj[:, 0:w - P].rearrange("p (s d) -> p s d", d=64), in0=ps[:, a:a + w - P].rearrange("p (s d) -> p s d", d=64),
                                             in1=bc(selm[:, t, g, 0:2 * t], 64), scale=1.0, scalar=-3e38,
                                             op0=ALU.add, op1=ALU.max, accum_out=sm[:, 0:1])
                dve.tensor_tensor_reduce(out=sj[:, w - P:w], in0=ps[:, a + w - P:a + w], in1=K["causal"], scale=1.0, scalar=-3e38,
                                         op0=ALU.add, op1=ALU.max, accum_out=sm[:, 1:2]).then_inc(added, 1)
                dve.wait_ge(added, j + 1)
                most = sm[:, 0:1] if n > 1 else sm[:, 1:2]
                dve.tensor_scalar(sm[:, 2:3], most, sm[:, 1:2], -SCALE, ALU.max, ALU.mult).then_inc(maxed, 1)

            def finish(t):
                dve.wait_ge(out_done, 4 * t + 4)
                for g in range(2):
                    hf = slice(64 * g, 64 * g + 64)
                    o = mixT[hf, ds(r, 1), t * P:(t + 1) * P].rearrange("p a t -> p (a t)")
                    b = (6 + t % 2) * BANK + g * P
                    m = dve.tensor_tensor(o, o, ps[hf, b:b + P], ALU.add)
                m.then_inc(summed, 1)

            mask(0)
            for j, job in enumerate(jobs):
                t, g, br = job
                w = keys(job)[1] * P
                if j + 1 < len(jobs):
                    mask(j + 1)
                dve.wait_ge(exped, j + 1)
                step(dve.reciprocal(st[:, j % 3, 4:5], st[:, j % 3, 3:4]))
                dve.tensor_scalar(s[:, j % 3, 0:w], s[:, j % 3, 0:w], st[:, j % 3, 4:5], gr[:, t, 1 + br, g:g + 1], ALU.mult, ALU.mult).then_inc(normed, 1)
                if j % 4 == 1 and t:
                    finish(t - 1)
            finish(SEQ // P - 1)


def sample_out(nc, ps, cst, os_d, mixT):
    with Scope(nc) as sc, stage(nc, "loaded turned kept") as (block, loaded, turned, kept):
        os_ = sc.sb("no_os", [NS, 512])

        @block.sync
        def _(sp):
            for b in range(NB):
                for g in range(2):
                    sp.dma_start(os_[b * NQ:(b + 1) * NQ, :].rearrange("q (r g d) -> q r g d", r=R4, g=2)[:, :, g],
                                 os_d[b, 32 * g:32 * g + 32].rearrange("(r q) d -> q r d", r=R4)).then_inc(loaded, 16)

        @block.tensor
        def _(pe):
            pe.wait_ge(loaded, 32 * NB)
            for r in range(R4):
                m = pe.transpose(ps[:, r * NS:(r + 1) * NS], os_[:, r * P:(r + 1) * P], cst["ident"][0:NS, 0:NS])
            m.then_inc(turned, 1)

        @block.scalar
        def _(act):
            act.wait_ge(turned, 1)
            act.copy(mixT[:, 0:4, SEQ:NT], ps[:, 0:R4 * NS].rearrange("p (r t) -> p r t", r=R4)).then_inc(kept, 1)


FPART = 8


def residual_product(nc, ps, l, k0, kt, xh, xl, w_d, xres):
    with Scope(nc) as sc, stage(nc, "pool_hold w_hi w_ready w_in0 w_in1 x_in0 x_in1 products added banks_read stored0 stored1 sp_hold") as (
            block, pool_hold, w_hi, w_ready, w0, w1, x0, x1, products, added, banks_read, st0, st1, sp_hold):
        w_in, x_in, stored = (w0, w1), (x0, x1), (st0, st1)
        wt = sc.sb("rs_w", [P, 2, kt, P])
        wh = sc.sb("rs_wh", [P, 2, kt, P], F32R)
        wl = sc.sb("rs_wl", [P, 2, kt, P], F32R)
        xr = sc.sb("rs_x", [P, 2, NT])

        @block.sync
        def _(sp):
            def load_w(n, u):
                sp.dma_start(wt[:, u], w_d[l, n, :, k0:k0 + kt, :]).then_inc(w_in[u], 16)

            def load_x(n, u):
                sp.dma_start(xr[:, u, :], xres[n]).then_inc(x_in[u], 16)

            for u in range(2):
                load_w(u, u)
            for u in range(2):
                load_x(u, u)
            with sp.Fori(0, KD // 2 - 1) as i:
                for u in range(2):
                    sp.wait_ge(added, 2 * i + u + 1)
                    sp.sem_inc(sp_hold, 1)
                    sp.dma_start(xres[2 * i + u], xr[:, u, :]).then_inc(stored[u], 16)
                    load_w(2 * i + u + 2, u)
                    sp.wait_ge(stored[u], 16 * i + 16)
                    sp.sem_inc(sp_hold, 1)
                    load_x(2 * i + u + 2, u)
            for u in range(2):
                sp.wait_ge(added, KD - 1 + u)
                sp.dma_start(xres[KD - 2 + u], xr[:, u, :]).then_inc(stored[u], 16)
            for u in range(2):
                sp.wait_ge(stored[u], 16 * (KD // 2))

        @block.tensor
        def _(pe):
            with pe.Fori(0, KD // 2) as i:
                for u in range(2):
                    pe.wait_ge(banks_read, 2 * i + u + 1)
                    product3(pe, ps, 3 * u, wh[:, u], wl[:, u], xh, xl, kt, w_ready,
                             lambda c: kt // CHUNK * (2 * i + u) + c).then_inc(products, 1)

        @block.gpsimd
        def _(pool):
            with pool.Fori(0, KD // 2) as i:
                for u in range(2):
                    pool.wait_ge(w_in[u], 16 * i + 16)
                    pool.sem_inc(pool_hold, 1)
                    split_weights(pool, wt[:, u], wh[:, u], wl[:, u], kt, w_hi, w_ready, lambda c: kt // CHUNK * (2 * i + u) + c)

        @block.vector
        def _(dve):
            dve.sem_inc(banks_read, 2)
            with dve.Fori(0, KD // 2) as i:
                for u in range(2):
                    dve.wait_ge(x_in[u], 16 * i + 16)
                    dve.wait_ge(products, 2 * i + u + 1)
                    for n, (o, w) in enumerate(GROUPS):
                        b = (3 * u + n) * BANK
                        m = dve.tensor_tensor(xr[:, u, o:o + w], xr[:, u, o:o + w], ps[:, b:b + w], ALU.add)
                    m.then_inc(added, 1)
                    dve.wait_ge(added, 2 * i + u + 1)
                    dve.sem_inc(banks_read, 1)


def split_features(nc, hi, lo, x):
    with stage(nc, "hi_ready split") as (block, hi_ready, split):
        @block.scalar
        def _(act):
            for k in range(KD):
                act.copy(hi[:, k, :], x[:, k, :]).then_inc(hi_ready, 1)

        @block.vector
        def _(dve):
            for k in range(KD):
                dve.wait_ge(hi_ready, k + 1)
                dve.tensor_tensor(lo[:, k, :], x[:, k, :], f32(hi[:, k, :]), ALU.subtract).then_inc(split, 1)


def ffn_up(nc, ps, l, f0, nf, xh, xl, hh, hl, wg_d, wu_d, conv_d, cstate_d, conv_out):
    with Scope(nc) as sc, stage(nc, "pool_hold w_hi w_ready gate_used up_used h_hi h_split w_in0 w_in1 gate_done up_done gate_copied conv_done silu_done h_done ext_free gate_free h_free sent0 sent1 chain zeroed sp_hold") as (
            block, pool_hold, w_hi, w_ready, gate_used, up_used, h_hi, h_split, w0, w1, gate_done, up_done, gate_copied, conv_done, silu_done, h_done, ext_free, gate_free, h_free, sent0, sent1, chain_sem, zeroed, sp_hold):
        w_in, sent = (w0, w1), (sent0, sent1)
        wt = sc.sb("fu_w", [P, 2, 2, KD, P])
        wh = sc.sb("fu_wh", [P, 2, KD, P], F32R)
        wl = sc.sb("fu_wl", [P, 2, KD, P], F32R)
        steps = KD // CHUNK
        cw = sc.sb("fu_cw", [P, 2, 4])
        cst_ = sc.sb("fu_cst", [P, 2, NB, 2])
        ge = sc.sb("fu_ge", [P, SEQ + 2])
        gs = sc.sb("fu_gs", [P, NB, NQ + 2])
        c = sc.sb("fu_c", [P, NT])
        h = sc.sb("fu_h", [P, NT])
        co = sc.sb("fu_co", [P, 2, NB + 1, 2])

        @block.sync
        def _(sp):
            def load(f, u):
                sp.dma_start(wt[:, u, 0], wg_d[l, f]).then_inc(w_in[u], 16)
                sp.dma_start(wt[:, u, 1], wu_d[l, f]).then_inc(w_in[u], 16)
                sp.dma_start(cw[:, u, :], conv_d[l, f]).then_inc(w_in[u], 16)
                sp.dma_start(cst_[:, u], cstate_d[l, f]).then_inc(w_in[u], 16)

            def store(f, u):
                sp.dma_start(conv_out[l, f], co[:, u].rearrange("p b e -> p (b e)")).then_inc(sent[u], 16)

            sp.sem_inc(sent[0], 16)
            sp.sem_inc(sent[1], 16)
            load(f0, 0)
            load(f0 + 1, 1)
            with sp.Fori(0, nf // 2 - 1) as i:
                for u in range(2):
                    sp.wait_ge(conv_done, 2 * i + u + 1)
                    sp.sem_inc(sp_hold, 1)
                    store(f0 + 2 * i + u, u)
                    sp.wait_ge(up_done, 2 * i + u + 1)
                    sp.sem_inc(sp_hold, 1)
                    load(f0 + 2 * i + u + 2, u)
            for u in range(2):
                sp.wait_ge(conv_done, nf - 1 + u)
                store(f0 + nf - 2 + u, u)
            for u in range(2):
                sp.wait_ge(sent[u], 16 * (nf // 2 + 1))

        @block.tensor
        def _(pe):
            pe.sem_inc(gate_used, 1)
            pe.sem_inc(up_used, 1)
            with pe.Fori(0, nf // 2) as i:
                for u in range(2):
                    for half, (free, done, used) in enumerate(((gate_free, gate_done, gate_used), (h_free, up_done, up_used))):
                        pe.wait_ge(free, 2 * i + u + 1)
                        product3(pe, ps, 3 * half, wh[:, half], wl[:, half], xh, xl, KD, w_ready,
                                 lambda c: 2 * steps * (2 * i + u) + steps * half + c).then_inc(done, 1)
                        pe.wait_ge(done, 2 * i + u + 1)
                        pe.sem_inc(used, 1)

        @block.gpsimd
        def _(pool):
            with pool.Fori(0, nf // 2) as i:
                for u in range(2):
                    pool.wait_ge(w_in[u], 64 * i + 64)
                    pool.sem_inc(pool_hold, 1)
                    for half, used in enumerate((gate_used, up_used)):
                        pool.wait_ge(used, 2 * i + u + 1)
                        pool.sem_inc(pool_hold, 1)
                        split_weights(pool, wt[:, u, half], wh[:, half], wl[:, half], KD, w_hi, w_ready,
                                      lambda c: 2 * steps * (2 * i + u) + steps * half + c)

        @block.scalar
        def _(act):
            act.sem_inc(gate_free, 1)
            with act.Fori(0, nf // 2) as i:
                for u in range(2):
                    act.wait_ge(gate_done, 2 * i + u + 1)
                    act.wait_ge(ext_free, 2 * i + u + 1)
                    act.copy(ge[:, 2:386], ps[:, 0:384])
                    act.copy(ge[:, 386:770], ps[:, BANK:BANK + 384])
                    act.copy(ge[:, 770:1026], ps[:, 2 * BANK:2 * BANK + 256])
                    act.copy(gs[:, :, 2:NQ + 2], ps[:, 2 * BANK + 256:2 * BANK + 320].rearrange("p (b q) -> p b q", b=NB)).then_inc(gate_copied, 1)
                    act.wait_ge(gate_copied, 2 * i + u + 1)
                    act.sem_inc(gate_free, 1)
                    act.wait_ge(conv_done, 2 * i + u + 1)
                    act.activation(c[:, :], c[:, :], ACT.Silu).then_inc(silu_done, 1)
                    act.wait_ge(h_done, 2 * i + u + 1)
                    act.copy(hh[:, ds(2 * i + u, 1), :].rearrange("p a t -> p (a t)"), h[:, :]).then_inc(h_hi, 1)

        @block.vector
        def _(dve):
            dve.memset(ge[:, 0:2], 0.0).then_inc(zeroed, 1)
            dve.wait_ge(zeroed, 1)
            dve.sem_inc(ext_free, 1)
            dve.sem_inc(h_free, 1)
            csam = c[:, SEQ:NT].rearrange("p (b q) -> p b q", b=NB)
            with dve.Fori(0, nf // 2) as i:
                for u in range(2):
                    dve.wait_ge(w_in[u], 64 * i + 64)
                    dve.wait_ge(gate_copied, 2 * i + u + 1)
                    dve.wait_ge(sent[u], 16 * i + 16)
                    dve.tensor_copy(co[:, u, 0, :], ge[:, SEQ:SEQ + 2])
                    dve.tensor_copy(co[:, u, 1:NB + 1, :], gs[:, :, NQ:NQ + 2])
                    dve.tensor_copy(gs[:, :, 0:2], cst_[:, u]).then_inc(chain_sem, 1)
                    dve.wait_ge(chain_sem, 3 * (2 * i + u) + 1)
                    dve.tensor_scalar(c[:, 0:SEQ], ge[:, 0:SEQ], cw[:, u, 0:1], cw[:, u, 3:4], ALU.mult, ALU.add)
                    dve.tensor_scalar(csam, gs[:, :, 0:NQ], cw[:, u, 0:1], cw[:, u, 3:4], ALU.mult, ALU.add).then_inc(chain_sem, 1)
                    dve.wait_ge(chain_sem, 3 * (2 * i + u) + 2)
                    dve.scalar_tensor_tensor(out=c[:, 0:SEQ], in0=ge[:, 1:SEQ + 1], scalar=cw[:, u, 1:2], in1=c[:, 0:SEQ], op0=ALU.mult, op1=ALU.add)
                    dve.scalar_tensor_tensor(out=csam, in0=gs[:, :, 1:NQ + 1], scalar=cw[:, u, 1:2], in1=csam, op0=ALU.mult, op1=ALU.add).then_inc(chain_sem, 1)
                    dve.wait_ge(chain_sem, 3 * (2 * i + u) + 3)
                    dve.scalar_tensor_tensor(out=c[:, 0:SEQ], in0=ge[:, 2:SEQ + 2], scalar=cw[:, u, 2:3], in1=c[:, 0:SEQ], op0=ALU.mult, op1=ALU.add)
                    dve.scalar_tensor_tensor(out=csam, in0=gs[:, :, 2:NQ + 2], scalar=cw[:, u, 2:3], in1=csam, op0=ALU.mult, op1=ALU.add).then_inc(conv_done, 1)
                    dve.wait_ge(conv_done, 2 * i + u + 1)
                    dve.sem_inc(ext_free, 1)
                    dve.wait_ge(silu_done, 2 * i + u + 1)
                    dve.wait_ge(up_done, 2 * i + u + 1)
                    for n, (o, w) in enumerate(GROUPS):
                        m = dve.tensor_tensor(h[:, o:o + w], c[:, o:o + w], ps[:, (3 + n) * BANK:(3 + n) * BANK + w], ALU.mult)
                    m.then_inc(h_done, 1)
                    dve.wait_ge(h_done, 2 * i + u + 1)
                    dve.sem_inc(h_free, 1)
                    dve.wait_ge(h_hi, 2 * i + u + 1)
                    high, low = (a[:, ds(2 * i + u, 1), :].rearrange("p a t -> p (a t)") for a in (hh, hl))
                    dve.tensor_tensor(low, h[:, :], f32(high), ALU.subtract).then_inc(h_split, 1)


def trunk(nc, A, O, X):
    with ExitStack() as top:
        pst = top.enter_context(nc.psum_tensor("ps", [P, 8 * BANK], F32))
        ps = pst[:, :]
        cbuf = top.enter_context(nc.sbuf_tensor("cbuf", [P, 3 * P], F32))
        ptab = top.enter_context(nc.sbuf_tensor("ptab", [1, NB * PAGES], I32))
        cst = {n: cbuf[:, i * P:(i + 1) * P] for i, n in enumerate(("ident", "ones", "blk"))}
        xres = X["xres"]
        with stage(nc, "loaded") as (block, loaded):
            @block.sync
            def _(sp):
                sp.dma_start(cbuf[:, :], A["const"][:, 0:3 * P]).then_inc(loaded, 16)
                sp.dma_start(ptab[:, :], A["page_table"]).then_inc(loaded, 16)
                for k in range(KD):
                    sp.dma_start(xres[k], A["xT"][k]).then_inc(loaded, 16)
                sp.wait_ge(loaded, 16 * (KD + 2))

        with nc.Fori(0, L) as l:
            with Scope(nc) as mixed:
                qT = mixed.sb("qT", [P, R4, NTP])
                ksT, kwT, vs, vw = (mixed.sb(n, [P, NTP]) for n in ("ksT", "kwT", "vs", "vw"))
                gate = mixed.sb("gate", [P, TT * 24])
                with Scope(nc) as sc:
                    xh = sc.sb("xh", [P, KD, NTP], F32R)
                    xl = sc.sb("xl", [P, KD, NTP], F32R)
                    with Scope(nc) as sn:
                        zero = sn.sb("zero", [P, NTP - NT])
                        with stage(nc, "zeroed padded") as (block, zeroed, padded):
                            @block.vector
                            def _(dve):
                                dve.memset(zero[:, :], 0.0).then_inc(zeroed, 1)
                                dve.wait_ge(zeroed, 1)
                                dve.tensor_copy(xh[:, :, NT:NTP], mid(zero[:, :], KD))
                                dve.tensor_copy(xl[:, :, NT:NTP], mid(zero[:, :], KD)).then_inc(padded, 1)
                        load_norm(nc, ps, cst, xres, A["norm_mix"][l], sn.sb("xn", [P, KD, NT]), hi=xh, lo=xl)
                    with Scope(nc) as sn:
                        w = sn.sb("wn", [P, KD, WN])
                        tmp = (sn.sb("np_xt", [P, 2, KD, P]), sn.sb("np_kv", [P, 2, 768]), sn.sb("np_q", [P, 2, 512]), sn.sb("np_q2", [P, 2, 512]),
                               sn.sb("np_tb", [P, 4, 256]), sn.sb("np_cs", [P, NSA_TILES, 64]))
                        with stage(nc, "loaded") as (block, loaded):
                            @block.sync
                            def _(sp):
                                for k in range(KD):
                                    sp.dma_start(w[:, k, :], A["w_nsa"][l, k]).then_inc(loaded, 16)
                                sp.wait_ge(loaded, 16 * KD)
                        with nc.Fori(0, TT // NSA_TILES) as t:
                            nsa_projection(nc, ps, cst, l, NSA_TILES * t, xh, xl, w, qT, ksT, kwT, vs, vw, gate, O["kvrows"], X["winr"], A["rope"], tmp)
                    rwkv_projection(nc, ps, cst, l, xh, xl, A["w_rw"], A["shift_in"], A["mu"][l], X["xmT"], O["shift"])
                mixT = mixed.sb("mixT", [P, KD, NT])
                with Scope(nc) as sc:
                    wend = sc.sb("wend", [P, 4, NCH + NB])
                    rwkv_features(nc, ps, cst, l, X["xmT"], A["lora"][l], A["rvec"][l], X["arbk"], X["rk"], wend, A["const"])
                    rwkv_scan(nc, ps, cst, l, wend, A["const"], X["arbk"], X["xmT"], X["yr"], X["vr"], A["wkv_in"], O["wkv"])
                    rwkv_output(nc, ps, cst, l, mixT, X["xmT"], X["rk"], X["yr"], X["vr"], A["g_b"], A["gn"], A["rk8"])
                with Scope(nc) as sc:
                    cp = Compressor(nc, sc)
                    with stage(nc, "stored") as (block, stored):
                        @block.sync
                        def _(sp):
                            sp.dma_start(O["win_p"][l], X["winr"][SEQ - 256:SEQ, :]).then_inc(stored, 16)
                            sp.dma_start(O["win_s"][l, :, 0:256 - NQ, :], A["state_win"][l, :, NQ:256, :]).then_inc(stored, 16)
                            sp.dma_start(O["win_s"][l, :, 256 - NQ:256, :], X["winr"][SEQ:NT, :].rearrange("(b q) n -> b q n", b=NB)).then_inc(stored, 16)
                            sp.dma_start(X["gs"], gate[0:NS, 24 * (TT - 1):24 * TT]).then_inc(stored, 16)
                            sp.wait_ge(stored, 64)
                    cp.weights(nc, ps, l, A["w1"], A["w2"], A["pe"])
                    sample_attention(nc, ps, cst, l, cp, qT, A["cache"], ptab, O["kvrows"], X["winr"], X["gs"], X["os"], A["state_win"], A["const"])

                    with nc.semaphore("rows_in") as rows_in:
                        def prompt_rows(sp):
                            for n in range(4):
                                sp.dma_start(cp.kvp[:, 0, n, :], O["kvrows"][l, n * 256:(n + 1) * 256, :].rearrange("(p e) n -> p (e n)", e=2)).then_inc(rows_in, 16)
                            sp.wait_ge(rows_in, 64)

                        cp.run(nc, ps, cst, 0, prompt_rows, used=(rows_in,))
                    selm = sc.sb("selm", [P, 8, 2, 16])
                    names = ("cvalid", "cadd", "keep", "add", "causal", "band", "low16")
                    off, w = {}, 0
                    for n in names:
                        off[n] = w
                        w += CO[n][1]
                    km = sc.sb("km", [P, w])
                    K = {n: km[:, off[n]:off[n] + CO[n][1]] for n in names}
                    pgb = sc.sb("pc_pgb", [P, 4, 66])
                    with stage(nc, "loaded zeroed") as (block, loaded, zeroed):
                        @block.sync
                        def _(sp):
                            for n in names:
                                a, ww = CO[n]
                                sp.dma_start(km[:, off[n]:off[n] + ww], A["const"][:, a:a + ww]).then_inc(loaded, 16)
                            sp.wait_ge(loaded, 16 * len(names))

                        @block.vector
                        def _(dve):
                            dve.memset(pgb[:, :, :], 0.0).then_inc(zeroed, 1)
                    with Scope(nc) as s2:
                        bufs = (s2.sb("pc_qt", [P, R4, 2 * P]), s2.sb("pc_s", [P, 2, 512]), s2.sb("pc_sg", [P, 2, 512]), s2.sb("pc_pT", [64, 2, HH, P]), s2.sb("pc_m8", [P, 2, 8]), pgb,
                                s2.sb("pc_im", [P, 4, 16]), s2.sb("pc_gt", [P, 4, 16, 16]), s2.sb("pc_eq", [P, 4, 16, 16]), s2.sb("pc_rank", [P, 4, 16]))
                        with nc.Fori(0, SEQ // (2 * P)) as t:
                            prompt_compressed(nc, ps, cst, 2 * t, cp, qT, gate, mixT, selm, bufs, K)
                    with Scope(nc) as s2:
                        bufs = (s2.sb("pa_qz", [P, 2, SEQ]), s2.sb("pa_s", [P, 3, SEQ]), s2.sb("pa_pT", [P, 2, 8, P]), s2.sb("pa_st", [P, 3, 5]), s2.sb("pa_gr", [P, 8, 3, 2]))
                        with stage(nc, "zeroed") as (block, zeroed):
                            @block.vector
                            def _(dve):
                                dve.memset(bufs[0][64:128, 0, :], 0.0)
                                dve.memset(bufs[0][0:64, 1, :], 0.0).then_inc(zeroed, 1)
                        with nc.Fori(0, R4) as r:
                            prompt_attention(nc, ps, cst, r, qT, ksT, kwT, vs, vw, gate, mixT, selm, bufs, K)
                    sample_out(nc, ps, cst, X["os"], mixT)
                mixh = mixed.sb("mixh", [P, KD, NT], F32R)
                mixl = mixed.sb("mixl", [P, KD, NT], F32R)
                split_features(nc, mixh, mixl, mixT)
                residual_product(nc, ps, l, 0, KD, mixh, mixl, A["w_out"], xres)
            with Scope(nc) as sc:
                xh = sc.sb("xh2", [P, KD, NT], F32R)
                xl = sc.sb("xl2", [P, KD, NT], F32R)
                with Scope(nc) as sn:
                    load_norm(nc, ps, cst, xres, A["norm_ffn"][l], sn.sb("xn2", [P, KD, NT]), hi=xh, lo=xl)
                hh = sc.sb("hh", [P, FPART, NT], F32R)
                hl = sc.sb("hl", [P, FPART, NT], F32R)
                for f0 in range(0, FF, FPART):
                    nf = min(FPART, FF - f0)
                    ffn_up(nc, ps, l, f0, nf, xh, xl, hh, hl, A["w_gate"], A["w_up"], A["conv_w"], A["conv_in"], O["conv"])
                    residual_product(nc, ps, l, f0, nf, hh, hl, A["w_down"], xres)
        with Scope(nc) as sc:
            xf = sc.sb("xf", [P, KD, NT])
            load_norm(nc, ps, cst, xres, A["norm_final"], xf, store=O["yT"])


QPERM = np.arange(512).reshape(2, 4, 64).transpose(1, 0, 2).reshape(-1)
GPERM = np.arange(24).reshape(2, 4, 3).transpose(2, 1, 0).reshape(-1)
RPERM = np.concatenate([np.arange(0, 512), np.arange(576, 1088), np.arange(1088, 1600),
                        np.arange(512, 576), np.arange(1600, 1664), np.arange(1664, 1792)])

SPERM = np.arange(512).reshape(4, 2, 64).transpose(1, 0, 2).reshape(-1)


def tiles(v, n):
    return np.ascontiguousarray(v.reshape(v.shape[0], n, P).transpose(0, 2, 1))


def layout(i):
    c = np.ascontiguousarray
    a = {"const": constants(), "rope": rope_tables()}
    x = np.concatenate([i["x_prompt"].reshape(SEQ, D), i["x_sample"].reshape(NS, D)])
    a["xT"] = c(x.T.reshape(KD, P, NT))
    a["page_table"] = c(i["page_table"].reshape(1, NB * PAGES))
    a["cache"] = c(i["cache_kv"].reshape(L, NPHYS, 64, 1024))
    a["state_win"] = c(i["state_win"].reshape(L, NB, 256, 256))
    w = i["w_in"]
    nsa = np.concatenate([QPERM, np.arange(512, 1280), 1280 + GPERM])
    a["w_nsa"] = c(w[:, :, nsa].reshape(L, KD, P, WN))
    a["w_rw"] = c(w[:, :, 1304 + RPERM].reshape(L, KD, P, FR, P).transpose(0, 3, 2, 1, 4))
    a["mu"] = tiles(i["rw_mu"][:, RPERM], FR)
    a["shift_in"] = c(i["state_shift"][:, :, RPERM].reshape(L, NB, FR, P).transpose(0, 2, 3, 1))
    a["lora"] = c(np.concatenate([i["rw_w_b"], i["rw_a_b"]], 1))
    a["rvec"] = c(np.stack([tiles(i[n], 4) for n in ("rw_w0", "rw_a0", "rw_k_k", "rw_k_a")], 2))
    a["g_b"] = c(i["rw_g_b"][:, :, SPERM])
    a["gn"] = c(np.stack([i["rw_gn_w"], i["rw_gn_b"]], 1)[:, :, SPERM])
    rk8 = np.zeros((L, P, 4, 8), np.float32)
    for h in range(HH):
        rk8[:, 64 * (h % 2):64 * (h % 2) + 64, h // 2, h % 2 * 4 + h // 2] = i["rw_r_k"][:, h]
    a["rk8"] = rk8
    a["wkv_in"] = c(i["state_wkv"].reshape(L, NB, 4, 2, HD, HD).transpose(0, 3, 5, 2, 1, 4).reshape(L, P, 4, NB, HD))
    a["w1"] = c(i["cmp_w1"].reshape(L, 2, 16, P, 256).transpose(0, 1, 3, 2, 4))
    a["w2"] = c(i["cmp_w2"].reshape(L, 2, 2, P, HD).transpose(0, 1, 3, 2, 4))
    a["pe"] = c(i["cmp_pe"].reshape(L, 2, 16, P).transpose(0, 1, 3, 2))
    wo = i["w_out"][:, np.concatenate([QPERM, 512 + SPERM]), :]
    a["w_out"] = c(wo.reshape(L, KD, P, KD, P).transpose(0, 3, 2, 1, 4))
    for n, k in (("w_gate", "ffn_w_gate"), ("w_up", "ffn_w_up")):
        z = np.zeros((L, D, FF * P), np.float32)
        z[:, :, :2752] = i[k]
        a[n] = c(z.reshape(L, KD, P, FF, P).transpose(0, 3, 2, 1, 4))
    z = np.zeros((L, FF * P, D), np.float32)
    z[:, :2752] = i["ffn_w_down"]
    a["w_down"] = c(z.reshape(L, FF, P, KD, P).transpose(0, 3, 2, 1, 4))
    z = np.zeros((L, FF * P, 4), np.float32)
    z[:, :2752, 0:3] = i["ffn_conv_w"].transpose(0, 2, 1)
    z[:, :2752, 3] = i["ffn_conv_b"]
    a["conv_w"] = z.reshape(L, FF, P, 4)
    z = np.zeros((L, FF * P, NB, 2), np.float32)
    z[:, :2752] = i["state_conv"].transpose(0, 3, 1, 2)
    a["conv_in"] = z.reshape(L, FF, P, NB, 2)
    a["norm_mix"] = tiles(i["norm_mix"], KD)
    a["norm_ffn"] = tiles(i["norm_ffn"], KD)
    a["norm_final"] = tiles(i["norm_final"][None], KD)[0]
    return a


OUTS = {"yT": (KD, P, NT), "kvrows": (L, NTP, 512), "win_p": (L, 256, 256), "win_s": (L, NB, 256, 256),
        "wkv": (L, P, 4, NB + 1, HD), "shift": (L, FR, P, NB + 1), "conv": (L, FF, P, 2 * (NB + 1))}
SCRATCH = {"xres": (KD, P, NT), "winr": (NTP, 256), "xmT": (FR, P, NT), "arbk": (NCH + 1, P, 4, 4 * CH),
           "rk": (4, P, NT), "yr": (NT, 512), "vr": (NT, 512), "gs": (NS, 24), "os": (NB, 64, HD)}


def build(nc, arrays):
    A = {n: nc.dram_tensor(f"in_{n}", a.shape, mybir.dt.from_np(a.dtype), kind="ExternalInput").ap() for n, a in arrays.items()}
    O = {n: nc.dram_tensor(f"out_{n}", s, F32, kind="ExternalOutput").ap() for n, s in OUTS.items()}
    X = {n: nc.dram_tensor(f"scr_{n}", s, F32, kind="Internal").ap() for n, s in SCRATCH.items()}
    trunk(nc, A, O, X)


def unlay(o):
    y = o["yT"].reshape(D, NT).T
    kv = o["kvrows"]
    rp = np.argsort(RPERM)
    wkv = o["wkv"].reshape(L, 2, HD, 4, NB + 1, HD).transpose(0, 4, 3, 1, 5, 2).reshape(L, NB + 1, HH, HD, HD)
    sh = o["shift"].reshape(L, FR * P, NB + 1)[:, rp].transpose(0, 2, 1)
    cv = o["conv"].reshape(L, FF * P, NB + 1, 2)[:, :2752].transpose(0, 2, 3, 1)
    c = np.ascontiguousarray
    return (c(y[:SEQ].reshape(1, SEQ, D)), c(y[SEQ:].reshape(NB, NQ, D)),
            c(kv[:, :SEQ].reshape(L, 1, SEQ, 4, 2, HD)), c(kv[:, SEQ:NT].reshape(L, NB, NQ, 4, 2, HD)),
            o["win_p"].reshape(L, 1, 256, 2, 2, HD), o["win_s"].reshape(L, NB, 256, 2, 2, HD),
            c(wkv[:, 0:1]), c(wkv[:, 1:]), c(sh[:, 0:1]), c(sh[:, 1:]), c(cv[:, 0:1]), c(cv[:, 1:]))


def kernel(**inputs):
    import concourse.bacc as bacc
    from concourse.bass_utils import run_bass_kernel_spmd as run

    arrays = layout({k: np.asarray(v) for k, v in inputs.items()})
    nc = bacc.Bacc("TRN2", target_bir_lowering=False, num_devices=1)
    build(nc, arrays)
    r = run(nc, [{f"in_{n}": a for n, a in arrays.items()}], core_ids=[0])
    return unlay({n: r.results[0][f"out_{n}"] for n in OUTS})
```
